# Optimizing a Trainium2 kernel written in Bass

```python
import math
import jax
import jax.numpy as jnp
from jax import lax
import numpy as np

D_MODEL = 1024
BATCH = 1
SEQ = 128
DEPTH = 2
DEC_BATCH = 1
DEC_SEQ = 512
PAST_LEN = 256

GRID_W = 64
Q_BLOCK = 128
CHUNK = 32
ROPE_THETA = 10000.0
EPS = 1e-6
LB_FLOOR = 1e-30
N_MOD = 6
N_BRANCH = 4
BRANCH_W = D_MODEL // 4
A_HEADS = 4
A_KV_HEADS = 2
A_HEAD_DIM = BRANCH_W // A_HEADS
C_HEADS = 4
C_HEAD_DIM = BRANCH_W // (2 * C_HEADS)
B_HEADS = 4
B_KEY_DIM = BRANCH_W // B_HEADS
B_VAL_DIM = BRANCH_W // B_HEADS
D_HEADS = 4
D_KEY_DIM = BRANCH_W // (2 * D_HEADS)
D_VAL_DIM = BRANCH_W // D_HEADS
D_GATE_RANK = 16
D_GATE_TAU = 16.0
D_FF = 11 * D_MODEL // 4
CONV_WIDTH = 3
IN_SPLITS = (
    A_HEADS * A_HEAD_DIM, A_KV_HEADS * A_HEAD_DIM, A_KV_HEADS * A_HEAD_DIM,
    2 * C_HEADS * C_HEAD_DIM, 2 * C_HEADS * C_HEAD_DIM, 2 * C_HEADS * C_HEAD_DIM,
    B_HEADS * B_KEY_DIM, B_HEADS * B_VAL_DIM, B_HEADS * B_KEY_DIM, B_HEADS * B_KEY_DIM, B_HEADS * B_VAL_DIM,
    D_HEADS * D_KEY_DIM, D_HEADS * D_KEY_DIM, D_HEADS * D_VAL_DIM, D_HEADS * D_VAL_DIM, D_GATE_RANK, D_GATE_RANK,
    N_BRANCH * D_MODEL,
)
IN_WIDTH = sum(IN_SPLITS)

kernel_name = 'hybrid_diffusion_prefix_trunk_step'

def rms_norm(x, g):
    xf = x.astype(jnp.float32)
    y = xf * lax.rsqrt(jnp.mean(xf * xf, axis=-1, keepdims=True) + EPS)
    return (y * g.astype(jnp.float32)).astype(x.dtype)

def axial_rope_tables(n_tokens, head_dim):
    rows = n_tokens // GRID_W
    row = jnp.repeat(jnp.arange(rows), GRID_W).astype(jnp.float32)
    col = jnp.tile(jnp.arange(GRID_W), rows).astype(jnp.float32)
    half = head_dim // 2
    freqs = ROPE_THETA ** (-jnp.arange(0, half, 2, dtype=jnp.float32) / half)
    ang_r = row[:, None] * freqs
    ang_c = col[:, None] * freqs
    ang = jnp.concatenate([ang_r, ang_r, ang_c, ang_c], axis=-1)
    return jnp.cos(ang), jnp.sin(ang)

def apply_rope(x, cos, sin):
    q4 = x.shape[-1] // 4
    xs = x.reshape(x.shape[:-1] + (2, 2, q4))
    rot = jnp.concatenate([-xs[..., 1:2, :], xs[..., 0:1, :]], axis=-2).reshape(x.shape)
    y = x.astype(jnp.float32) * cos[:, None, :] + rot.astype(jnp.float32) * sin[:, None, :]
    return y.astype(x.dtype)

def attend(q, k, v, scale):
    b, tq = q.shape[:2]
    nb = tq // Q_BLOCK
    qb = jnp.moveaxis(q.reshape((b, nb, Q_BLOCK) + q.shape[2:]), 1, 0)
    kf = k.astype(jnp.float32)
    vf = v.astype(jnp.float32)

    def block(qblk):
        s = jnp.einsum('bqgrd,bkgd->bgrqk', qblk.astype(jnp.float32), kf) * scale
        p = jax.nn.softmax(s, axis=-1)
        return jnp.einsum('bgrqk,bkgv->bqgrv', p, vf)

    o = lax.map(block, qb)
    return jnp.moveaxis(o, 0, 1).reshape((b, tq) + o.shape[3:]).astype(q.dtype)

def chunked_gla(q, k, v, log_a, s0):
    bsz, t, h, dk = q.shape
    dv = v.shape[-1]
    n = t // CHUNK
    q, k, log_a = [a.astype(jnp.float32).reshape(bsz, n, CHUNK, h, dk) for a in (q, k, log_a)]
    v = v.astype(jnp.float32).reshape(bsz, n, CHUNK, h, dv)
    cum = jnp.cumsum(log_a, axis=2)
    cum_last = cum[:, :, -1]
    mask = jnp.tril(jnp.ones((CHUNK, CHUNK), dtype=bool))[:, :, None, None]
    diff = cum[:, :, :, None] - cum[:, :, None, :]
    decay = jnp.where(mask, jnp.exp(jnp.where(mask, diff, 0.0)), 0.0)
    scores = jnp.einsum('bnthk,bnshk,bntshk->bnhts', q, k, decay)
    o_intra = jnp.einsum('bnhts,bnshv->bnthv', scores, v)
    q_in = q * jnp.exp(cum)
    k_out = k * jnp.exp(cum_last[:, :, None] - cum)

    def step(s, xs):
        qi, ko, vc, cl = xs
        o = jnp.einsum('bthk,bhkv->bthv', qi, s)
        s = jnp.exp(cl)[..., None] * s + jnp.einsum('bthk,bthv->bhkv', ko, vc)
        return s, o

    xs = tuple(jnp.moveaxis(a, 1, 0) for a in (q_in, k_out, v, cum_last))
    s_final, o_inter = lax.scan(step, s0.astype(jnp.float32), xs)
    o = o_intra + jnp.moveaxis(o_inter, 0, 1)
    return o.reshape(bsz, t, h, dv), s_final

def bidir_gla(q, k_f, k_b, v, la_f, la_b, s0_f, s0_b):
    o_f, s_f = chunked_gla(q, k_f, v, la_f, s0_f)
    flip = lambda a: jnp.flip(a, axis=1)
    o_b, s_b = chunked_gla(flip(q), flip(k_b), flip(v), flip(la_b), s0_b)
    return o_f + flip(o_b), s_f, s_b

def hgrn_forget(z, lb):
    z = z.astype(jnp.float32)
    log_f = jnp.logaddexp(jnp.log(jnp.maximum(lb, LB_FLOOR)), jnp.log1p(-lb) + jax.nn.log_sigmoid(z))
    k = (1.0 - lb) * jax.nn.sigmoid(-z)
    return k, log_f

def conv_ffn(h, w_up, conv_w, conv_b, w_down):
    u = h @ w_up
    pad = CONV_WIDTH // 2
    t = u.shape[1]
    up = jnp.pad(u, ((0, 0), (pad, pad), (0, 0)))
    u = sum(up[:, j:j + t] * conv_w[j] for j in range(CONV_WIDTH)) + conv_b
    a, g = jnp.split(u, 2, axis=-1)
    return (jax.nn.silu(g) * a) @ w_down

def trunk_layer(x, cond, ctx, p, lam_init):
    bsz, t, _ = x.shape
    dt = x.dtype
    mod = jax.nn.silu(cond) @ p['w_ada'] + p['b_ada']
    sh1, sc1, g1, sh2, sc2, g2 = [m[:, None, :] for m in jnp.split(mod, N_MOD, axis=-1)]
    h = rms_norm(x, p['norm1_g']) * (1 + sc1) + sh1
    z = h @ p['w_in']
    (a_q, a_k, a_v, c_q, c_k, c_v, b_q, b_i, b_ff, b_fb, b_g,
     d_q, d_k, d_v, d_g, d_rf, d_rb, merge_logits) = jnp.split(z, np.cumsum(IN_SPLITS)[:-1].tolist(), axis=-1)

    aq = rms_norm(a_q.reshape(bsz, t, A_HEADS, A_HEAD_DIM), p['a_qn_g'])
    ak = rms_norm(a_k.reshape(bsz, t, A_KV_HEADS, A_HEAD_DIM), p['a_kn_g'])
    av = a_v.reshape(bsz, t, A_KV_HEADS, A_HEAD_DIM)
    cq = rms_norm(c_q.reshape(bsz, t, 2 * C_HEADS, C_HEAD_DIM), p['c_qn_g'])
    ck = rms_norm(c_k.reshape(bsz, t, 2 * C_HEADS, C_HEAD_DIM), p['c_kn_g'])
    cv = c_v.reshape(bsz, t, C_HEADS, 2 * C_HEAD_DIM)

    if ctx is None:
        ctx_out = [ak, av, ck.reshape(bsz, t, C_HEADS, 2, C_HEAD_DIM), cv]
        s_hgrn = jnp.zeros((bsz, 2, B_HEADS, B_KEY_DIM, B_VAL_DIM), jnp.float32)
        s_gla = jnp.zeros((bsz, 2, D_HEADS, D_KEY_DIM, D_VAL_DIM), jnp.float32)
    else:
        ctx_ak, ctx_av, ctx_ck, ctx_cv, s_hgrn, s_gla = ctx
        cos_a, sin_a = axial_rope_tables(t, A_HEAD_DIM)
        cos_c, sin_c = axial_rope_tables(t, C_HEAD_DIM)
        aq = apply_rope(aq, cos_a, sin_a)
        ak = jnp.concatenate([ctx_ak, apply_rope(ak, cos_a, sin_a)], axis=1)
        av = jnp.concatenate([ctx_av, av], axis=1)
        cq = apply_rope(cq, cos_c, sin_c)
        ck = jnp.concatenate([ctx_ck.reshape(bsz, -1, 2 * C_HEADS, C_HEAD_DIM), apply_rope(ck, cos_c, sin_c)], axis=1)
        cv = jnp.concatenate([ctx_cv, cv], axis=1)

    y_a = attend(aq.reshape(bsz, t, A_KV_HEADS, A_HEADS // A_KV_HEADS, A_HEAD_DIM), ak, av,
                 A_HEAD_DIM ** -0.5).reshape(bsz, t, BRANCH_W)

    cq = cq.reshape(bsz, t, C_HEADS, 2, C_HEAD_DIM)
    ck = ck.reshape(bsz, -1, C_HEADS, 2, C_HEAD_DIM)
    o1 = attend(cq[:, :, :, 0:1], ck[:, :, :, 0], cv, C_HEAD_DIM ** -0.5)
    o2 = attend(cq[:, :, :, 1:2], ck[:, :, :, 1], cv, C_HEAD_DIM ** -0.5)
    lq1, lk1, lq2, lk2 = p['c_lambda'].astype(jnp.float32)
    lam = jnp.exp(jnp.sum(lq1 * lk1)) - jnp.exp(jnp.sum(lq2 * lk2)) + lam_init
    y_c = (rms_norm((o1 - lam * o2)[:, :, :, 0], p['c_subln_g']) * (1.0 - lam_init)).reshape(bsz, t, BRANCH_W)

    bq = jax.nn.silu(b_q).reshape(bsz, t, B_HEADS, B_KEY_DIM)
    bi = b_i.reshape(bsz, t, B_HEADS, B_VAL_DIM)
    lb = p['b_lb'].reshape(2, B_HEADS, B_KEY_DIM)
    kb_f, lf_f = hgrn_forget(b_ff.reshape(bsz, t, B_HEADS, B_KEY_DIM), lb[0])
    kb_b, lf_b = hgrn_forget(b_fb.reshape(bsz, t, B_HEADS, B_KEY_DIM), lb[1])
    o_b, sb_f, sb_b = bidir_gla(bq, kb_f, kb_b, bi, lf_f, lf_b, s_hgrn[:, 0], s_hgrn[:, 1])
    y_b = (rms_norm(o_b, p['b_norm_g']) * jax.nn.silu(b_g.reshape(bsz, t, B_HEADS, B_VAL_DIM))).reshape(bsz, t, BRANCH_W)

    dq = d_q.reshape(bsz, t, D_HEADS, D_KEY_DIM) * D_KEY_DIM ** -0.5
    dk = d_k.reshape(bsz, t, D_HEADS, D_KEY_DIM)
    dv = d_v.reshape(bsz, t, D_HEADS, D_VAL_DIM)
    la_f, la_b = [(jax.nn.log_sigmoid((r @ p['d_alpha_w'][i] + p['d_alpha_b'][i]).astype(jnp.float32))
                   / D_GATE_TAU).reshape(bsz, t, D_HEADS, D_KEY_DIM) for i, r in enumerate((d_rf, d_rb))]
    o_d, sd_f, sd_b = bidir_gla(dq, dk, dk, dv, la_f, la_b, s_gla[:, 0], s_gla[:, 1])
    y_d = (rms_norm(o_d, p['d_norm_g']) * jax.nn.silu(d_g.reshape(bsz, t, D_HEADS, D_VAL_DIM))).reshape(bsz, t, BRANCH_W)

    branches = jnp.stack([y_a, y_b, y_c, y_d], axis=2).astype(dt)
    proj = jnp.einsum('btnw,nwd->btnd', branches, p['w_branch'])
    gates = jax.nn.sigmoid(merge_logits.reshape(bsz, t, N_BRANCH, D_MODEL))
    mixed = jnp.sum(gates * proj, axis=2) @ p['w_out']
    x = x + g1 * mixed

    h2 = rms_norm(x, p['norm2_g']) * (1 + sc2) + sh2
    x = x + g2 * conv_ffn(h2, p['w_up'], p['conv_w'], p['conv_b'], p['w_down'])
    if ctx is None:
        ctx_out = ctx_out + [jnp.stack([sb_f, sb_b], axis=1), jnp.stack([sd_f, sd_b], axis=1)]
        return x, ctx_out
    return x, None

def setup_inputs(seed: int = 0) -> dict:
    key = jax.random.key(seed)
    ks = iter(jax.random.split(key, 40))

    def nrm(shape, scale):
        return jax.random.normal(next(ks), shape, jnp.float32) * scale

    def gain(shape):
        return 1.0 + nrm(shape, 0.02)

    return {
        'x_prompt': nrm((BATCH, SEQ, D_MODEL), 1.0),
        'x_sample': nrm((DEC_BATCH, DEC_SEQ, D_MODEL), 1.0),
        'cache_a_k': nrm((DEC_BATCH, DEPTH, PAST_LEN, A_KV_HEADS, A_HEAD_DIM), 1.0),
        'cache_a_v': nrm((DEC_BATCH, DEPTH, PAST_LEN, A_KV_HEADS, A_HEAD_DIM), 1.0),
        'cache_c_k': nrm((DEC_BATCH, DEPTH, PAST_LEN, C_HEADS, 2, C_HEAD_DIM), 1.0),
        'cache_c_v': nrm((DEC_BATCH, DEPTH, PAST_LEN, C_HEADS, 2 * C_HEAD_DIM), 1.0),
        'state_hgrn': nrm((DEC_BATCH, DEPTH, 2, B_HEADS, B_KEY_DIM, B_VAL_DIM), 0.5),
        'state_gla': nrm((DEC_BATCH, DEPTH, 2, D_HEADS, D_KEY_DIM, D_VAL_DIM), 0.5),
        'c': nrm((DEC_BATCH, D_MODEL), 1.0),
        'c_ctx': nrm((D_MODEL,), 1.0),
        'w_ada': nrm((DEPTH, D_MODEL, N_MOD * D_MODEL), 0.5 * D_MODEL ** -0.5),
        'b_ada': nrm((DEPTH, N_MOD * D_MODEL), 0.02),
        'norm1_g': gain((DEPTH, D_MODEL)),
        'norm2_g': gain((DEPTH, D_MODEL)),
        'w_in': nrm((DEPTH, D_MODEL, IN_WIDTH), D_MODEL ** -0.5),
        'a_qn_g': gain((DEPTH, A_HEAD_DIM)),
        'a_kn_g': gain((DEPTH, A_HEAD_DIM)),
        'c_qn_g': gain((DEPTH, C_HEAD_DIM)),
        'c_kn_g': gain((DEPTH, C_HEAD_DIM)),
        'c_lambda': nrm((DEPTH, 4, C_HEAD_DIM), 0.1),
        'c_subln_g': gain((DEPTH, 2 * C_HEAD_DIM)),
        'b_lb_logits': nrm((2, DEPTH, B_HEADS * B_KEY_DIM), 0.5),
        'b_norm_g': gain((DEPTH, B_VAL_DIM)),
        'd_alpha_w': nrm((DEPTH, 2, D_GATE_RANK, D_HEADS * D_KEY_DIM), D_GATE_RANK ** -0.5),
        'd_alpha_b': nrm((DEPTH, 2, D_HEADS * D_KEY_DIM), 0.1),
        'd_norm_g': gain((DEPTH, D_VAL_DIM)),
        'w_branch': nrm((DEPTH, N_BRANCH, BRANCH_W, D_MODEL), BRANCH_W ** -0.5),
        'w_out': nrm((DEPTH, D_MODEL, D_MODEL), D_MODEL ** -0.5),
        'w_up': nrm((DEPTH, D_MODEL, 2 * D_FF), D_MODEL ** -0.5),
        'conv_w': nrm((DEPTH, CONV_WIDTH, 2 * D_FF), CONV_WIDTH ** -0.5),
        'conv_b': nrm((DEPTH, 2 * D_FF), 0.01),
        'w_down': nrm((DEPTH, D_FF, D_MODEL), D_FF ** -0.5),
    }

def reference(x_prompt, x_sample, cache_a_k, cache_a_v, cache_c_k, cache_c_v, state_hgrn, state_gla,
              c, c_ctx, w_ada, b_ada, norm1_g, norm2_g, w_in, a_qn_g, a_kn_g, c_qn_g, c_kn_g,
              c_lambda, c_subln_g, b_lb_logits, b_norm_g, d_alpha_w, d_alpha_b, d_norm_g,
              w_branch, w_out, w_up, conv_w, conv_b, w_down):
    lb_p = jax.nn.softmax(b_lb_logits.astype(jnp.float32), axis=1)
    lb_all = jnp.cumsum(lb_p, axis=1) - lb_p[:, :1]
    y_prompt = x_prompt
    y_sample = x_sample
    collected = [[] for _ in range(6)]
    for l in range(DEPTH):
        p = {
            'w_ada': w_ada[l], 'b_ada': b_ada[l], 'norm1_g': norm1_g[l], 'norm2_g': norm2_g[l],
            'w_in': w_in[l], 'a_qn_g': a_qn_g[l], 'a_kn_g': a_kn_g[l], 'c_qn_g': c_qn_g[l],
            'c_kn_g': c_kn_g[l], 'c_lambda': c_lambda[l], 'c_subln_g': c_subln_g[l],
            'b_lb': lb_all[:, l], 'b_norm_g': b_norm_g[l], 'd_alpha_w': d_alpha_w[l],
            'd_alpha_b': d_alpha_b[l], 'd_norm_g': d_norm_g[l], 'w_branch': w_branch[l],
            'w_out': w_out[l], 'w_up': w_up[l], 'conv_w': conv_w[l], 'conv_b': conv_b[l],
            'w_down': w_down[l],
        }
        lam_init = 0.8 - 0.6 * math.exp(-0.3 * l)
        y_prompt, ctx_l = trunk_layer(y_prompt, c_ctx[None, :], None, p, lam_init)
        cached = (cache_a_k[:, l], cache_a_v[:, l], cache_c_k[:, l], cache_c_v[:, l],
                  state_hgrn[:, l], state_gla[:, l])
        y_sample, _ = trunk_layer(y_sample, c, cached, p, lam_init)
        for acc, arr in zip(collected, ctx_l):
            acc.append(arr)
    new_cache_a_k, new_cache_a_v, new_cache_c_k, new_cache_c_v, new_state_hgrn, new_state_gla = [
        jnp.stack(acc, axis=1) for acc in collected]
    return (y_prompt, y_sample, new_cache_a_k, new_cache_a_v, new_cache_c_k, new_cache_c_v, new_state_hgrn, new_state_gla)


_drawn_inputs = setup_inputs


def setup_inputs(seed=0):
    import zlib

    import numpy as np

    out = dict(_drawn_inputs(seed))
    spreads = {}
    factors = {'cache_a_k': 8.0,
     'cache_a_v': 6.668,
     'state_hgrn': 8.0,
     'state_gla': 8.0,
     'norm2_g': 6.856,
     'a_qn_g': 8.0,
     'a_kn_g': 7.58,
     'c_qn_g': 8.0,
     'c_kn_g': 2.861,
     'c_lambda': 7.05,
     'c_subln_g': 23.079,
     'b_norm_g': 27.113,
     'd_norm_g': 25.029,
     'conv_b': 8.0,
     'cache_c_k': 8.0,
     'cache_c_v': 8.0}
    for name, (base, spread) in spreads.items():
        noise = np.random.default_rng([zlib.crc32(name.encode()), seed]).standard_normal(out[name].shape)
        drawn = base * np.exp(spread * noise) if base else spread * noise
        out[name] = jnp.asarray(drawn.astype(out[name].dtype))
    for name, factor in factors.items():
        out[name] = (out[name] * factor).astype(out[name].dtype)
    return out
```

```python
from contextlib import ExitStack

import concourse.bass as bass
from concourse import mybir

F32 = mybir.dt.float32
U8 = mybir.dt.uint8
ALU = mybir.AluOpType
ACT = mybir.ActivationFunctionType
AX = mybir.AxisListType

P = 128
D = 1024
KT = D // P
DEPTH = 2
TS, TC = 512, 128
T = TS + TC
NT = T // P
PAST = 256
FF = 2816
FT = FF // P
EPS = 1e-6
LB_FLOOR = 1e-30
SEG = ((0, TS), (TS, T))
Z_COLS = 3360

AQ, BG, CQ, DG, AK, CK, BQ, BFF, BFB, BKF, BKB, DQ, DK, DR, DAB, NZ = 0, 2, 4, 6, 8, 9, 11, 13, 15, 17, 19, 21, 22, 23, 24, 25
DAF = DR
MIXT = 8
V_A, V_C, V_B, V_D, NV = 0, 128, 384, 640, 896

(C_BADA, C_N1, C_N2, C_CB, C_AQ, C_AK, C_CQ, C_CK, C_SUB, C_BN, C_DN, C_AB, C_W0, C_W1, C_W2, C_LB, C_COND, C_LC, C_LAM, NCOL) = (
    0, 48, 56, 64, 108, 109, 110, 111, 112, 113, 114, 115, 117, 161, 205, 249, 257, 273, 276, 404)

N_SLOT = 4
C_ADA1, C_Z, C_ADA2, C_MIX, C_OUT, C_UP, C_DOWN, CHUNKS = 0, 8, 22, 38, 70, 74, 96, 112
SLOT_W = 2048

Z_PLAN = [("q", AQ), ("kv", AK), ("fm", CQ), ("fm", CK), ("tm", V_C), ("silu", BQ), ("tm", V_B), ("ff", BFF),
          ("ff", BFB), ("silu", BG), ("dqk", DQ), ("tm", V_D), ("silu", DG), ("r", DR)]


def z_tiles():
    out = []
    for c, (kind, dst) in enumerate(Z_PLAN):
        if kind == "kv":
            out += [(c, "fm", AK, 0), (c, "tm1", V_A, 1)]
        elif kind == "tm":
            out += [(c, "tm", dst, 0), (c, "tm", dst, 1)]
        elif kind == "r":
            out += [(c, "r", dst, 0)]
        else:
            out += [(c, kind, dst + j, j) for j in range(2)]
    return out


ZT_TILES = z_tiles()
NZT = len(ZT_TILES)
USES_Z = [(NZT + 1) // 2, NZT // 2, 0, 0]
USES_MIX, USES_OUT, USES_UP, USES_DOWN = 16, 2, 11, 2
USES = [u + USES_MIX + USES_OUT + USES_UP + USES_DOWN for u in USES_Z]
N_GEMM = NZT + 64 + 8 + 44 + 8
G_MIX, G_OUT, G_UP, G_DOWN = NZT, NZT + 64, NZT + 72, NZT + 116

STEPS = 4096
QK_TILES = [(AQ, C_AQ, 64), (AQ + 1, C_AQ, 64), (AK, C_AK, 64), (CQ, C_CQ, 32), (CQ + 1, C_CQ, 32),
            (CK, C_CK, 32), (CK + 1, C_CK, 32)]
NQK = len(QK_TILES)
ATT = [(AQ + j, 64 * g, 64, AK, 0, V_A + 64 * g, 64 ** -0.5, 2 * g + j) for j in range(2) for g in range(2)] + \
      [(CQ + h // 2, 64 * (h % 2) + 32 * m, 32, CK + h // 2, 1 + h // 2, V_C + 64 * h, 32 ** -0.5, 4 + 4 * m + h)
       for m in range(2) for h in range(4)]
NU = len(ATT)
GLA = [(BQ, (BKF, BKB), (BFF, BFB), BG, V_B, 64, 1, C_BN), (BQ + 1, (BKF + 1, BKB + 1), (BFF + 1, BFB + 1), BG + 1, V_B + 128, 64, 1, C_BN),
       (DQ, (DK, DK), (DAF, DAB), DG, V_D, 32, 2, C_DN)]
LEVELS = 7
NG = NT * NU
NPASS = 2 * LEVELS + 2
NGRP = sum(g[6] for g in GLA)
NSC = NGRP * (NPASS + 1)




def keys(i):
    return 1 if i == NT - 1 else (TS + PAST) // P


def tail_step(i):
    return NU * (i + 1) + 1


def y_step(i):
    return NU * (i + 1) + 3


class Chain:

    def __init__(self, sem):
        self.sem, self.n, self.base = sem, 0, 0

    def layer(self, l):
        self.l, self.n, self.base = l, 0, l * STEPS

    def mark(self, ins):
        self.n += 1
        ins.then_inc(self.sem, 1)

    def settle(self, eng):
        eng.wait_ge(self.sem, self.base + self.n)

    def enter(self, it, per):
        self.n0, self.per, self.base = self.n, per, self.l * STEPS + it * per

    def leave(self, count):
        assert self.n - self.n0 == self.per, (self.n - self.n0, self.per)
        self.n, self.base = self.n0 + count * self.per, self.l * STEPS

    def end(self, eng):
        assert self.n <= STEPS, self.n
        if self.n < STEPS:
            eng.sem_inc(self.sem, STEPS - self.n)


def build(nc, A, O):
    ctx = ExitStack()
    with ctx:
        def sb(name, shape, dt=F32):
            return ctx.enter_context(nc.sbuf_tensor(name, shape, dt))

        def sem(name):
            return ctx.enter_context(nc.semaphore(name))

        XT = sb("XT", [P, KT, T])
        HT = sb("HT", [P, KT, T])
        RING = sb("RING", [P, N_SLOT, SLOT_W])
        ZT = sb("ZT", [P, NZ, T])
        V = sb("V", [P, NT, NV])
        WORK = sb("WORK", [P, 5120])
        KO = sb("KO", [P, T])
        KOT = sb("KOT", [P, NT, P])
        CONST = sb("CONST", [P, 4 * TS + 6 * P])
        MASK = sb("MASK", [P, NPASS, 64], U8)
        KTC = sb("KTC", [P, 3, PAST])
        VC = sb("VC", [P, 2, V_B])
        ST = sb("ST", [P, 2, 3, NT, 64])
        FIN = sb("FIN", [P, 2, 3, 64])
        COLS = sb("COLS", [P, NCOL])
        MOD = sb("MOD", [P, 48, 2])
        A1 = sb("A1", [P, KT, 2])
        A2 = sb("A2", [P, KT, 2])
        SC = sb("SC", [P, KT, 2])
        SG = sb("SG", [P, 2, KT])
        LBE = sb("LBE", [P, 2, 2, 2])
        LBM = sb("LBM", [P, 2, 2])
        LBF = sb("LBF", [P, 2, 2])
        OML = sb("OML", [P, 2, 2])
        LMS = sb("LMS", [P, 2])
        NLAM = sb("NLAM", [P, 1])
        WAL = sb("WAL", [32, 2, P])
        SUBG = sb("SUBG", [P, 1])
        EPSC = sb("EPSC", [P, 1])
        NMX = sb("NMX", [P, 2, 2])
        SUMS = sb("SUMS", [P, 2, NU])
        RCP = sb("RCP", [P, NU])
        SS = sb("SS", [P, 10])
        DEC = sb("DEC", [P, NT])
        PS = ctx.enter_context(nc.psum_tensor("PS", [P, 4, 1024], F32))

        cosA, sinA, cosC, sinC = (CONST[:, i * TS:(i + 1) * TS] for i in range(4))
        IDENT, ONES, BLK64, BLK32, ROTA, ROTC = (CONST[:, 4 * TS + i * P:4 * TS + (i + 1) * P] for i in range(6))
        LPR = WORK[:, 0:64].rearrange("p (a n) -> p a n", a=2)
        SQ = [WORK[:, 0:T], WORK[:, T:2 * T]]
        RSTD = [WORK[:, 2 * T:3 * T], WORK[:, 3 * T:4 * T]]
        TMP = [WORK[:, 4 * T:5 * T], WORK[:, 5 * T:6 * T]]
        FB = [[WORK[:, (2 * b + h) * T:(2 * b + h + 1) * T] for h in range(2)] for b in range(2)]
        PROB = [WORK[:, 0:768], WORK[:, 768:1536]]
        PROBT = [WORK[:, 1536:2304], WORK[:, 2304:3072]]
        YTOK = WORK[:, 3072:3584]
        OALL = WORK[:, 3584:4352]
        OSQ = WORK[:, 4352:4608]
        SCORE = WORK[:, 0:2560].rearrange("p (g n t) -> p g n t", g=2, n=10)
        SX = WORK[:, 2560:3200]
        QM = [WORK[:, 3200:3520], WORK[:, 3520:3840]]
        KM = [WORK[:, 3840:4480], WORK[:, 4480:5120]]

        landed = [sem(f"landed{i}") for i in range(N_SLOT)]
        landed_q = sem("landed_q")
        slot_freed = sem("slot_freed")
        x_in, consts_in, params_in, stored, states_stored, y_stored = sem("x_in"), sem("consts_in"), sem("params_in"), sem("stored"), sem("states_stored"), sem("y_stored")
        eps_set, zero_set, mask_set = sem("eps_set"), sem("zero_set"), sem("mask_set")
        cond_sig, cond_ready = sem("cond_sig"), sem("cond_ready")
        lb_shift, lb_exp, lam_sum, lam_exp, small_ready = (sem(n) for n in ("lb_shift", "lb_exp", "lam_sum", "lam_exp", "small_ready"))
        ada_done, mod_ready = sem("ada_done"), sem("mod_ready")
        sq_ready, ms_ready, rstd_ready, h_ready = sem("sq_ready"), sem("ms_ready"), sem("rstd_ready"), sem("h_ready")
        gemm_full = sem("gemm_full")
        gemm_free = [sem(f"gemm_free{i}") for i in range(4)]
        silu_sig, gla_in = sem("silu_sig"), sem("gla_in")
        qk_sq, qk_ms, qk_rstd, qk_normed, qk_rot, qk_done = (sem(f"qk_{n}") for n in ("sq", "ms", "rstd", "normed", "rot", "done"))
        al_full, al_lin, al_log, al_pow, al_ready = (sem(f"al_{n}") for n in ("full", "lin", "log", "pow", "ready"))
        s_full, nmax_ready, p_ready, pt_full, pt_a, pt_b, pv_done = (
            sem(n) for n in ("s_full", "nmax_ready", "p_ready", "pt_full", "pt_a", "pt_b", "pv_done"))
        o_taken, csq_ready, crstd, ytok_ready, yt_full, yt_kept = (
            sem(n) for n in ("o_taken", "csq_ready", "crstd", "ytok_ready", "yt_full", "yt_kept"))
        lvl_ready, sc_full, sc_kept, scores_seen = sem("lvl_ready"), sem("sc_full"), sem("sc_kept"), sem("scores_seen")
        ko_ready, ko_turned, ko_kept, ds_full, st_ready = (sem(n) for n in ("ko_ready", "ko_turned", "ko_kept", "ds_full", "st_ready"))
        go_ss, go_rstd, go_y, gy_full, gy_kept = (sem(n) for n in ("go_ss", "go_rstd", "go_y", "gy_full", "gy_kept"))
        gate_ready, mix_done, xo_done = sem("gate_ready"), sem("mix_done"), sem("xo_done")
        centre_ready, g_silu, act_done = sem("centre_ready"), sem("g_silu"), sem("act_done")
        layer_done = sem("layer_done")
        dve, act_ = Chain(sem("dve_step")), Chain(sem("act_step"))
        N_PARAM = 16 * 8
        N_STORE = 16 * 2

        def pair(i):
            return PS[:, i, :]

        def use(n):
            if n < G_MIX:
                return n % 2, n // 2
            return (n - G_MIX) % 4, USES_Z[(n - G_MIX) % 4] + (n - G_MIX) // 4

        def wait_taken(eng, l, n, turns=0):
            p, k = use(n)
            eng.wait_ge(gemm_free[p], l * USES[p] + turns + (k + 1))

        def wait_room(eng, l, n, turns=0):
            p, k = use(n)
            eng.wait_ge(gemm_free[p], l * USES[p] + turns + k)

        def wait_full(eng, l, n, tiles=0):
            eng.wait_ge(gemm_full, l * N_GEMM + tiles + (n + 1))

        def z_index(tile):
            return next(n for n, t in enumerate(ZT_TILES) if t[1] not in ("tm", "tm1") and t[2] == tile)

        Z_OF = [z_index(t) for t in range(NZ) if t not in (BKF, BKF + 1, BKB, BKB + 1, DAB)]
        block = ctx.enter_context(nc.Block())

        @block.sync
        def _(sp):
            w_ada = A["w_ada"].rearrange("l (k p) n -> p l k n", p=P)
            w_in = A["w_in"].rearrange("l (k p) n -> p l k n", p=P)
            w_br = A["w_branch"].rearrange("l b (k p) n -> p l b k n", p=P)
            w_out = A["w_out"].rearrange("l (k p) n -> p l k n", p=P)
            w_up = A["w_up"].rearrange("l (k p) n -> p l k n", p=P)
            w_dn = A["w_down"].rearrange("l (k p) n -> p l k n", p=P)

            sp.sem_inc(slot_freed, N_SLOT - 1)
            sp.dma_start(XT[:], A["xT"]).then_inc(x_in, 16)
            with sp.Fori(0, DEPTH) as l:
                def slot_free(i, chunks=0):
                    sp.wait_ge(slot_freed, l * CHUNKS + chunks + (i + 1))

                def part(dst, w, s, k0, k1, col, width):
                    src = w[:, bass.ds(l, 1), k0:k1, bass.ds(col, width)].rearrange("p l k n -> p (l k) n")
                    sp.dma_start(dst, src).then_inc(landed[s], 16)

                def columns(w, s, col, width):
                    dst = RING[:, s, 0:8 * width].rearrange("p (k n) -> p k n", n=width)
                    part(dst[:, 0:4, :], w, s, 0, 4, col, width)
                    part(dst[:, 4:8, :], w, s, 4, 8, col, width)

                def up_chunk(j, s, col):
                    for h in range(2):
                        dst = RING[:, s, 1024 * h:1024 * h + 1024].rearrange("p (k n) -> p k n", n=P)
                        part(dst, w_up, s, 0, 8, col + (h * FF + j * P), P)

                with sp.Fori(0, 2) as it:
                    for s in range(4):
                        slot_free(C_ADA1 + s, it * 4)
                        columns(w_ada, s, it * 1024 + 256 * s, 256)
                for c in range(14):
                    slot_free(C_Z + c)
                    if c == 0:
                        dst = RING[:, C_Z % 4, :].rearrange("p (k j g d) -> p k j g d", j=2, g=2, d=64)
                        src = w_in[:, bass.ds(l, 1), :, 0:256].rearrange("p l k (g j d) -> p (l k) j g d", g=2, j=2)
                        for j in range(2):
                            for g in range(2):
                                sp.dma_start(dst[:, :, j, g], src[:, :, j, g]).then_inc(landed_q if j else landed[C_Z % 4], 16)
                        continue
                    columns(w_in, (C_Z + c) % 4, 256 * c, 256 if c < 13 else 32)
                with sp.Fori(0, 4) as it:
                    for s in range(4):
                        slot_free(C_ADA2 + s, it * 4)
                        columns(w_ada, (C_ADA2 + s) % 4, it * 1024 + (2048 + 256 * s), 256)
                with sp.Fori(0, KT) as it:
                    for n in range(4):
                        s = (C_MIX + n) % 4
                        slot_free(C_MIX + n, it * 4)
                        part(RING[:, s, 0:1024].rearrange("p (k n) -> p k n", n=P), w_in, s, 0, 8, it * P + (Z_COLS + n * D), P)
                        src = w_br[:, bass.ds(l, 1), n, :, bass.ds(it * P, P)].rearrange("p l k n -> p (l k) n")
                        sp.dma_start(RING[:, s, 1024:1280].rearrange("p (k n) -> p k n", n=P), src).then_inc(landed[s], 16)
                for c in range(4):
                    slot_free(C_OUT + c)
                    columns(w_out, (C_OUT + c) % 4, 256 * c, 256)
                with sp.Fori(0, 5) as it:
                    for j in range(4):
                        slot_free(C_UP + j, it * 4)
                        up_chunk(j, (C_UP + j) % 4, it * 4 * P)
                for j in range(20, 22):
                    slot_free(C_UP + j)
                    up_chunk(j, (C_UP + j) % 4, 0)
                with sp.Fori(0, 2) as it:
                    for j in range(8):
                        s = (C_DOWN + j) % 4
                        slot_free(C_DOWN + j, it * 8)
                        k0 = 11 * (j % 2)
                        dst = RING[:, s, 0:11 * P].rearrange("p (k n) -> p k n", n=P)
                        part(dst[:, 0:6, :], w_dn, s, k0, k0 + 6, it * 4 * P + (j // 2) * P, P)
                        part(dst[:, 6:11, :], w_dn, s, k0 + 6, k0 + 11, it * 4 * P + (j // 2) * P, P)
            sp.wait_ge(layer_done, DEPTH)
            sp.dma_start(O["yT"], XT[:]).then_inc(y_stored, 16)
            sp.wait_ge(y_stored, 16)

        @block.gpsimd
        def _(pool):
            pool.dma_start(CONST[:], A["const"]).then_inc(consts_in, 16)
            pool.memset(ST[:], 0.0).then_inc(zero_set, 1)
            pool.memset(WORK[:], 0.0).then_inc(zero_set, 1)
            pool.wait_ge(zero_set, 2)
            pool.dma_start(WORK[:, 0:NPASS * 64], A["mask"]).then_inc(consts_in, 16)

        @block.tensor
        def _(pe):
            pe.wait_ge(consts_in, 32)
            with pe.Fori(0, DEPTH) as l:
                def chunk(i, turns=0):
                    pe.wait_ge(landed[i % N_SLOT], l * (32 * CHUNKS // N_SLOT) + turns * 32 + 32 * (i // N_SLOT + 1))

                def release(ins, first):
                    if first:
                        ins.then_inc(slot_freed, 1)

                def wide(out, lhsT, rhs, start, stop, first=False):
                    release(pe.matmul(out[:, 0:TS], lhsT, rhs[:, 0:TS], start=start, stop=stop), first)
                    return pe.matmul(out[:, TS:T], lhsT, rhs[:, TS:T], start=start, stop=stop)

                def weights(i, width):
                    return RING[:, i % N_SLOT, 0:8 * width].rearrange("p (k n) -> p k n", n=width)

                def ada(first, col, turns):
                    for s in range(4):
                        chunk(first + s, turns)
                        w = weights(first + s, 256)
                        for h in range(2):
                            for k in range(KT):
                                last = pe.matmul(pair(3)[:, bass.ds(turns * 16 + (col + 4 * s + 2 * h), 2)],
                                                 w[:, k, h * P:(h + 1) * P], SC[:, k, :], start=k == 0, stop=k == KT - 1)
                                release(last, h == 0 and k == 0)
                        last.then_inc(ada_done, 1)

                def mean_square(which):
                    for k in range(KT):
                        pe.wait_ge(sq_ready, l * 16 + (8 * which + k + 1))
                        wide(pair(2), ONES, SQ[k % 2], k == 0, k == KT - 1).then_inc(ms_ready, 1)

                with pe.Fori(0, 2) as it:
                    pe.wait_ge(cond_ready, l + 1)
                    ada(C_ADA1, 0, it)
                mean_square(0)
                pe.wait_ge(h_ready, l * 16 + 8)
                for n, (c, kind, dst, j) in enumerate(ZT_TILES):
                    chunk(C_Z + c)
                    fresh = n == 0 or ZT_TILES[n - 1][0] != c
                    if n == 1:
                        pe.wait_ge(landed_q, l * 32 + 32)
                    wait_room(pe, l, n)
                    out = pair(use(n)[0])
                    if kind == "tm":
                        w = weights(C_Z + c, 256)
                        for i in range(3 * j, 3 if j == 0 else NT):
                            for k in range(KT):
                                last = pe.matmul(out[:, (i - 3 * j) * 256:(i - 3 * j + 1) * 256], HT[:, k, i * P:(i + 1) * P],
                                                 w[:, k, :], start=k == 0, stop=k == KT - 1)
                                release(last, fresh and i == 0 and k == 0)
                    elif kind == "tm1":
                        w = weights(C_Z + c, 256)
                        for i in range(NT):
                            for k in range(KT):
                                last = pe.matmul(out[:, i * P:(i + 1) * P], HT[:, k, i * P:(i + 1) * P],
                                                 w[:, k, P:2 * P], start=k == 0, stop=k == KT - 1)
                    elif kind == "r":
                        w = weights(C_Z + c, 32)
                        for k in range(KT):
                            last = wide(out[0:32], w[:, k, :], HT[:, k, :], k == 0, k == KT - 1, k == 0)
                    else:
                        w = weights(C_Z + c, 256)
                        for k in range(KT):
                            last = wide(out, w[:, k, j * P:(j + 1) * P], HT[:, k, :], k == 0, k == KT - 1, fresh and k == 0)
                    last.then_inc(gemm_full, 1)
                with pe.Fori(0, 4) as it:
                    ada(C_ADA2, 32, it)
                pe.wait_ge(mod_ready, l * 2 + 2)
                for i, (t, _, hd) in enumerate(QK_TILES):
                    pe.wait_ge(qk_sq, l * NQK + (i + 1))
                    pe.wait_ge(qk_rstd, l * NQK + i)
                    wide(pair(2), BLK64 if hd == 64 else BLK32, SQ[i % 2], True, True).then_inc(qk_ms, 1)
                    pe.wait_ge(qk_normed, l * NQK + (i + 1))
                    pe.wait_ge(qk_done, l * NQK + i)
                    pe.matmul(pair(3)[:, 0:TS], ROTA if hd == 64 else ROTC, ZT[:, t, 0:TS], start=True, stop=True).then_inc(qk_rot, 1)
                wait_taken(pe, l, NZT - 1)
                wait_taken(pe, l, NZT - 2)
                for d in range(2):
                    wide(pair(d), WAL[:, d, :], ZT[0:32, DR, :], True, True).then_inc(al_full, 1)
                pe.wait_ge(al_lin, l * 2 + 2)
                pe.wait_ge(qk_done, l * NQK + NQK)

                def scores(g):
                    i, u = divmod(g, NU)
                    q, r0, rows, k, kc, _, _, _ = ATT[u]
                    if g >= 2:
                        pe.wait_ge(p_ready, l * NG + (g - 1))
                    out = pair(1 + g % 2)
                    qs = ZT[r0:r0 + rows, q, i * P:(i + 1) * P]
                    if i < NT - 1:
                        pe.matmul(out[:, 0:TS], qs, ZT[r0:r0 + rows, k, 0:TS], start=True, stop=True)
                        last = pe.matmul(out[:, TS:TS + PAST], qs, KTC[r0:r0 + rows, kc, :], start=True, stop=True)
                    else:
                        last = pe.matmul(out[:, 0:P], qs, ZT[r0:r0 + rows, k, TS:T], start=True, stop=True)
                    last.then_inc(s_full, 1)

                def turn(g):
                    i, u = divmod(g, NU)
                    pe.wait_ge(p_ready, l * NG + (g + 1))
                    pe.wait_ge(pt_a, l * NG + g)
                    pe.wait_ge(pt_b, l * NG + g)
                    pe.wait_ge(yt_kept, l * NT + sum(g > y_step(t) for t in range(NT)))
                    for k in range(keys(i)):
                        last = pe.transpose(pair(3)[:, k * P:(k + 1) * P], PROB[g % 2][:, k * P:(k + 1) * P], IDENT)
                    last.then_inc(pt_full, 1)

                def weigh(g):
                    i, u = divmod(g, NU)
                    v, place = ATT[u][5], ATT[u][7]
                    pe.wait_ge(pt_a, l * NG + (g + 1))
                    pe.wait_ge(pt_b, l * NG + (g + 1))
                    if u == 0 and i:
                        pe.wait_ge(o_taken, l * NT + i)
                    for k in range(keys(i)):
                        rhs = V[:, NT - 1, v:v + 64] if i == NT - 1 else V[:, k, v:v + 64] if k < 4 else VC[:, k - 4, v:v + 64]
                        last = pe.matmul(pair(0)[:, place * 64:(place + 1) * 64], PROBT[g % 2][:, k * P:(k + 1) * P], rhs,
                                         start=k == 0, stop=k == keys(i) - 1)
                    last.then_inc(pv_done, 1)

                def turn_y(i):
                    pe.wait_ge(ytok_ready, l * NT + (i + 1))
                    g = min(y_step(i) + 1, NG)
                    pe.wait_ge(pt_a, l * NG + g)
                    pe.wait_ge(pt_b, l * NG + g)
                    for k in range(4):
                        last = pe.transpose(pair(3)[:, k * P:(k + 1) * P], YTOK[:, k * P:(k + 1) * P], IDENT)
                    last.then_inc(yt_full, 1)

                scores(0)
                for g in range(NG + 8):
                    if g + 1 < NG:
                        scores(g + 1)
                    if g < NG:
                        turn(g)
                    if 1 <= g <= NG:
                        weigh(g - 1)
                    for i in range(NT):
                        if g == y_step(i):
                            turn_y(i)

                pe.wait_ge(yt_kept, l * NT + NT)
                pe.wait_ge(al_ready, l * 2 + 2)
                cnt = 0

                def group_room(cnt):
                    if cnt >= 2:
                        pe.wait_ge(sc_kept, l * NSC + (cnt - 1))
                    return pair(2 + cnt % 2)

                for x, (q, _, a, gate, vb, rows, groups, _) in enumerate(GLA):
                    for p in range(NPASS):
                        pe.wait_ge(lvl_ready, l * 45 + (15 * x + max(p, 1)))
                        for grp in range(groups):
                            out = group_room(cnt)
                            cnt += 1
                            for n in range(10):
                                i, hh = divmod(n, 2)
                                r0 = (2 * grp + hh) * rows
                                if p < 2:
                                    lhsT = KO[r0:r0 + rows, i * P:(i + 1) * P]
                                    rhs = ZT[r0:r0 + rows, q, i * P + p:(i + 1) * P:2]
                                else:
                                    lhsT = KM[p % 2][r0:r0 + rows, i * P:(i + 1) * P]
                                    rhs = QM[p % 2][r0:r0 + rows, i * 64:(i + 1) * 64]
                                last = pe.matmul(out[:, hh * TS + i * 64:hh * TS + (i + 1) * 64], lhsT, rhs, start=True, stop=True)
                            last.then_inc(sc_full, 1)
                        if p in (1 + LEVELS, 1 + 2 * LEVELS):
                            d = 0 if p == 1 + LEVELS else 1
                            n6 = 2 * x + d
                            pe.wait_ge(ko_ready, l * 6 + (n6 + 1))
                            pe.wait_ge(gy_kept, l * NGRP + sum(g[6] for g in GLA[:x]))
                            for i in range(NT):
                                last = pe.transpose(pair(0)[:, i * P:(i + 1) * P], KO[:, i * P:(i + 1) * P], IDENT)
                            last.then_inc(ko_turned, 1)
                            pe.wait_ge(ko_kept, l * 6 + (n6 + 1))
                            if n6:
                                pe.wait_ge(st_ready, l * 6 + n6)
                            for i in range(NT):
                                for h in range(P // rows):
                                    last = pe.matmul(pair(1)[h * rows:(h + 1) * rows, i * 64:(i + 1) * 64],
                                                     KOT[:, i, h * rows:(h + 1) * rows], V[:, i, vb + 64 * h:vb + 64 * h + 64],
                                                     start=True, stop=True)
                            last.then_inc(ds_full, 1)
                    pe.wait_ge(st_ready, l * 6 + (2 * x + 2))
                    pe.wait_ge(sc_kept, l * NSC + cnt)
                    for grp in range(groups):
                        out = group_room(cnt)
                        cnt += 1
                        for n in range(10):
                            i, hh = divmod(n, 2)
                            h = 2 * grp + hh
                            r = slice(h * rows, (h + 1) * rows)
                            o = out[:, hh * TS + i * 64:hh * TS + (i + 1) * 64]
                            pe.matmul(o, SCORE[:, grp, hh * NT + i, :], V[:, i, vb + 64 * h:vb + 64 * h + 64], start=True, stop=False)
                            for d in range(2):
                                last = pe.matmul(o, ZT[r, a[d], i * P:(i + 1) * P], ST[r, d, x, i, :], start=False, stop=d == 1)
                        last.then_inc(sc_full, 1)
                    for grp in range(groups):
                        g0 = sum(g[6] for g in GLA[:x]) + grp
                        pe.wait_ge(go_y, l * NGRP + (g0 + 1))
                        if grp:
                            pe.wait_ge(gy_kept, l * NGRP + g0)
                        for i in range(NT):
                            last = pe.transpose(pair(0)[:, i * P:(i + 1) * P], KM[1][:, i * P:(i + 1) * P], IDENT)
                        last.then_inc(gy_full, 1)

                with pe.Fori(0, KT) as it:
                    pe.wait_ge(gy_kept, l * NGRP + NGRP)
                    for n in range(4):
                        chunk(C_MIX + n, it)
                        w = RING[:, (C_MIX + n) % 4, 0:1280].rearrange("p (k n) -> p k n", n=P)
                        g = G_MIX + 2 * n
                        wait_room(pe, l, g, it * 2)
                        for k in range(KT):
                            last = wide(pair(use(g)[0]), w[:, k, :], HT[:, k, :], k == 0, k == KT - 1, k == 0)
                        last.then_inc(gemm_full, 1)
                        wait_room(pe, l, g + 1, it * 2)
                        for k in range(2):
                            last = wide(pair(use(g + 1)[0]), w[:, KT + k, :], ZT[:, 2 * n + k, :], k == 0, k == 1)
                        last.then_inc(gemm_full, 1)
                pe.wait_ge(mix_done, l * KT + KT)
                for c in range(4):
                    chunk(C_OUT + c)
                    w = weights(C_OUT + c, 256)
                    for h in range(2):
                        g = G_OUT + 2 * c + h
                        wait_room(pe, l, g)
                        for k in range(KT):
                            last = wide(pair(use(g)[0]), w[:, k, h * P:(h + 1) * P], ZT[:, MIXT + k, :], k == 0, k == KT - 1, h == 0 and k == 0)
                        last.then_inc(gemm_full, 1)
                mean_square(1)

                def up(j, turns):
                    chunk(C_UP + j, turns)
                    for h in range(2):
                        w = RING[:, (C_UP + j) % 4, 1024 * h:1024 * h + 1024].rearrange("p (k n) -> p k n", n=P)
                        g = G_UP + 2 * j + h
                        wait_room(pe, l, g, turns * 2)
                        for k in range(KT):
                            last = wide(pair(use(g)[0]), w[:, k, :], HT[:, k, :], k == 0, k == KT - 1, h == 0 and k == 0)
                        last.then_inc(gemm_full, 1)

                with pe.Fori(0, 5) as it:
                    pe.wait_ge(h_ready, l * 16 + 16)
                    for j in range(4):
                        up(j, it)
                for j in range(20, 22):
                    up(j, 0)
                with pe.Fori(0, 2) as it:
                    pe.wait_ge(act_done, l * FT + (FT + 2))
                    for j in range(4):
                        g = G_DOWN + j
                        wait_room(pe, l, g, it)
                        for h in range(2):
                            i = C_DOWN + 2 * j + h
                            chunk(i, it * 2)
                            w = RING[:, i % 4, 0:11 * P].rearrange("p (k n) -> p k n", n=P)
                            for k in range(11):
                                last = wide(pair(use(g)[0]), w[:, k, :], ZT[:, 11 * h + k, :], h == 0 and k == 0, h == 1 and k == 10, k == 0)
                        last.then_inc(gemm_full, 1)

        @block.scalar
        def _(act):
            step = act_
            act.wait_ge(x_in, 16)
            act.wait_ge(eps_set, 1)
            act.wait_ge(zero_set, 2)
            with act.Fori(0, DEPTH) as l:
                step.layer(l)
                at = bass.ds(l, 1)
                act.wait_ge(layer_done, l)
                act.wait_ge(states_stored, l * 16)
                act.dma_start(COLS[:], A["cols"][at].rearrange("l p n -> p (l n)")).then_inc(params_in, 16)
                act.dma_start(WAL[:], A["w_alpha"][at].rearrange("l p d n -> p (l d) n")).then_inc(params_in, 16)
                act.dma_start(KTC[:], A["keysT"][at].rearrange("l p a n -> p (l a) n")).then_inc(params_in, 16)
                act.dma_start(VC[:], A["vals"][at].rearrange("l (t p) n -> p (l t) n", p=P)).then_inc(params_in, 16)
                for d in range(2):
                    first = 0 if d == 0 else TS // P - 1
                    act.dma_start(ST[:, d, 0:2, first, :], A["hgrn"][at, :, d].rearrange("l p u v -> p (l u) v")).then_inc(params_in, 16)
                    act.dma_start(ST[:, d, 2:3, first, :], A["gla"][at, :, d:d + 1].rearrange("l p u v -> p (l u) v")).then_inc(params_in, 16)
                act.wait_ge(params_in, l * N_PARAM + N_PARAM)

                def inv_root(out, src, scale=1.0):
                    step.mark(act.activation(out, src, ACT.Ln, bias=EPSC[:, 0:1], scale=scale))
                    step.settle(act)
                    return act.activation(out, out, ACT.Exp, scale=-0.5)

                def squares(which):
                    for k in range(KT):
                        if k >= 2:
                            act.wait_ge(ms_ready, l * 16 + (8 * which + k - 1))
                        act.activation(SQ[k % 2], XT[:, k, :], ACT.Square).then_inc(sq_ready, 1)
                    act.wait_ge(ms_ready, l * 16 + (8 * which + 8))
                    inv_root(RSTD[0], pair(2)[:, 0:T]).then_inc(rstd_ready, 1)

                act.activation(SG[:].rearrange("p a b -> p (a b)"), COLS[:, C_COND:C_COND + 16], ACT.Sigmoid).then_inc(cond_sig, 1)
                act.wait_ge(lb_shift, l + 1)
                act.activation(LBE[:].rearrange("p a b c -> p (a b c)"), LBE[:].rearrange("p a b c -> p (a b c)"), ACT.Exp).then_inc(lb_exp, 1)
                act.wait_ge(lam_sum, l + 1)
                act.activation(LMS[:], LMS[:], ACT.Exp).then_inc(lam_exp, 1)
                squares(0)
                sig = 0
                for n, (c, kind, dst, j) in enumerate(ZT_TILES):
                    wait_full(act, l, n)
                    p = use(n)[0]
                    src = pair(p)[:, 0:T]
                    if kind == "tm":
                        m = 3 - j
                        act.activation(V[:, 3 * j:3 * j + m, dst:dst + 256], pair(p)[:, 0:256 * m].rearrange("p (i n) -> p i n", n=256),
                                       ACT.Copy).then_inc(gemm_free[p], 1)
                    elif kind == "tm1":
                        act.activation(V[:, :, dst:dst + P], src.rearrange("p (i n) -> p i n", n=P), ACT.Copy).then_inc(gemm_free[p], 1)
                    elif kind == "r":
                        act.activation(ZT[0:32, dst, :], src[0:32], ACT.Copy).then_inc(gemm_free[p], 1)
                    elif kind == "silu":
                        act.activation(ZT[:, dst, :], src, ACT.Sigmoid).then_inc(silu_sig, 1)
                    elif kind == "ff":
                        step.mark(act.activation(ZT[:, dst, :], src, ACT.Sigmoid))
                        act.activation(ZT[:, dst + BKF - BFF, :], src, ACT.Sigmoid, scale=-1.0).then_inc(gemm_free[p], 1)
                    elif kind == "dqk" and j == 0:
                        act.activation(ZT[:, dst, :], src, ACT.Copy, scale=32 ** -0.5).then_inc(gemm_free[p], 1)
                    else:
                        act.activation(ZT[:, dst, :], src, ACT.Copy).then_inc(gemm_free[p], 1)

                def qk_square(i):
                    wait_taken(act, l, z_index(QK_TILES[i][0]))
                    if i >= 2:
                        act.wait_ge(qk_ms, l * NQK + (i - 1))
                    act.activation(SQ[i % 2], ZT[:, QK_TILES[i][0], :], ACT.Square).then_inc(qk_sq, 1)

                qk_square(0)
                for i in range(NQK):
                    if i + 1 < NQK:
                        qk_square(i + 1)
                    act.wait_ge(qk_ms, l * NQK + (i + 1))
                    if i >= 2:
                        act.wait_ge(qk_normed, l * NQK + (i - 1))
                    inv_root(RSTD[i % 2], pair(2)[:, 0:T]).then_inc(qk_rstd, 1)
                act.wait_ge(qk_done, l * NQK + NQK)
                act.dma_start(O["keysT"][at].rearrange("l p a t -> p (l a) t"), ZT[:, AK:AK + 3, TS:T]).then_inc(stored, 16)
                act.dma_start(O["vals"][at].rearrange("l p n -> p (l n)"), V[:, NT - 1, 0:V_B]).then_inc(stored, 16)
                for d in range(2):
                    act.wait_ge(al_full, l * 2 + (d + 1))
                    act.activation(TMP[d], pair(d)[:, 0:T], ACT.Identity, bias=COLS[:, C_AB + d:C_AB + d + 1])
                    act.activation(SQ[d], pair(d)[:, 0:T], ACT.Abs, bias=COLS[:, C_AB + d:C_AB + d + 1]).then_inc(al_lin, 1)
                for d in range(2):
                    act.wait_ge(al_lin, l * 2 + (d + 1))
                    step.mark(act.activation(SQ[d], SQ[d], ACT.Exp, scale=-1.0))
                    step.settle(act)
                    act.activation(SQ[d], SQ[d], ACT.Ln, bias=1.0).then_inc(al_log, 1)
                for d in range(2):
                    act.wait_ge(al_pow, l * 2 + (d + 1))
                    act.activation(ZT[:, (DAF, DAB)[d], :], TMP[d], ACT.Exp, scale=1.0 / 16).then_inc(al_ready, 1)

                for g in range(NG + 8):
                    i, u = divmod(g, NU)
                    if g < NG:
                        n = keys(i) * P
                        act.wait_ge(nmax_ready, l * NG + (g + 1))
                        if g >= 2:
                            act.wait_ge(pt_full, l * NG + (g - 1))
                        elif g == 0:
                            act.wait_ge(al_ready, l * 2 + 2)
                        if u == 0 and i >= 2:
                            act.wait_ge(o_taken, l * NT + (i - 1))
                        act.activation(PROB[g % 2][:, 0:n], pair(1 + g % 2)[:, 0:n], ACT.Exp, bias=NMX[:, g % 2, 1:2],
                                       scale=ATT[u][6], accum_out=SUMS[:, i % 2, ATT[u][7]:ATT[u][7] + 1]).then_inc(p_ready, 1)
                        act.wait_ge(pt_full, l * NG + (g + 1))
                        if g >= 2:
                            act.wait_ge(pv_done, l * NG + (g - 1))
                        act.activation(PROBT[g % 2][:, 0:min(n, TS)], pair(3)[:, 0:min(n, TS)], ACT.Copy).then_inc(pt_a, 1)
                    for i in range(NT):
                        if g == tail_step(i) + 1:
                            act.wait_ge(csq_ready, l * NT + (i + 1))
                            inv_root(SS[:, 0:4], SS[:, 0:4], 1.0 / 64).then_inc(crstd, 1)

                for x, g in enumerate(GLA):
                    for d in range(2):
                        n6 = 2 * x + d
                        act.wait_ge(ko_turned, l * 6 + (n6 + 1))
                        if n6:
                            act.wait_ge(ds_full, l * 6 + n6)
                        act.activation(KOT[:].rearrange("p i n -> p (i n)"), pair(0)[:, 0:T], ACT.Copy).then_inc(ko_kept, 1)
                    for grp in range(g[6]):
                        act.wait_ge(go_ss, l * NGRP + (sum(y[6] for y in GLA[:x]) + grp + 1))
                        inv_root(SS[:], SS[:], 1.0 / 64).then_inc(go_rstd, 1)

                act.wait_ge(st_ready, l * 6 + 6)
                act.dma_start(O["fin"][at].rearrange("l p n -> p (l n)"), FIN[:].rearrange("p a b c -> p (a b c)")).then_inc(states_stored, 16)
                with act.Fori(0, KT) as it:
                    for n in range(4):
                        g = G_MIX + 2 * n
                        wait_full(act, l, g, it * 8)
                        wait_room(act, l, g + 1, it * 2)
                        act.activation(SQ[n % 2], pair(use(g)[0])[:, 0:T], ACT.Sigmoid).then_inc(gemm_free[use(g)[0]], 1)
                act.wait_ge(xo_done, l * KT + KT)
                squares(1)

                def ffn(j, turns):
                    f = turns * 4 + j
                    for h in range(2):
                        g = G_UP + 2 * j + h
                        wait_full(act, l, g, turns * 8)
                        if h == 0:
                            act.wait_ge(act_done, l * FT + f + 1)
                        col = f + h * FT
                        act.activation(FB[j % 2][h], pair(use(g)[0])[:, 0:T], ACT.Identity,
                                       bias=COLS[:, bass.ds(col + C_CB, 1)], scale=COLS[:, bass.ds(col + C_W1, 1)]).then_inc(centre_ready, 1)
                    wait_taken(act, l, g, turns * 2)
                    act.activation(FB[j % 2][1], FB[j % 2][1], ACT.Silu).then_inc(g_silu, 1)

                with act.Fori(0, 5) as it:
                    for j in range(4):
                        ffn(j, it)
                for j in range(20, 22):
                    ffn(j, 0)
                step.end(act)
            act.wait_ge(stored, DEPTH * N_STORE)
            act.wait_ge(states_stored, DEPTH * 16)

        @block.vector
        def _(v):
            step = dve
            nv = nc.vector
            v.wait_ge(x_in, 16)
            v.wait_ge(consts_in, 32)
            nv.tensor_copy(MASK[:].rearrange("p a b -> p (a b)"), WORK[:, 0:NPASS * 64]).then_inc(mask_set, 1)
            v.wait_ge(mask_set, 1)
            nv.memset(EPSC[:], EPS).then_inc(eps_set, 1)
            v.sem_inc(act_done, 2)
            with v.Fori(0, DEPTH) as l:
                step.layer(l)

                def link(ins):
                    step.mark(ins)
                    step.settle(v)

                def bc(ap, n):
                    return ap.to_broadcast(list(ap.shape[:-1]) + [n])

                v.wait_ge(params_in, l * N_PARAM + N_PARAM)
                lbl = COLS[:, C_LB:C_LB + 8].rearrange("p (d l t) -> p d l t", d=2, l=2)
                link(nv.tensor_tensor(LBM[:], lbl[:, :, 0, :], lbl[:, :, 1, :], ALU.max))
                step.mark(nv.tensor_tensor(LBE[:, :, 0, :], lbl[:, :, 0, :], LBM[:], ALU.subtract))
                nv.tensor_tensor(LBE[:, :, 1, :], lbl[:, :, 1, :], LBM[:], ALU.subtract).then_inc(lb_shift, 1)
                lam = COLS[:, C_LAM:C_LAM + 128].rearrange("p (a b n) -> p a b n", a=2, b=2)
                link(nv.tensor_tensor(LPR, lam[:, :, 0, :], lam[:, :, 1, :], ALU.mult))
                nv.tensor_reduce(LMS[:], LPR, AX.X, ALU.add).then_inc(lam_sum, 1)
                v.wait_ge(cond_sig, l + 1)
                nv.tensor_tensor(SC[:].rearrange("p k g -> p g k"), COLS[:, C_COND:C_COND + 16].rearrange("p (g k) -> p g k", g=2),
                                 SG[:], ALU.mult).then_inc(cond_ready, 1)
                v.wait_ge(lb_exp, l + 1)
                link(nv.tensor_tensor(LBM[:], LBE[:, :, 0, :], LBE[:, :, 1, :], ALU.add))
                link(nv.reciprocal(LBM[:], LBM[:]))
                link(nv.tensor_tensor(LBM[:], LBM[:], LBE[:, :, 1, :], ALU.mult))
                link(nv.tensor_scalar(LBM[:], LBM[:], COLS[:, C_LC + 2:C_LC + 3], None, ALU.mult))
                step.mark(nv.tensor_scalar(LBF[:], LBM[:], LB_FLOOR, None, ALU.max))
                step.mark(nv.tensor_scalar(OML[:], LBM[:], -1.0, 1.0, ALU.mult, ALU.add))
                v.wait_ge(lam_exp, l + 1)
                link(nv.tensor_tensor(NLAM[:], LMS[:, 1:2], LMS[:, 0:1], ALU.subtract))
                step.mark(nv.tensor_tensor(NLAM[:], NLAM[:], COLS[:, C_LC:C_LC + 1], ALU.subtract))
                step.mark(nv.tensor_tensor(SUBG[:], COLS[:, C_SUB:C_SUB + 1], COLS[:, C_LC + 1:C_LC + 2], ALU.mult))

                def modulation(which, a, b):
                    v.wait_ge(ada_done, l * 24 + (8, 24)[which])
                    ps = pair(3)[:, 2 * a:2 * b].rearrange("p (j g) -> p j g", g=2)
                    link(nv.tensor_tensor(MOD[:, a:b, :], ps, bc(COLS[:, C_BADA + a:C_BADA + b].rearrange("p (j o) -> p j o", o=1), 2), ALU.add))
                    scale, dst, gain = (MOD[:, 8:16, :], A1, C_N1) if which == 0 else (MOD[:, 32:40, :], A2, C_N2)
                    g = COLS[:, gain:gain + KT].rearrange("p (j o) -> p j o", o=1)
                    nv.scalar_tensor_tensor(out=dst[:], in0=scale, scalar=1.0, in1=bc(g, 2), op0=ALU.add, op1=ALU.mult).then_inc(mod_ready, 1)
                    v.wait_ge(mod_ready, l * 2 + (which + 1))

                def normed(which, gain, shift):
                    v.wait_ge(rstd_ready, l * 2 + (which + 1))
                    for k in range(KT):
                        link(nv.tensor_tensor(TMP[k % 2], XT[:, k, :], RSTD[0], ALU.mult))
                        for g, (a, b) in enumerate(SEG):
                            last = nv.tensor_scalar(HT[:, k, a:b], TMP[k % 2][:, a:b], gain[:, k, g:g + 1], MOD[:, shift + k, g:g + 1],
                                                    ALU.mult, ALU.add)
                            if g == 0:
                                step.mark(last)
                        last.then_inc(h_ready, 1)

                modulation(0, 0, 16)
                normed(0, A1, 0)
                sig = 0
                for n, (c, kind, dst, j) in enumerate(ZT_TILES):
                    if kind == "silu":
                        sig += 1
                        v.wait_ge(silu_sig, l * 6 + sig)
                        p = use(n)[0]
                        nv.tensor_tensor(ZT[:, dst, :], ZT[:, dst, :], pair(p)[:, 0:T], ALU.mult).then_inc(gemm_free[p], 1)
                    if kind == "ff":
                        d = (dst - BFF) // 2
                        wait_taken(v, l, n)
                        step.mark(nv.tensor_scalar(ZT[:, dst, :], ZT[:, dst, :], OML[:, d, j:j + 1], LBF[:, d, j:j + 1], ALU.mult, ALU.add))
                        nv.tensor_scalar(ZT[:, dst + BKF - BFF, :], ZT[:, dst + BKF - BFF, :], OML[:, d, j:j + 1], None, ALU.mult).then_inc(gla_in, 1)
                modulation(1, 16, 48)

                for i, (t, col, hd) in enumerate(QK_TILES):
                    cos, sin = (cosA, sinA) if hd == 64 else (cosC, sinC)
                    v.wait_ge(qk_rstd, l * NQK + (i + 1))
                    nv.scalar_tensor_tensor(out=ZT[:, t, :], in0=ZT[:, t, :], scalar=COLS[:, col:col + 1], in1=RSTD[i % 2],
                                            op0=ALU.mult, op1=ALU.mult).then_inc(qk_normed, 1)
                    v.wait_ge(qk_normed, l * NQK + (i + 1))
                    step.mark(nv.tensor_tensor(TMP[0][:, 0:TS], ZT[:, t, 0:TS], cos, ALU.mult))
                    v.wait_ge(qk_rot, l * NQK + (i + 1))
                    link(nv.tensor_tensor(TMP[1][:, 0:TS], pair(3)[:, 0:TS], sin, ALU.mult))
                    nv.tensor_tensor(ZT[:, t, 0:TS], TMP[0][:, 0:TS], TMP[1][:, 0:TS], ALU.add).then_inc(qk_done, 1)
                for d in range(2):
                    v.wait_ge(al_log, l * 2 + (d + 1))
                    nv.scalar_tensor_tensor(out=TMP[d], in0=TMP[d], scalar=0.0, in1=SQ[d], op0=ALU.min, op1=ALU.subtract).then_inc(al_pow, 1)

                def maxima(g):
                    i, u = divmod(g, NU)
                    n = keys(i) * P
                    v.wait_ge(s_full, l * NG + (g + 1))
                    link(nv.tensor_reduce(NMX[:, g % 2, 0:1], pair(1 + g % 2)[:, 0:n], AX.X, ALU.max, negate=True))
                    nv.tensor_scalar(NMX[:, g % 2, 1:2], NMX[:, g % 2, 0:1], ATT[u][6], None, ALU.mult).then_inc(nmax_ready, 1)

                v.wait_ge(al_ready, l * 2 + 2)
                maxima(0)
                for g in range(NG + 8):
                    i, u = divmod(g, NU)
                    if g + 1 < NG:
                        maxima(g + 1)
                    if g < NG:
                        n = keys(i) * P
                        v.wait_ge(pt_full, l * NG + (g + 1))
                        if g >= 2:
                            v.wait_ge(pv_done, l * NG + (g - 1))
                        if n > TS:
                            nv.tensor_copy(PROBT[g % 2][:, TS:n], pair(3)[:, TS:n]).then_inc(pt_b, 1)
                        else:
                            v.sem_inc(pt_b, 1)
                    for i in range(NT):
                        if g == tail_step(i):
                            v.wait_ge(pv_done, l * NG + NU * (i + 1))
                            link(nv.reciprocal(RCP[:], SUMS[:, i % 2, :]))
                            link(nv.tensor_scalar(RCP[:, 8:12], RCP[:, 8:12], NLAM[:, 0:1], None, ALU.mult))
                            if i:
                                v.wait_ge(yt_full, l * NT + i)
                            o = pair(0)[:, 0:768].rearrange("p (u n) -> p u n", n=64)
                            r = RCP[:].rearrange("p (u o) -> p u o", o=1)
                            step.mark(nv.tensor_tensor(YTOK[:, 0:256].rearrange("p (u n) -> p u n", n=64), o[:, 0:4, :], bc(r[:, 0:4, :], 64), ALU.mult))
                            nv.tensor_tensor(OALL[:, 256:768].rearrange("p (u n) -> p u n", n=64), o[:, 4:12, :], bc(r[:, 4:12, :], 64),
                                             ALU.mult).then_inc(o_taken, 1)
                            v.wait_ge(o_taken, l * NT + (i + 1))
                            link(nv.tensor_tensor(OALL[:, 0:256], OALL[:, 256:512], OALL[:, 512:768], ALU.add))
                            link(nv.tensor_tensor(OSQ, OALL[:, 0:256], OALL[:, 0:256], ALU.mult))
                            nv.tensor_reduce(SS[:, 0:4], OSQ.rearrange("p (u n) -> p u n", n=64), AX.X, ALU.add).then_inc(csq_ready, 1)
                        if g == tail_step(i) + 1:
                            v.wait_ge(crstd, l * NT + (i + 1))
                            ss = SS[:, 0:4].rearrange("p (u o) -> p u o", o=1)
                            nv.tensor_tensor(YTOK[:, 256:512].rearrange("p (u n) -> p u n", n=64),
                                             OALL[:, 0:256].rearrange("p (u n) -> p u n", n=64), bc(ss, 64), ALU.mult).then_inc(ytok_ready, 1)
                        if g == y_step(i):
                            v.wait_ge(yt_full, l * NT + (i + 1))
                            y = pair(3)[:, 0:512].rearrange("p (a b t) -> p a b t", a=2, b=2)
                            step.mark(nv.tensor_copy(ZT[:, AQ:AQ + 2, i * P:(i + 1) * P], y[:, 0, :, :]))
                            nv.tensor_scalar(ZT[:, CQ:CQ + 2, i * P:(i + 1) * P], y[:, 1, :, :], SUBG[:, 0:1], None, ALU.mult).then_inc(yt_kept, 1)

                v.wait_ge(yt_kept, l * NT + NT)
                v.wait_ge(gla_in, l * 4 + 4)
                cnt = 0

                def keep(grp, p):
                    nonlocal cnt
                    v.wait_ge(sc_full, l * NSC + (cnt + 1))
                    v.sem_inc(scores_seen, 1)
                    for hh in range(2):
                        ps, tile = pair(2 + cnt % 2)[:, hh * TS:hh * TS + 320], SCORE[:, grp, hh * NT:(hh + 1) * NT, :]
                        if p < 2:
                            out, m = tile[:, :, p::2], MASK[:, 2 * LEVELS + p, :]
                            data = ps.rearrange("p (n t) -> p n t", n=NT)
                            m = m.rearrange("p (o t) -> p o t", o=1).to_broadcast([P, NT, 64])
                        else:
                            d, m0 = divmod(p - 2, LEVELS)
                            h = 1 << m0
                            out = tile.rearrange("p n (b w h) -> p n b w h", w=2, h=h)[:, :, :, 1 - d, :]
                            data = ps.rearrange("p (n b h) -> p n b h", n=NT, h=h)
                            m = MASK[:, p - 2, :].rearrange("p (o b h) -> p o b h", o=1, h=h).to_broadcast([P, NT, 64 // h, h])
                        ins = nv.copy_predicated(out, m, data)
                        if hh == 0:
                            step.mark(ins)
                    ins.then_inc(sc_kept, 1)
                    cnt += 1

                def states(x, d):
                    v.wait_ge(ds_full, l * 6 + (2 * x + d + 1))
                    ds = pair(1)[:, 0:320].rearrange("p (i n) -> p i n", n=64)
                    for i in (range(0, 3) if d == 0 else range(3, 0, -1)):
                        nxt = i + 1 if d == 0 else i - 1
                        link(nv.scalar_tensor_tensor(out=ST[:, d, x, nxt, :], in0=ST[:, d, x, i, :], scalar=DEC[:, i:i + 1], in1=ds[:, i, :],
                                                     op0=ALU.mult, op1=ALU.add))
                    nv.tensor_copy(FIN[:, d, x, :], ds[:, NT - 1, :]).then_inc(st_ready, 1)

                for x, (q, ks, a, gate, vb, rows, groups, gain) in enumerate(GLA):
                    before = sum(g[6] for g in GLA[:x])
                    if x:
                        v.wait_ge(ko_turned, l * 6 + 2 * x)
                    if ks[0] == ks[1]:
                        ins = nv.tensor_scalar(KO[:], ZT[:, ks[0], :], 2.0, None, ALU.mult)
                    else:
                        ins = nv.tensor_tensor(KO[:], ZT[:, ks[0], :], ZT[:, ks[1], :], ALU.add)
                    ins.then_inc(lvl_ready, 1)
                    for d in range(2):
                        R = ZT[:, a[d], :]
                        link(nv.memset(SX, 1.0))
                        for m in range(LEVELS):
                            p, h = 2 + LEVELS * d + m, 1 << m
                            near, far = (1, 0) if d == 0 else (0, 1)

                            def half(ap, w):
                                return ap.rearrange("p (b w h) -> p b w h", w=2, h=h)[:, :, w, :]

                            def edge(ap, w):
                                e = half(ap, w)
                                return e[:, :, h - 1:h] if d == 0 else e[:, :, 0:1]

                            k_out, q_out = KM[p % 2], QM[p % 2]
                            if p >= 4:
                                v.wait_ge(sc_full, l * NSC + (before * (NPASS + 1) + groups * (p - 1)))
                            step.mark(nv.tensor_tensor(half(k_out, far), half(ZT[:, ks[d], :], far), half(SX, far), ALU.mult))
                            nv.tensor_tensor(q_out.rearrange("p (b h) -> p b h", h=h), half(ZT[:, q, :], near), half(R, near), ALU.mult).then_inc(lvl_ready, 1)
                            link(nv.tensor_tensor(half(SX, far), half(SX, far), bc(edge(R, near), h), ALU.mult))
                            link(nv.tensor_tensor(half(R, near), half(R, near), bc(edge(R, far), h), ALU.mult))
                            for done in ([0, 1] if p == 2 else [p - 1]):
                                for grp in range(groups):
                                    keep(grp, done)
                            if m == 1 and d == 1:
                                states(x, 0)
                        edges = R.rearrange("p (i t) -> p i t", t=P)[:, :, P - 1 if d == 0 else 0]
                        step.mark(nv.tensor_copy(DEC[:], edges))
                        if d:
                            v.wait_ge(ko_turned, l * 6 + (2 * x + 1))
                        link(nv.tensor_tensor(KO[:], ZT[:, ks[d], :], SX, ALU.mult))
                        nv.tensor_tensor(R, ZT[:, q, :], R, ALU.mult).then_inc(ko_ready, 1)
                        if d:
                            for grp in range(groups):
                                keep(grp, p)
                            states(x, 1)
                    for grp in range(groups):
                        g0 = before + grp
                        v.wait_ge(sc_full, l * NSC + (cnt + 1))
                        o = pair(2 + cnt % 2).rearrange("p (hh c) -> p hh c", hh=2)[:, :, 0:320].rearrange("p hh (i v) -> p hh i v", v=64)
                        nv.tensor_copy(KM[0].rearrange("p (i hh v) -> p hh i v", hh=2, v=64), o).then_inc(sc_kept, 1)
                        cnt += 1
                        v.wait_ge(sc_kept, l * NSC + cnt)
                        link(nv.tensor_tensor(KM[1], KM[0], KM[0], ALU.mult))
                        nv.tensor_reduce(SS[:], KM[1].rearrange("p (n v) -> p n v", v=64), AX.X, ALU.add).then_inc(go_ss, 1)
                        v.wait_ge(go_rstd, l * NGRP + (g0 + 1))
                        nv.tensor_tensor(KM[1].rearrange("p (n v) -> p n v", v=64), KM[0].rearrange("p (n v) -> p n v", v=64),
                                         bc(SS[:].rearrange("p (n o) -> p n o", o=1), 64), ALU.mult).then_inc(go_y, 1)
                        v.wait_ge(gy_full, l * NGRP + (g0 + 1))
                        nv.scalar_tensor_tensor(out=ZT[:, gate + grp, :], in0=pair(0)[:, 0:T], scalar=COLS[:, gain:gain + 1],
                                                in1=ZT[:, gate + grp, :], op0=ALU.mult, op1=ALU.mult).then_inc(gy_kept, 1)

                with v.Fori(0, KT) as it:
                    v.wait_ge(stored, l * N_STORE + N_STORE)
                    step.enter(it, 3)
                    for n in range(4):
                        g = G_MIX + 2 * n
                        p = use(g + 1)[0]
                        wait_taken(v, l, g, it * 2)
                        wait_full(v, l, g + 1, it * 8)
                        dst = ZT[:, bass.ds(it + MIXT, 1), :].rearrange("p a t -> p (a t)")
                        if n == 0:
                            nv.tensor_tensor(dst, SQ[0], pair(p)[:, 0:T], ALU.mult).then_inc(gemm_free[p], 1)
                            wait_taken(v, l, g + 1, it * 2)
                        else:
                            nv.tensor_tensor(TMP[n % 2], SQ[n % 2], pair(p)[:, 0:T], ALU.mult).then_inc(gemm_free[p], 1)
                            wait_taken(v, l, g + 1, it * 2)
                            link(nv.tensor_tensor(dst, dst, TMP[n % 2], ALU.add))
                    v.sem_inc(mix_done, 1)
                step.leave(KT)

                def residual(g, k, shift, turns, flag):
                    p = use(g)[0]
                    for s, (a, b) in enumerate(SEG):
                        x = XT[:, bass.ds(k, 1), a:b].rearrange("p a t -> p (a t)")
                        gate = MOD[:, bass.ds(k + shift, 1), s:s + 1].rearrange("p a t -> p (a t)")
                        ins = nv.scalar_tensor_tensor(out=x, in0=pair(p)[:, a:b], scalar=gate, in1=x, op0=ALU.mult, op1=ALU.add)
                        if s == 0:
                            step.mark(ins)
                    ins.then_inc(gemm_free[p], 1)

                for k in range(KT):
                    wait_full(v, l, G_OUT + k)
                    residual(G_OUT + k, k, 16, 0, None)
                wait_taken(v, l, G_OUT + KT - 2)
                wait_taken(v, l, G_OUT + KT - 1)
                v.sem_inc(xo_done, KT)
                normed(1, A2, 24)

                def conv(j, turns):
                    f = turns * 4 + j
                    for h in range(2):
                        g = G_UP + 2 * j + h
                        u = pair(use(g)[0])
                        c = FB[j % 2][h]
                        v.wait_ge(centre_ready, l * 44 + turns * 8 + (2 * j + h + 1))
                        col = f + h * FT
                        for s, (a, b) in enumerate(SEG):
                            step.mark(nv.scalar_tensor_tensor(out=c[:, a + 1:b], in0=u[:, a:b - 1], scalar=COLS[:, bass.ds(col + C_W0, 1)],
                                                              in1=c[:, a + 1:b], op0=ALU.mult, op1=ALU.add))
                        step.settle(v)
                        for s, (a, b) in enumerate(SEG):
                            ins = nv.scalar_tensor_tensor(out=c[:, a:b - 1], in0=u[:, a + 1:b], scalar=COLS[:, bass.ds(col + C_W2, 1)],
                                                          in1=c[:, a:b - 1], op0=ALU.mult, op1=ALU.add)
                            if s == 0:
                                step.mark(ins)
                        ins.then_inc(gemm_free[use(g)[0]], 1)
                    v.wait_ge(g_silu, l * FT + f + 1)
                    nv.tensor_tensor(ZT[:, bass.ds(f, 1), :].rearrange("p a t -> p (a t)"), FB[j % 2][0], FB[j % 2][1], ALU.mult).then_inc(act_done, 1)

                with v.Fori(0, 5) as it:
                    step.enter(it, 24)
                    for j in range(4):
                        conv(j, it)
                step.leave(5)
                for j in range(20, 22):
                    conv(j, 0)
                with v.Fori(0, 2) as it:
                    step.enter(it, 4)
                    for j in range(4):
                        wait_full(v, l, G_DOWN + j, it * 4)
                        residual(G_DOWN + j, it * 4 + j, 40, it, None)
                step.leave(2)
                for n in range(4, 8):
                    wait_taken(v, l, G_DOWN + n)
                v.sem_inc(layer_done, 1)
                step.end(v)


def shape_constants():
    import numpy as np

    def rope(hd):
        half = hd // 2
        freqs = np.float32(10000.0) ** (-np.arange(0, half, 2, dtype=np.float32) / np.float32(half))
        row = np.repeat(np.arange(TS // 64), 64).astype(np.float32)
        col = np.tile(np.arange(64), TS // 64).astype(np.float32)
        r, c = row[:, None] * freqs, col[:, None] * freqs
        ang = np.concatenate([r, r, c, c], axis=-1)
        return [np.tile(f(ang).T, (P // hd, 1)).astype(np.float32) for f in (np.cos, np.sin)]

    def rotation(hd):
        q = hd // 4
        m = np.zeros((P, P), np.float32)
        for d in range(P):
            if d // q % 2 == 0:
                m[d + q, d] = -1.0
            else:
                m[d - q, d] = 1.0
        return m

    s = np.arange(P)
    blocks = [np.eye(P), np.full((P, P), 1.0 / D), (s[:, None] // 64 == s // 64) / 64.0, (s[:, None] // 32 == s // 32) / 32.0,
              rotation(64), rotation(32)]
    const = np.concatenate(rope(64) + rope(32) + blocks, axis=1).astype(np.float32)
    mask = np.zeros((P, NPASS, 64), np.float32)
    c = np.arange(64)
    for m in range(LEVELS):
        h = 1 << m
        same = s[:, None] // (2 * h) == c // h
        late = (s % (2 * h) >= h)[:, None]
        mask[:, m] = same & ~late
        mask[:, LEVELS + m] = same & late
    for odd in range(2):
        mask[:, 2 * LEVELS + odd] = s[:, None] == 2 * c + odd
    return const, mask.reshape(P, -1)


def kernel(**inputs):
    import math

    import concourse.bacc as _bacc
    import numpy as np
    from concourse.bass_utils import run_bass_kernel_spmd as _run

    a = {k: np.asarray(v) for k, v in inputs.items()}

    def columns(x):
        return x.reshape(x.shape[0], -1, P).transpose(0, 2, 1)

    def twice(x):
        return np.tile(x, (1, P // x.shape[1]))[:, :, None]

    def each(x):
        return np.broadcast_to(x, (DEPTH,) + x.shape)

    lb = a["b_lb_logits"].reshape(2, DEPTH, 2, P).transpose(3, 0, 1, 2).reshape(P, 8)
    cond = np.stack([a["c"][0].reshape(KT, P), a["c_ctx"].reshape(KT, P)]).transpose(2, 0, 1).reshape(P, 16)
    lam_init = [0.8 - 0.6 * math.exp(-0.3 * l) for l in range(DEPTH)]
    layer_const = np.array([[[x, 1.0 - x, float(l > 0)]] * P for l, x in enumerate(lam_init)], np.float32)
    cols = np.concatenate([
        columns(a["b_ada"]), columns(a["norm1_g"]), columns(a["norm2_g"]), columns(a["conv_b"]),
        twice(a["a_qn_g"]), twice(a["a_kn_g"]), twice(a["c_qn_g"]), twice(a["c_kn_g"]), twice(a["c_subln_g"]),
        twice(a["b_norm_g"]), twice(a["d_norm_g"]), a["d_alpha_b"].transpose(0, 2, 1),
        columns(a["conv_w"][:, 0]), columns(a["conv_w"][:, 1]), columns(a["conv_w"][:, 2]), each(lb), each(cond), layer_const,
        np.broadcast_to(a["c_lambda"].reshape(DEPTH, 1, P), (DEPTH, P, P)),
    ], axis=2)
    assert cols.shape == (DEPTH, P, NCOL)
    w_alpha = np.zeros((DEPTH, 32, 2, P), np.float32)
    for d in range(2):
        w_alpha[:, 16 * d:16 * d + 16, d] = a["d_alpha_w"][:, d]
    keys_a = a["cache_a_k"][0].reshape(DEPTH, PAST, 1, P)
    keys_c = a["cache_c_k"][0].reshape(DEPTH, PAST, 2, P)
    const, mask = shape_constants()
    arrays = {
        "xT": np.concatenate([a["x_sample"][0], a["x_prompt"][0]]).reshape(T, KT, P).transpose(2, 1, 0),
        "cols": cols, "w_alpha": w_alpha, "const": const, "mask": mask,
        "keysT": np.concatenate([keys_a, keys_c], axis=2).transpose(0, 3, 2, 1),
        "vals": np.concatenate([a["cache_a_v"][0].reshape(DEPTH, PAST, P), a["cache_c_v"][0].reshape(DEPTH, PAST, 256)], axis=2),
        "hgrn": a["state_hgrn"][0].reshape(DEPTH, 2, 2, P, 64).transpose(0, 3, 1, 2, 4),
        "gla": a["state_gla"][0].reshape(DEPTH, 2, P, 64).transpose(0, 2, 1, 3),
        "w_ada": a["w_ada"], "w_in": a["w_in"], "w_branch": a["w_branch"], "w_out": a["w_out"], "w_up": a["w_up"], "w_down": a["w_down"],
    }
    arrays = {k: np.ascontiguousarray(x) for k, x in arrays.items()}
    outs = {"yT": (P, KT, T), "keysT": (DEPTH, P, 3, P), "vals": (DEPTH, P, V_B), "fin": (DEPTH, P, 2 * 3 * 64)}
    nc = _bacc.Bacc("TRN2", target_bir_lowering=False, num_devices=1)
    A = {k: nc.dram_tensor(f"in_{k}", x.shape, mybir.dt.from_np(x.dtype), kind="ExternalInput").ap() for k, x in arrays.items()}
    O = {k: nc.dram_tensor(f"out_{k}", s, F32, kind="ExternalOutput").ap() for k, s in outs.items()}
    build(nc, A, O)
    r = _run(nc, [{f"in_{k}": x for k, x in arrays.items()}], core_ids=[0]).results[0]
    y = r["out_yT"].transpose(2, 1, 0).reshape(T, D)
    keys_ = r["out_keysT"].transpose(0, 3, 2, 1)
    vals = r["out_vals"]
    fin = r["out_fin"].reshape(DEPTH, P, 2, 3, 64)
    hgrn = fin[:, :, :, 0:2].transpose(0, 2, 3, 1, 4).reshape(1, DEPTH, 2, 4, 64, 64)
    gla = fin[:, :, :, 2].transpose(0, 2, 1, 3).reshape(1, DEPTH, 2, 4, 32, 64)
    outputs = (y[TS:][None], y[:TS][None], keys_[:, :, 0].reshape(1, DEPTH, TC, 2, 64), vals[:, :, 0:P].reshape(1, DEPTH, TC, 2, 64),
               keys_[:, :, 1:3].reshape(1, DEPTH, TC, 4, 2, 32), vals[:, :, P:].reshape(1, DEPTH, TC, 4, 64), hgrn, gla)
    return tuple(np.ascontiguousarray(x) for x in outputs)
```

```python
from contextlib import ExitStack

import concourse.bass as bass
from concourse import mybir

F32 = mybir.dt.float32
U8 = mybir.dt.uint8
ALU = mybir.AluOpType
ACT = mybir.ActivationFunctionType
AX = mybir.AxisListType

P = 128
D = 1024
KT = D // P
DEPTH = 2
TS, TC = 512, 128
T = TS + TC
NT = T // P
PAST = 256
FF = 2816
FT = FF // P
EPS = 1e-6
LB_FLOOR = 1e-30
SEG = ((0, TS), (TS, T))
Z_COLS = 3360

AQ, BG, CQ, DG, AK, CK, BQ, BFF, BFB, BKF, BKB, DQ, DK, DR, DAB, NZ = 0, 2, 4, 6, 8, 9, 11, 13, 15, 17, 19, 21, 22, 23, 24, 25
DAF = DR
MIXT = 8
V_A, V_C, V_B, V_D, NV = 0, 128, 384, 640, 896

(C_BADA, C_N1, C_N2, C_CB, C_AQ, C_AK, C_CQ, C_CK, C_SUB, C_BN, C_DN, C_AB, C_W0, C_W1, C_W2, C_LB, C_COND, C_LC, C_LAM, NCOL) = (
    0, 48, 56, 64, 108, 109, 110, 111, 112, 113, 114, 115, 117, 161, 205, 249, 257, 273, 276, 404)

N_SLOT = 4
C_MIX, C_OUT, C_UP, C_DOWN, CHUNKS = 38, 70, 74, 96, 112
SLOT_W = 2048
N_ADA1, N_ADA = 8, 24
CHUNK_Z = [N_ADA1 + 2 * c for c in range(14)]
CHUNK_ADA = list(range(N_ADA1)) + [N_ADA1 + 1 + 2 * c for c in range(14)] + [36, 37]

Z_PLAN = [(0, "q", AQ), (1, "kv", AK), (2, "fm", CQ), (3, "fm", CK), (13, "r", DR), (4, "tm", V_C), (5, "silu", BQ),
          (6, "tm", V_B), (7, "ff", BFF), (8, "ff", BFB), (9, "silu", BG), (10, "dqk", DQ), (11, "tm", V_D), (12, "silu", DG)]
QK_AT = 4


def z_tiles():
    out = []
    for c, (_, kind, dst) in enumerate(Z_PLAN):
        if kind == "kv":
            out += [(c, "fm", AK, 0), (c, "tm1", V_A, 1)]
        elif kind == "tm":
            out += [(c, "tm", dst, 0), (c, "tm", dst, 1)]
        elif kind == "r":
            out += [(c, "r", dst, 0)]
        else:
            out += [(c, kind, dst + j, j) for j in range(2)]
    return out


ZT_TILES = z_tiles()
NZT = len(ZT_TILES)
USES_Z = [(NZT + 1) // 2, NZT // 2, 0, 0]
USES_MIX, USES_OUT, USES_UP, USES_DOWN = 16, 2, 11, 2
USES = [u + USES_MIX + USES_OUT + USES_UP + USES_DOWN for u in USES_Z]
N_GEMM = NZT + 64 + 8 + 44 + 8
G_MIX, G_OUT, G_UP, G_DOWN = NZT, NZT + 64, NZT + 72, NZT + 116

STEPS = 4096
QK_TILES = [(AQ, C_AQ, 64), (AQ + 1, C_AQ, 64), (AK, C_AK, 64), (CQ, C_CQ, 32), (CQ + 1, C_CQ, 32),
            (CK, C_CK, 32), (CK + 1, C_CK, 32)]
NQK = len(QK_TILES)
ATT = [(AQ + j, 64 * g, 64, AK, 0, V_A + 64 * g, g, 64 * j, None) for j in range(2) for g in range(2)] + \
      [(CQ + h // 2, 64 * (h % 2) + 32 * m, 32, CK + h // 2, 1 + h // 2, V_C + 64 * h, 2 + h // 2, 64 * (h % 2), m)
       for h in range(4) for m in range(2)]
NU = len(ATT)
GLA = [(BQ, (BKF, BKB), (BFF, BFB), BG, V_B, 64, 1, C_BN), (BQ + 1, (BKF + 1, BKB + 1), (BFF + 1, BFB + 1), BG + 1, V_B + 128, 64, 1, C_BN),
       (DQ, (DK, DK), (DAF, DAB), DG, V_D, 32, 2, C_DN)]
LEVELS = 7
NG = NT * NU
NPASS = LEVELS + 1
NGRP = sum(g[6] for g in GLA)
NSC = NGRP * (2 * NPASS + 1)




def keys(i):
    return 1 if i == NT - 1 else (TS + PAST) // P


class Chain:

    def __init__(self, sem):
        self.sem, self.n, self.base = sem, 0, 0

    def layer(self, l):
        self.l, self.n, self.base = l, 0, l * STEPS

    def mark(self, ins):
        self.n += 1
        ins.then_inc(self.sem, 1)

    def settle(self, eng):
        eng.wait_ge(self.sem, self.base + self.n)

    def enter(self, it, per):
        self.n0, self.per, self.base = self.n, per, self.l * STEPS + it * per

    def leave(self, count):
        assert self.n - self.n0 == self.per, (self.n - self.n0, self.per)
        self.n, self.base = self.n0 + count * self.per, self.l * STEPS

    def end(self, eng):
        assert self.n <= STEPS, self.n
        if self.n < STEPS:
            eng.sem_inc(self.sem, STEPS - self.n)


def build(nc, A, O):
    ctx = ExitStack()
    with ctx:
        def sb(name, shape, dt=F32):
            return ctx.enter_context(nc.sbuf_tensor(name, shape, dt))

        def sem(name):
            return ctx.enter_context(nc.semaphore(name))

        XT = sb("XT", [P, KT, T])
        HT = sb("HT", [P, KT, T])
        RING = sb("RING", [P, N_SLOT, SLOT_W])
        ZT = sb("ZT", [P, NZ, T])
        V = sb("V", [P, NT, NV])
        WORK = sb("WORK", [P, 5120])
        KO = sb("KO", [P, 2, T])
        KOT = WORK[:, 2560:3840].rearrange("p (d i n) -> p d i n", d=2, i=NT)
        CONST = sb("CONST", [P, 4 * TS + 6 * P])
        MASK = sb("MASK", [P, NPASS, P], U8)
        KTC = sb("KTC", [P, 3, PAST])
        VC = sb("VC", [P, 2, V_B])
        ST = sb("ST", [P, 2, 3, NT, 64])
        FIN = sb("FIN", [P, 2, 3, 64])
        COLS = sb("COLS", [P, NCOL])
        MOD = sb("MOD", [P, 48, 2])
        A1 = sb("A1", [P, KT, 2])
        A2 = sb("A2", [P, KT, 2])
        SC = sb("SC", [P, KT, 2])
        SG = sb("SG", [P, 2, KT])
        LBE = sb("LBE", [P, 2, 2, 2])
        LBM = sb("LBM", [P, 2, 2])
        LBF = sb("LBF", [P, 2, 2])
        OML = sb("OML", [P, 2, 2])
        LMS = sb("LMS", [P, 2])
        NLAM = sb("NLAM", [P, 1])
        WAL = sb("WAL", [32, 2, P])
        SUBG = sb("SUBG", [P, 1])
        EPSC = sb("EPSC", [P, 1])
        NMX = sb("NMX", [P, 2])
        SUMS = sb("SUMS", [P, 2])
        RCP = sb("RCP", [P, 2])
        QG = sb("QG", [P, 2])
        DEC = sb("DEC", [P, 2, NT])
        PS = ctx.enter_context(nc.psum_tensor("PS", [P, 4, 1024], F32))

        cosA, sinA, cosC, sinC = (CONST[:, i * TS:(i + 1) * TS] for i in range(4))
        IDENT, ONES, BLK64, BLK32, ROTA, ROTC = (CONST[:, 4 * TS + i * P:4 * TS + (i + 1) * P] for i in range(6))
        LPR = WORK[:, 4096:4160].rearrange("p (a n) -> p a n", a=2)
        SQ = [WORK[:, 0:T], WORK[:, T:2 * T]]
        RSTD = [WORK[:, 2 * T:3 * T], WORK[:, 3 * T:4 * T]]
        TMP = [WORK[:, 4 * T:5 * T], WORK[:, 5 * T:6 * T]]
        FB = [[WORK[:, (2 * b + h) * T:(2 * b + h + 1) * T] for h in range(2)] for b in range(2)]
        ROW = [WORK[0:2, 4608 + 256 * b:4864 + 256 * b] for b in range(2)]
        PROB = [WORK[:, 0:768], WORK[:, 768:1536]]
        PROBT = [WORK[:, 1536:2304], WORK[:, 2304:3072]]
        CSQ, CRSTD = WORK[:, 2560:3200], WORK[:, 3200:3840]
        SCORE = WORK[:, 0:2560].rearrange("p (h n t) -> p h n t", h=4, n=NT)
        KM = [WORK[:, 3840:4480], WORK[:, 4480:5120]]
        QM = [RING[:, b, 1280:1280 + T] for b in range(2)]
        SX = RING[:, 2:4, 1280:1280 + T]

        landed = [sem(f"landed{i}") for i in range(N_SLOT)]
        landed_q = sem("landed_q")
        slot_freed = sem("slot_freed")
        x_in, consts_in, params_in, stored, states_stored, y_stored = sem("x_in"), sem("consts_in"), sem("params_in"), sem("stored"), sem("states_stored"), sem("y_stored")
        eps_set, zero_set, mask_set = sem("eps_set"), sem("zero_set"), sem("mask_set")
        cond_sig, cond_ready = sem("cond_sig"), sem("cond_ready")
        lb_shift, lb_exp, lam_sum, lam_exp, small_ready = (sem(n) for n in ("lb_shift", "lb_exp", "lam_sum", "lam_exp", "small_ready"))
        ada_row, row_kept, ada_done, mod_ready = sem("ada_row"), sem("row_kept"), sem("ada_done"), sem("mod_ready")
        sq_ready, ms_ready, rstd_ready, h_ready = sem("sq_ready"), sem("ms_ready"), sem("rstd_ready"), sem("h_ready")
        gemm_full = sem("gemm_full")
        gemm_free = [sem(f"gemm_free{i}") for i in range(4)]
        silu_sig, gla_in = sem("silu_sig"), sem("gla_in")
        qk_sq, qk_ms, qk_rstd, qk_normed, qk_rot, qk_done = (sem(f"qk_{n}") for n in ("sq", "ms", "rstd", "normed", "rot", "done"))
        al_full, al_lin, al_log, al_cut, al_ready = (sem(f"al_{n}") for n in ("full", "lin", "log", "cut", "ready"))
        s_full, nmax_ready, p_ready, normed_p, pt_full, pt_kept, pv_done, o_taken = (
            sem(n) for n in ("s_full", "nmax_ready", "p_ready", "normed_p", "pt_full", "pt_kept", "pv_done", "o_taken"))
        csq_ready, cms_ready, crstd_ready, yc_done = (sem(n) for n in ("csq_ready", "cms_ready", "crstd_ready", "yc_done"))
        lvl_ready, sc_full, sc_kept, scores_seen = sem("lvl_ready"), sem("sc_full"), sem("sc_kept"), sem("scores_seen")
        ko_ready, ko_turned, ko_kept, ds_full, st_ready = (sem(n) for n in ("ko_ready", "ko_turned", "ko_kept", "ds_full", "st_ready"))
        go_sq, go_ms, go_rstd, gy_kept = (sem(n) for n in ("go_sq", "go_ms", "go_rstd", "gy_kept"))
        mix_done = sem("mix_done")
        centre_ready, g_silu, act_done = sem("centre_ready"), sem("g_silu"), sem("act_done")
        layer_done = sem("layer_done")
        dve, act_ = Chain(sem("dve_step")), Chain(sem("act_step"))
        N_PARAM = 16 * 8
        N_STORE = 16 * 2

        def pair(i):
            return PS[:, i, :]

        def ada_out(s):
            return pair(s % 2)[0:2, 0:256] if s < N_ADA1 else pair(3)[0:2, 768:1024]

        def use(n):
            if n < G_MIX:
                return n % 2, n // 2
            return (n - G_MIX) % 4, USES_Z[(n - G_MIX) % 4] + (n - G_MIX) // 4

        def wait_taken(eng, l, n, turns=0):
            p, k = use(n)
            eng.wait_ge(gemm_free[p], l * USES[p] + turns + (k + 1))

        def wait_room(eng, l, n, turns=0):
            p, k = use(n)
            eng.wait_ge(gemm_free[p], l * USES[p] + turns + k)

        def wait_full(eng, l, n, tiles=0):
            eng.wait_ge(gemm_full, l * N_GEMM + tiles + (n + 1))

        def z_index(tile):
            return next(n for n, t in enumerate(ZT_TILES) if t[1] not in ("tm", "tm1") and t[2] == tile)

        Z_OF = [z_index(t) for t in range(NZ) if t not in (BKF, BKF + 1, BKB, BKB + 1, DAB)]
        block = ctx.enter_context(nc.Block())

        @block.sync
        def _(sp):
            w_ada = A["w_ada"].rearrange("l (k p) n -> p l k n", p=P)
            w_in = A["w_in"].rearrange("l (k p) n -> p l k n", p=P)
            w_br = A["w_branch"].rearrange("l b (k p) n -> p l b k n", p=P)
            w_out = A["w_out"].rearrange("l (k p) n -> p l k n", p=P)
            w_up = A["w_up"].rearrange("l (k p) n -> p l k n", p=P)
            w_dn = A["w_down"].rearrange("l (k p) n -> p l k n", p=P)

            sp.sem_inc(slot_freed, N_SLOT - 1)
            sp.dma_start(XT[:], A["xT"]).then_inc(x_in, 16)
            with sp.Fori(0, DEPTH) as l:
                def slot_free(i, chunks=0):
                    sp.wait_ge(slot_freed, l * CHUNKS + chunks + (i + 1))

                def part(dst, w, s, k0, k1, col, width):
                    src = w[:, bass.ds(l, 1), k0:k1, bass.ds(col, width)].rearrange("p l k n -> p (l k) n")
                    sp.dma_start(dst, src).then_inc(landed[s], 16)

                def columns(w, s, col, width):
                    dst = RING[:, s, 0:8 * width].rearrange("p (k n) -> p k n", n=width)
                    part(dst[:, 0:4, :], w, s, 0, 4, col, width)
                    part(dst[:, 4:8, :], w, s, 4, 8, col, width)

                def up_chunk(j, s, col):
                    for h in range(2):
                        dst = RING[:, s, 1024 * h:1024 * h + 1024].rearrange("p (k n) -> p k n", n=P)
                        part(dst, w_up, s, 0, 8, col + (h * FF + j * P), P)

                def ada_chunk(s):
                    i = CHUNK_ADA[s]
                    slot_free(i)
                    columns(w_ada, i % N_SLOT, 256 * s, 256)

                def z_chunk(c):
                    i = CHUNK_Z[c]
                    slot_free(i)
                    if c:
                        columns(w_in, i % N_SLOT, 256 * Z_PLAN[c][0], 32 if Z_PLAN[c][1] == "r" else 256)
                        return
                    dst = RING[:, i % N_SLOT, :].rearrange("p (k j g d) -> p k j g d", j=2, g=2, d=64)
                    src = w_in[:, bass.ds(l, 1), :, 0:256].rearrange("p l k (g j d) -> p (l k) j g d", g=2, j=2)
                    for j in range(2):
                        for g in range(2):
                            sp.dma_start(dst[:, :, j, g], src[:, :, j, g]).then_inc(landed_q if j else landed[i % N_SLOT], 16)

                for s in range(N_ADA1):
                    ada_chunk(s)
                for c in range(14):
                    z_chunk(c)
                    ada_chunk(N_ADA1 + c)
                for s in range(N_ADA1 + 14, N_ADA):
                    ada_chunk(s)
                with sp.Fori(0, KT) as it:
                    for n in range(4):
                        s = (C_MIX + n) % 4
                        slot_free(C_MIX + n, it * 4)
                        part(RING[:, s, 0:1024].rearrange("p (k n) -> p k n", n=P), w_in, s, 0, 8, it * P + (Z_COLS + n * D), P)
                        src = w_br[:, bass.ds(l, 1), n, :, bass.ds(it * P, P)].rearrange("p l k n -> p (l k) n")
                        sp.dma_start(RING[:, s, 1024:1280].rearrange("p (k n) -> p k n", n=P), src).then_inc(landed[s], 16)
                for c in range(4):
                    slot_free(C_OUT + c)
                    columns(w_out, (C_OUT + c) % 4, 256 * c, 256)
                with sp.Fori(0, 5) as it:
                    for j in range(4):
                        slot_free(C_UP + j, it * 4)
                        up_chunk(j, (C_UP + j) % 4, it * 4 * P)
                for j in range(20, 22):
                    slot_free(C_UP + j)
                    up_chunk(j, (C_UP + j) % 4, 0)
                with sp.Fori(0, 2) as it:
                    for j in range(8):
                        s = (C_DOWN + j) % 4
                        slot_free(C_DOWN + j, it * 8)
                        k0 = 11 * (j % 2)
                        dst = RING[:, s, 0:11 * P].rearrange("p (k n) -> p k n", n=P)
                        part(dst[:, 0:6, :], w_dn, s, k0, k0 + 6, it * 4 * P + (j // 2) * P, P)
                        part(dst[:, 6:11, :], w_dn, s, k0 + 6, k0 + 11, it * 4 * P + (j // 2) * P, P)
            sp.wait_ge(layer_done, DEPTH)
            sp.dma_start(O["yT"], XT[:]).then_inc(y_stored, 16)
            sp.wait_ge(y_stored, 16)

        @block.gpsimd
        def _(pool):
            pool.dma_start(CONST[:], A["const"]).then_inc(consts_in, 16)
            pool.memset(ST[:], 0.0).then_inc(zero_set, 1)
            pool.dma_start(WORK[:, 0:NPASS * P], A["mask"]).then_inc(consts_in, 16)

        @block.tensor
        def _(pe):
            pe.wait_ge(consts_in, 32)
            with pe.Fori(0, DEPTH) as l:
                def chunk(i, turns=0):
                    pe.wait_ge(landed[i % N_SLOT], l * (32 * CHUNKS // N_SLOT) + turns * 32 + 32 * (i // N_SLOT + 1))

                def release(ins, first):
                    if first:
                        ins.then_inc(slot_freed, 1)

                def wide(out, lhsT, rhs, start, stop, first=False):
                    release(pe.matmul(out[:, 0:TS], lhsT, rhs[:, 0:TS], start=start, stop=stop), first)
                    return pe.matmul(out[:, TS:T], lhsT, rhs[:, TS:T], start=start, stop=stop)

                def weights(i, width):
                    return RING[:, i % N_SLOT, 0:8 * width].rearrange("p (k n) -> p k n", n=width)

                def ada(s):
                    chunk(CHUNK_ADA[s])
                    w = weights(CHUNK_ADA[s], 256)
                    for k in range(KT):
                        last = pe.matmul(ada_out(s), SC[:, k, :], w[:, k, :], start=k == 0, stop=k == KT - 1)
                        release(last, k == 0)
                    last.then_inc(ada_row, 1)

                def ada_turn(s):
                    pe.wait_ge(row_kept, l * N_ADA + (s + 1))
                    for h in range(2):
                        last = pe.matmul(pair(3)[:, TS + 4 * s + 2 * h:TS + 4 * s + 2 * h + 2], ROW[s % 2][:, h * P:(h + 1) * P], IDENT[0:2, 0:2], start=True, stop=True)
                    last.then_inc(ada_done, 1)

                def mean_square(which):
                    if which:
                        wait_taken(pe, l, G_OUT + 6)
                    for k in range(KT):
                        pe.wait_ge(sq_ready, l * 16 + (8 * which + k + 1))
                        wide(pair(2), ONES, SQ[k % 2], k == 0, k == KT - 1).then_inc(ms_ready, 1)

                mean_square(0)
                pe.wait_ge(cond_ready, l + 1)
                for s in range(N_ADA1):
                    ada(s)
                    if s:
                        ada_turn(s - 1)
                ada_turn(N_ADA1 - 1)
                def head_mean_square(i):
                    pe.wait_ge(qk_sq, l * NQK + (i + 1))
                    if i:
                        pe.wait_ge(qk_rstd, l * NQK + i)
                    wide(pair(2), BLK64 if QK_TILES[i][2] == 64 else BLK32, SQ[i % 2], True, True).then_inc(qk_ms, 1)

                def rotate(i):
                    t, _, hd = QK_TILES[i]
                    pe.wait_ge(qk_normed, l * NQK + (i + 1))
                    if i:
                        pe.wait_ge(qk_done, l * NQK + i)
                    pe.matmul(pair(3)[:, 0:TS], ROTA if hd == 64 else ROTC, ZT[:, t, 0:TS], start=True, stop=True).then_inc(qk_rot, 1)

                def decay(d):
                    if d:
                        pe.wait_ge(al_lin, l * 2 + 1)
                    else:
                        pe.wait_ge(qk_rstd, l * NQK + NQK)
                        wait_taken(pe, l, z_index(DR))
                    wide(pair(2), WAL[:, d, :], ZT[0:32, DR, :], True, True).then_inc(al_full, 1)

                for n, (c, kind, dst, j) in enumerate(ZT_TILES):
                    chunk(CHUNK_Z[c])
                    fresh = n == 0 or ZT_TILES[n - 1][0] != c
                    if n == 1:
                        pe.wait_ge(landed_q, l * 32 + 32)
                    wait_room(pe, l, n)
                    out = pair(use(n)[0])
                    if kind == "tm":
                        w = weights(CHUNK_Z[c], 256)
                        for i in range(3 * j, 3 if j == 0 else NT):
                            for k in range(KT):
                                last = pe.matmul(out[:, (i - 3 * j) * 256:(i - 3 * j + 1) * 256], HT[:, k, i * P:(i + 1) * P],
                                                 w[:, k, :], start=k == 0, stop=k == KT - 1)
                                release(last, fresh and i == 0 and k == 0)
                    elif kind == "tm1":
                        w = weights(CHUNK_Z[c], 256)
                        for i in range(NT):
                            for k in range(KT):
                                last = pe.matmul(out[:, i * P:(i + 1) * P], HT[:, k, i * P:(i + 1) * P],
                                                 w[:, k, P:2 * P], start=k == 0, stop=k == KT - 1)
                    elif kind == "r":
                        w = weights(CHUNK_Z[c], 32)
                        for k in range(KT):
                            last = wide(out[0:32], w[:, k, :], HT[:, k, :], k == 0, k == KT - 1, k == 0)
                    else:
                        w = weights(CHUNK_Z[c], 256)
                        for k in range(KT):
                            if n == 0:
                                pe.wait_ge(h_ready, l * 16 + (k + 1))
                            last = wide(out, w[:, k, j * P:(j + 1) * P], HT[:, k, :], k == 0, k == KT - 1, fresh and k == 0)
                    last.then_inc(gemm_full, 1)
                    if n < NZT - 1 and ZT_TILES[n + 1][0] == c:
                        continue
                    if 0 <= c - QK_AT - 1 < NQK:
                        head_mean_square(c - QK_AT - 1)
                    if 0 <= c - QK_AT - 2 < NQK:
                        rotate(c - QK_AT - 2)
                    if c == 12:
                        decay(0)
                    if c:
                        ada_turn(N_ADA1 + c - 1)
                    ada(N_ADA1 + c)
                for s in range(N_ADA1 + 14, N_ADA + 1):
                    ada_turn(s - 1)
                    if s < N_ADA:
                        ada(s)
                decay(1)
                pe.wait_ge(al_lin, l * 2 + 2)
                pe.wait_ge(mod_ready, l * 2 + 2)
                pe.wait_ge(qk_done, l * NQK + NQK)
                wait_taken(pe, l, NZT - 1)
                wait_taken(pe, l, NZT - 2)

                def scores(g):
                    i, u = divmod(g, NU)
                    q, r0, rows, k, kc = ATT[u][:5]
                    if g >= 2:
                        pe.wait_ge(p_ready, l * NG + (g - 1))
                    out = pair(1 + g % 2)
                    qs = ZT[r0:r0 + rows, q, i * P:(i + 1) * P]
                    if i < NT - 1:
                        pe.matmul(out[:, 0:TS], qs, ZT[r0:r0 + rows, k, 0:TS], start=True, stop=True)
                        last = pe.matmul(out[:, TS:TS + PAST], qs, KTC[r0:r0 + rows, kc, :], start=True, stop=True)
                    else:
                        last = pe.matmul(out[:, 0:P], qs, ZT[r0:r0 + rows, k, TS:T], start=True, stop=True)
                    last.then_inc(s_full, 1)

                def turn(g):
                    i, u = divmod(g, NU)
                    pe.wait_ge(normed_p, l * NG + (g + 1))
                    if g:
                        pe.wait_ge(pt_kept, l * NG + g)
                    for k in range(keys(i)):
                        last = pe.transpose(pair(3)[:, k * P:(k + 1) * P], PROB[g % 2][:, k * P:(k + 1) * P], IDENT)
                    last.then_inc(pt_full, 1)

                def weigh(g):
                    i, u = divmod(g, NU)
                    v, tile, o0, m = ATT[u][5:]
                    pe.wait_ge(pt_kept, l * NG + (g + 1))
                    if u == 0 and i >= 2:
                        pe.wait_ge(o_taken, l * NT + (i - 1))
                    out = pair(0)[o0:o0 + 64, i % 2 * TS + tile * P:i % 2 * TS + (tile + 1) * P]
                    for k in range(keys(i)):
                        vals = V[:, NT - 1, v:v + 64] if i == NT - 1 else V[:, k, v:v + 64] if k < 4 else VC[:, k - 4, v:v + 64]
                        last = pe.matmul(out, vals, PROBT[g % 2][:, k * P:(k + 1) * P], start=k == 0 and m != 1, stop=k == keys(i) - 1 and m != 0)
                    last.then_inc(pv_done, 1)

                scores(0)
                scores(1)
                for g in range(NG + 1):
                    if g + 2 < NG:
                        scores(g + 2)
                    if g < NG:
                        turn(g)
                    if g:
                        weigh(g - 1)

                def mean_square_c(j):
                    pe.wait_ge(csq_ready, l * 2 + (j + 1))
                    if j:
                        pe.wait_ge(crstd_ready, l * 2 + j)
                    wide(pair(0), BLK64, CSQ, True, True).then_inc(cms_ready, 1)

                pe.wait_ge(al_ready, l * 2 + 2)
                cnt = 0

                def group_room(cnt):
                    if cnt >= 2:
                        pe.wait_ge(sc_kept, l * NSC + (cnt - 1))
                    return pair(2 + cnt % 2)

                for x, (q, _, a, gate, vb, rows, groups, _) in enumerate(GLA):
                    before = sum(g[6] for g in GLA[:x])
                    for p in range(NPASS):
                        pe.wait_ge(lvl_ready, l * 3 * NPASS + (x * NPASS + p + 1))
                        for h in range(2 * groups):
                            out = group_room(cnt)
                            cnt += 1
                            r = slice(h * rows, (h + 1) * rows)
                            for i in range(NT):
                                ti = slice(i * P, (i + 1) * P)
                                if p == 0:
                                    last = pe.matmul(out[:, ti], KO[r, 0, ti], ZT[r, q, ti], start=True, stop=True)
                                else:
                                    last = pe.matmul(out[:, ti], KM[p % 2][r, ti], QM[p % 2][r, ti], start=True, stop=True)
                            last.then_inc(sc_full, 1)
                        if x == 0 and p in (1, 3):
                            mean_square_c(p // 2)
                    for d in range(2):
                        pe.wait_ge(ko_ready, l * 6 + (2 * x + d + 1))
                        if d == 0 and x == 0:
                            pe.wait_ge(crstd_ready, l * 2 + 2)
                        elif d == 0:
                            pe.wait_ge(go_rstd, l * NGRP + before)
                        else:
                            pe.wait_ge(ko_kept, l * 6 + (2 * x + 1))
                        for i in range(NT):
                            last = pe.transpose(pair(0)[:, i * P:(i + 1) * P], KO[:, d, i * P:(i + 1) * P], IDENT)
                        last.then_inc(ko_turned, 1)
                    for d in range(2):
                        pe.wait_ge(ko_kept, l * 6 + (2 * x + d + 1))
                        if x:
                            pe.wait_ge(st_ready, l * 6 + 2 * x)
                        for i in range(NT):
                            for h in range(P // rows):
                                last = pe.matmul(pair(1)[h * rows:(h + 1) * rows, d * TS + i * 64:d * TS + (i + 1) * 64],
                                                 KOT[:, d, i, h * rows:(h + 1) * rows], V[:, i, vb + 64 * h:vb + 64 * h + 64],
                                                 start=True, stop=True)
                        last.then_inc(ds_full, 1)
                    pe.wait_ge(st_ready, l * 6 + (2 * x + 2))
                    pe.wait_ge(sc_kept, l * NSC + cnt)
                    for grp in range(groups):
                        out = group_room(cnt)
                        cnt += 1
                        for hh in range(2):
                            h = 2 * grp + hh
                            r = slice(h * rows, (h + 1) * rows)
                            for i in range(NT):
                                ti = slice(i * P, (i + 1) * P)
                                o = out[64 * hh:64 * hh + 64, ti]
                                pe.matmul(o, V[:, i, vb + 64 * h:vb + 64 * h + 64], SCORE[:, h, i, :], start=True, stop=False)
                                for d in range(2):
                                    last = pe.matmul(o, ST[r, d, x, i, :], ZT[r, a[d], ti], start=False, stop=d == 1)
                        last.then_inc(sc_full, 1)
                    for grp in range(groups):
                        g0 = before + grp
                        pe.wait_ge(go_sq, l * NGRP + (g0 + 1))
                        if grp:
                            pe.wait_ge(go_rstd, l * NGRP + g0)
                        wide(pair(0), BLK64, KM[0], True, True).then_inc(go_ms, 1)

                with pe.Fori(0, KT) as it:
                    pe.wait_ge(gy_kept, l * NGRP + NGRP)
                    for n in range(4):
                        chunk(C_MIX + n, it)
                        w = RING[:, (C_MIX + n) % 4, 0:1280].rearrange("p (k n) -> p k n", n=P)
                        g = G_MIX + 2 * n
                        wait_room(pe, l, g, it * 2)
                        for k in range(KT):
                            last = wide(pair(use(g)[0]), w[:, k, :], HT[:, k, :], k == 0, k == KT - 1, k == 0)
                        last.then_inc(gemm_full, 1)
                        wait_room(pe, l, g + 1, it * 2)
                        for k in range(2):
                            last = wide(pair(use(g + 1)[0]), w[:, KT + k, :], ZT[:, 2 * n + k, :], k == 0, k == 1)
                        last.then_inc(gemm_full, 1)
                pe.wait_ge(mix_done, l * KT + KT)
                for c in range(4):
                    chunk(C_OUT + c)
                    w = weights(C_OUT + c, 256)
                    for h in range(2):
                        g = G_OUT + 2 * c + h
                        wait_room(pe, l, g)
                        for k in range(KT):
                            last = wide(pair(use(g)[0]), w[:, k, h * P:(h + 1) * P], ZT[:, MIXT + k, :], k == 0, k == KT - 1, h == 0 and k == 0)
                        last.then_inc(gemm_full, 1)
                mean_square(1)

                def up(j, turns):
                    chunk(C_UP + j, turns)
                    for h in range(2):
                        w = RING[:, (C_UP + j) % 4, 1024 * h:1024 * h + 1024].rearrange("p (k n) -> p k n", n=P)
                        g = G_UP + 2 * j + h
                        wait_room(pe, l, g, turns * 2)
                        for k in range(KT):
                            if j == 0 and h == 0:
                                pe.wait_ge(h_ready, l * 16 + (8 + k + 1))
                            last = wide(pair(use(g)[0]), w[:, k, :], HT[:, k, :], k == 0, k == KT - 1, h == 0 and k == 0)
                        last.then_inc(gemm_full, 1)

                with pe.Fori(0, 5) as it:
                    for j in range(4):
                        up(j, it)
                for j in range(20, 22):
                    up(j, 0)
                with pe.Fori(0, 2) as it:
                    pe.wait_ge(act_done, l * FT + (FT + 2))
                    for j in range(4):
                        g = G_DOWN + j
                        wait_room(pe, l, g, it)
                        for h in range(2):
                            i = C_DOWN + 2 * j + h
                            chunk(i, it * 2)
                            w = RING[:, i % 4, 0:11 * P].rearrange("p (k n) -> p k n", n=P)
                            for k in range(11):
                                last = wide(pair(use(g)[0]), w[:, k, :], ZT[:, 11 * h + k, :], h == 0 and k == 0, h == 1 and k == 10, k == 0)
                        last.then_inc(gemm_full, 1)

        @block.scalar
        def _(act):
            step = act_
            act.wait_ge(x_in, 16)
            act.wait_ge(eps_set, 1)
            act.wait_ge(zero_set, 1)
            act.wait_ge(mask_set, 1)
            with act.Fori(0, DEPTH) as l:
                step.layer(l)
                at = bass.ds(l, 1)
                act.wait_ge(layer_done, l)
                act.wait_ge(states_stored, l * 16)
                act.dma_start(COLS[:], A["cols"][at].rearrange("l p n -> p (l n)")).then_inc(params_in, 16)
                act.dma_start(WAL[:], A["w_alpha"][at].rearrange("l p d n -> p (l d) n")).then_inc(params_in, 16)
                act.dma_start(KTC[:], A["keysT"][at].rearrange("l p a n -> p (l a) n")).then_inc(params_in, 16)
                act.dma_start(VC[:], A["vals"][at].rearrange("l (t p) n -> p (l t) n", p=P)).then_inc(params_in, 16)
                for d in range(2):
                    first = 0 if d == 0 else TS // P - 1
                    act.dma_start(ST[:, d, 0:2, first, :], A["hgrn"][at, :, d].rearrange("l p u v -> p (l u) v")).then_inc(params_in, 16)
                    act.dma_start(ST[:, d, 2:3, first, :], A["gla"][at, :, d:d + 1].rearrange("l p u v -> p (l u) v")).then_inc(params_in, 16)
                act.wait_ge(params_in, l * N_PARAM + N_PARAM)

                def inv_root(out, src, scale=1.0):
                    step.mark(act.activation(out, src, ACT.Ln, bias=EPSC[:, 0:1], scale=scale))
                    step.settle(act)
                    return act.activation(out, out, ACT.Exp, scale=-0.5)

                def squares(which):
                    for k in range(KT):
                        if k >= 2:
                            act.wait_ge(ms_ready, l * 16 + (8 * which + k - 1))
                        if which:
                            wait_taken(act, l, G_OUT + k)
                        act.activation(SQ[k % 2], XT[:, k, :], ACT.Square).then_inc(sq_ready, 1)
                    act.wait_ge(ms_ready, l * 16 + (8 * which + 8))
                    inv_root(RSTD[0], pair(2)[:, 0:T]).then_inc(rstd_ready, 1)

                squares(0)
                act.activation(SG[:].rearrange("p a b -> p (a b)"), COLS[:, C_COND:C_COND + 16], ACT.Sigmoid).then_inc(cond_sig, 1)
                act.wait_ge(lb_shift, l + 1)
                act.activation(LBE[:].rearrange("p a b c -> p (a b c)"), LBE[:].rearrange("p a b c -> p (a b c)"), ACT.Exp).then_inc(lb_exp, 1)
                act.wait_ge(lam_sum, l + 1)
                act.activation(LMS[:], LMS[:], ACT.Exp).then_inc(lam_exp, 1)

                def ada_row_out(s):
                    act.wait_ge(ada_row, l * N_ADA + (s + 1))
                    if s >= 2:
                        act.wait_ge(ada_done, l * N_ADA + (s - 1))
                    act.activation(ROW[s % 2], ada_out(s), ACT.Copy).then_inc(row_kept, 1)

                for s in range(N_ADA1):
                    ada_row_out(s)
                def head_square(i):
                    wait_taken(act, l, z_index(QK_TILES[i][0]))
                    if i >= 2:
                        act.wait_ge(qk_ms, l * NQK + (i - 1))
                    act.activation(SQ[i % 2], ZT[:, QK_TILES[i][0], :], ACT.Square).then_inc(qk_sq, 1)

                def head_inv_root(i):
                    act.wait_ge(qk_ms, l * NQK + (i + 1))
                    if i >= 2:
                        act.wait_ge(qk_normed, l * NQK + (i - 1))
                    inv_root(RSTD[i % 2], pair(2)[:, 0:T]).then_inc(qk_rstd, 1)

                for n, (c, kind, dst, j) in enumerate(ZT_TILES):
                    wait_full(act, l, n)
                    p = use(n)[0]
                    src = pair(p)[:, 0:T]
                    if kind == "tm":
                        m = 3 - j
                        act.activation(V[:, 3 * j:3 * j + m, dst:dst + 256], pair(p)[:, 0:256 * m].rearrange("p (i n) -> p i n", n=256),
                                       ACT.Copy).then_inc(gemm_free[p], 1)
                    elif kind == "tm1":
                        act.activation(V[:, :, dst:dst + P], src.rearrange("p (i n) -> p i n", n=P), ACT.Copy).then_inc(gemm_free[p], 1)
                    elif kind == "r":
                        act.activation(ZT[0:32, dst, :], src[0:32], ACT.Copy).then_inc(gemm_free[p], 1)
                    elif kind == "silu":
                        act.activation(ZT[:, dst, :], src, ACT.Sigmoid).then_inc(silu_sig, 1)
                    elif kind == "ff":
                        step.mark(act.activation(ZT[:, dst, :], src, ACT.Sigmoid))
                        act.activation(ZT[:, dst + BKF - BFF, :], src, ACT.Sigmoid, scale=-1.0).then_inc(gemm_free[p], 1)
                    elif kind == "dqk" and j == 0:
                        act.activation(ZT[:, dst, :], src, ACT.Copy, scale=32 ** -0.5).then_inc(gemm_free[p], 1)
                    else:
                        act.activation(ZT[:, dst, :], src, ACT.Copy).then_inc(gemm_free[p], 1)
                    if n < NZT - 1 and ZT_TILES[n + 1][0] == c:
                        continue
                    if 0 <= c - QK_AT - 1 < NQK:
                        head_inv_root(c - QK_AT - 1)
                    if 0 <= c - QK_AT < NQK:
                        head_square(c - QK_AT)
                    ada_row_out(N_ADA1 + c)
                for s in range(N_ADA1 + 14, N_ADA):
                    ada_row_out(s)

                act.wait_ge(qk_done, l * NQK + NQK)
                act.dma_start(O["keysT"][at].rearrange("l p a t -> p (l a) t"), ZT[:, AK:AK + 3, TS:T]).then_inc(stored, 16)
                act.dma_start(O["vals"][at].rearrange("l p n -> p (l n)"), V[:, NT - 1, 0:V_B]).then_inc(stored, 16)
                for d in range(2):
                    act.wait_ge(al_full, l * 2 + (d + 1))
                    step.mark(act.activation(TMP[d], pair(2)[:, 0:T], ACT.Identity, bias=COLS[:, C_AB + d:C_AB + d + 1]))
                    act.activation(SQ[d], pair(2)[:, 0:T], ACT.Abs, bias=COLS[:, C_AB + d:C_AB + d + 1]).then_inc(al_lin, 1)
                    act.wait_ge(al_lin, l * 2 + (d + 1))
                    step.mark(act.activation(SQ[d], SQ[d], ACT.Exp, scale=-1.0))
                    step.settle(act)
                    act.activation(SQ[d], SQ[d], ACT.Ln, bias=1.0).then_inc(al_log, 1)
                for d in range(2):
                    act.wait_ge(al_cut, l * 2 + (d + 1))
                    act.activation(ZT[:, (DAF, DAB)[d], :], TMP[d], ACT.Exp, scale=1.0 / 16).then_inc(al_ready, 1)

                def exponentials(g):
                    i, u = divmod(g, NU)
                    n = keys(i) * P
                    act.wait_ge(nmax_ready, l * NG + (g + 1))
                    act.activation(PROB[g % 2][:, 0:n], pair(1 + g % 2)[:, 0:n], ACT.Exp, bias=NMX[:, g % 2:g % 2 + 1],
                                   accum_out=SUMS[:, g % 2:g % 2 + 1]).then_inc(p_ready, 1)

                act.wait_ge(al_ready, l * 2 + 2)
                exponentials(0)
                exponentials(1)
                for g in range(NG):
                    n = keys(g // NU) * P
                    act.wait_ge(pt_full, l * NG + (g + 1))
                    if g >= 2:
                        act.wait_ge(pv_done, l * NG + (g - 1))
                    act.activation(PROBT[g % 2][:, 0:n], pair(3)[:, 0:n], ACT.Copy).then_inc(pt_kept, 1)
                    if g + 2 < NG:
                        exponentials(g + 2)
                act.wait_ge(o_taken, l * NT + NT)
                for j in range(2):
                    if j:
                        act.wait_ge(cms_ready, l * 2 + j)
                    act.activation(CSQ, ZT[:, CQ + j, :], ACT.Square).then_inc(csq_ready, 1)
                    act.wait_ge(cms_ready, l * 2 + (j + 1))
                    if j:
                        act.wait_ge(yc_done, l * 2 + j)
                    inv_root(CRSTD, pair(0)[:, 0:T]).then_inc(crstd_ready, 1)
                act.wait_ge(yc_done, l * 2 + 2)

                n_sc = 0
                for x, g in enumerate(GLA):
                    for d in range(2):
                        n6 = 2 * x + d
                        act.wait_ge(ko_turned, l * 6 + (n6 + 1))
                        if x:
                            act.wait_ge(ds_full, l * 6 + (n6 - 1))
                        act.activation(KOT[:, d].rearrange("p i n -> p (i n)"), pair(0)[:, 0:T], ACT.Copy).then_inc(ko_kept, 1)
                    n_sc += 2 * g[6] * NPASS
                    for grp in range(g[6]):
                        n_sc += 1
                        g0 = sum(y[6] for y in GLA[:x]) + grp
                        act.wait_ge(sc_full, l * NSC + n_sc)
                        if grp:
                            act.wait_ge(go_ms, l * NGRP + g0)
                        act.activation(KM[0], pair(2 + (n_sc - 1) % 2)[:, 0:T], ACT.Square).then_inc(go_sq, 1)
                        act.wait_ge(go_ms, l * NGRP + (g0 + 1))
                        if grp:
                            act.wait_ge(gy_kept, l * NGRP + g0)
                        inv_root(KM[1], pair(0)[:, 0:T]).then_inc(go_rstd, 1)

                act.wait_ge(st_ready, l * 6 + 6)
                act.dma_start(O["fin"][at].rearrange("l p n -> p (l n)"), FIN[:].rearrange("p a b c -> p (a b c)")).then_inc(states_stored, 16)
                with act.Fori(0, KT) as it:
                    for n in range(4):
                        g = G_MIX + 2 * n
                        wait_full(act, l, g, it * 8)
                        wait_room(act, l, g + 1, it * 2)
                        act.activation(SQ[n % 2], pair(use(g)[0])[:, 0:T], ACT.Sigmoid).then_inc(gemm_free[use(g)[0]], 1)
                squares(1)

                def ffn(j, turns):
                    f = turns * 4 + j
                    for h in range(2):
                        g = G_UP + 2 * j + h
                        wait_full(act, l, g, turns * 8)
                        if h == 0:
                            act.wait_ge(act_done, l * FT + f + 1)
                        col = f + h * FT
                        act.activation(FB[j % 2][h], pair(use(g)[0])[:, 0:T], ACT.Identity,
                                       bias=COLS[:, bass.ds(col + C_CB, 1)], scale=COLS[:, bass.ds(col + C_W1, 1)]).then_inc(centre_ready, 1)
                    wait_taken(act, l, g, turns * 2)
                    act.activation(FB[j % 2][1], FB[j % 2][1], ACT.Silu).then_inc(g_silu, 1)

                with act.Fori(0, 5) as it:
                    for j in range(4):
                        ffn(j, it)
                for j in range(20, 22):
                    ffn(j, 0)
                step.end(act)
            act.wait_ge(stored, DEPTH * N_STORE)
            act.wait_ge(states_stored, DEPTH * 16)

        @block.vector
        def _(v):
            step = dve
            nv = nc.vector
            v.wait_ge(x_in, 16)
            v.wait_ge(consts_in, 32)
            nv.tensor_copy(MASK[:].rearrange("p a b -> p (a b)"), WORK[:, 0:NPASS * P]).then_inc(mask_set, 1)
            v.wait_ge(mask_set, 1)
            nv.memset(EPSC[:], EPS).then_inc(eps_set, 1)
            v.sem_inc(act_done, 2)
            with v.Fori(0, DEPTH) as l:
                step.layer(l)

                def link(ins):
                    step.mark(ins)
                    step.settle(v)

                def bc(ap, n):
                    return ap.to_broadcast(list(ap.shape[:-1]) + [n])

                v.wait_ge(params_in, l * N_PARAM + N_PARAM)
                lbl = COLS[:, C_LB:C_LB + 8].rearrange("p (d l t) -> p d l t", d=2, l=2)
                link(nv.tensor_tensor(LBM[:], lbl[:, :, 0, :], lbl[:, :, 1, :], ALU.max))
                step.mark(nv.tensor_tensor(LBE[:, :, 0, :], lbl[:, :, 0, :], LBM[:], ALU.subtract))
                nv.tensor_tensor(LBE[:, :, 1, :], lbl[:, :, 1, :], LBM[:], ALU.subtract).then_inc(lb_shift, 1)
                lam = COLS[:, C_LAM:C_LAM + 128].rearrange("p (a b n) -> p a b n", a=2, b=2)
                link(nv.tensor_tensor(LPR, lam[:, :, 0, :], lam[:, :, 1, :], ALU.mult))
                nv.tensor_reduce(LMS[:], LPR, AX.X, ALU.add).then_inc(lam_sum, 1)
                v.wait_ge(cond_sig, l + 1)
                nv.tensor_tensor(SC[:].rearrange("p k g -> p g k"), COLS[:, C_COND:C_COND + 16].rearrange("p (g k) -> p g k", g=2),
                                 SG[:], ALU.mult).then_inc(cond_ready, 1)
                v.wait_ge(lb_exp, l + 1)
                link(nv.tensor_tensor(LBM[:], LBE[:, :, 0, :], LBE[:, :, 1, :], ALU.add))
                link(nv.reciprocal(LBM[:], LBM[:]))
                link(nv.tensor_tensor(LBM[:], LBM[:], LBE[:, :, 1, :], ALU.mult))
                link(nv.tensor_scalar(LBM[:], LBM[:], COLS[:, C_LC + 2:C_LC + 3], None, ALU.mult))
                step.mark(nv.tensor_scalar(LBF[:], LBM[:], LB_FLOOR, None, ALU.max))
                step.mark(nv.tensor_scalar(OML[:], LBM[:], -1.0, 1.0, ALU.mult, ALU.add))
                v.wait_ge(lam_exp, l + 1)
                link(nv.tensor_tensor(NLAM[:], LMS[:, 1:2], LMS[:, 0:1], ALU.subtract))
                step.mark(nv.tensor_tensor(NLAM[:], NLAM[:], COLS[:, C_LC:C_LC + 1], ALU.subtract))
                step.mark(nv.tensor_scalar(QG[:, 0:1], COLS[:, C_AQ:C_AQ + 1], 64 ** -0.5, None, ALU.mult))
                step.mark(nv.tensor_scalar(QG[:, 1:2], COLS[:, C_CQ:C_CQ + 1], 32 ** -0.5, None, ALU.mult))
                step.mark(nv.tensor_tensor(SUBG[:], COLS[:, C_SUB:C_SUB + 1], COLS[:, C_LC + 1:C_LC + 2], ALU.mult))

                def modulation(which, a, b):
                    v.wait_ge(ada_done, l * N_ADA + (N_ADA1, N_ADA)[which])
                    ps = pair(3)[:, TS + 2 * a:TS + 2 * b].rearrange("p (j g) -> p j g", g=2)
                    link(nv.tensor_tensor(MOD[:, a:b, :], ps, bc(COLS[:, C_BADA + a:C_BADA + b].rearrange("p (j o) -> p j o", o=1), 2), ALU.add))
                    scale, dst, gain = (MOD[:, 8:16, :], A1, C_N1) if which == 0 else (MOD[:, 32:40, :], A2, C_N2)
                    g = COLS[:, gain:gain + KT].rearrange("p (j o) -> p j o", o=1)
                    nv.scalar_tensor_tensor(out=dst[:], in0=scale, scalar=1.0, in1=bc(g, 2), op0=ALU.add, op1=ALU.mult).then_inc(mod_ready, 1)
                    v.wait_ge(mod_ready, l * 2 + (which + 1))

                def normed(which, gain, shift):
                    v.wait_ge(rstd_ready, l * 2 + (which + 1))
                    for k in range(KT):
                        link(nv.tensor_tensor(TMP[k % 2], XT[:, k, :], RSTD[0], ALU.mult))
                        for g, (a, b) in enumerate(SEG):
                            last = nv.tensor_scalar(HT[:, k, a:b], TMP[k % 2][:, a:b], gain[:, k, g:g + 1], MOD[:, shift + k, g:g + 1],
                                                    ALU.mult, ALU.add)
                            if g == 0:
                                step.mark(last)
                        last.then_inc(h_ready, 1)

                modulation(0, 0, 16)
                normed(0, A1, 0)

                def head_norm(i):
                    t, col, hd = QK_TILES[i]
                    gain = {C_AQ: QG[:, 0:1], C_CQ: QG[:, 1:2]}.get(col, COLS[:, col:col + 1])
                    v.wait_ge(qk_rstd, l * NQK + (i + 1))
                    nv.scalar_tensor_tensor(out=ZT[:, t, :], in0=ZT[:, t, :], scalar=gain, in1=RSTD[i % 2],
                                            op0=ALU.mult, op1=ALU.mult).then_inc(qk_normed, 1)
                    v.wait_ge(qk_normed, l * NQK + (i + 1))
                    step.mark(nv.tensor_tensor(TMP[0][:, 0:TS], ZT[:, t, 0:TS], cosA if hd == 64 else cosC, ALU.mult))

                def head_rotary(i):
                    t, _, hd = QK_TILES[i]
                    v.wait_ge(qk_rot, l * NQK + (i + 1))
                    link(nv.tensor_tensor(TMP[1][:, 0:TS], pair(3)[:, 0:TS], sinA if hd == 64 else sinC, ALU.mult))
                    nv.tensor_tensor(ZT[:, t, 0:TS], TMP[0][:, 0:TS], TMP[1][:, 0:TS], ALU.add).then_inc(qk_done, 1)

                sig = 0
                for n, (c, kind, dst, j) in enumerate(ZT_TILES):
                    if kind == "silu":
                        sig += 1
                        v.wait_ge(silu_sig, l * 6 + sig)
                        p = use(n)[0]
                        nv.tensor_tensor(ZT[:, dst, :], ZT[:, dst, :], pair(p)[:, 0:T], ALU.mult).then_inc(gemm_free[p], 1)
                    if kind == "ff":
                        d = (dst - BFF) // 2
                        wait_taken(v, l, n)
                        step.mark(nv.tensor_scalar(ZT[:, dst, :], ZT[:, dst, :], OML[:, d, j:j + 1], LBF[:, d, j:j + 1], ALU.mult, ALU.add))
                        nv.tensor_scalar(ZT[:, dst + BKF - BFF, :], ZT[:, dst + BKF - BFF, :], OML[:, d, j:j + 1], None, ALU.mult).then_inc(gla_in, 1)
                    if n < NZT - 1 and ZT_TILES[n + 1][0] == c:
                        continue
                    if 0 <= c - QK_AT - 2 < NQK:
                        head_rotary(c - QK_AT - 2)
                    if 0 <= c - QK_AT - 1 < NQK:
                        head_norm(c - QK_AT - 1)
                modulation(1, 16, 48)

                for d in range(2):
                    v.wait_ge(al_log, l * 2 + (d + 1))
                    nv.scalar_tensor_tensor(out=TMP[d], in0=TMP[d], scalar=0.0, in1=SQ[d], op0=ALU.min, op1=ALU.subtract).then_inc(al_cut, 1)

                def maxima(g):
                    v.wait_ge(s_full, l * NG + (g + 1))
                    nv.tensor_reduce(NMX[:, g % 2:g % 2 + 1], pair(1 + g % 2)[:, 0:keys(g // NU) * P], AX.X, ALU.max,
                                     negate=True).then_inc(nmax_ready, 1)

                def normalise(g):
                    i, u = divmod(g, NU)
                    p = PROB[g % 2][:, 0:keys(i) * P]
                    v.wait_ge(p_ready, l * NG + (g + 1))
                    link(nv.reciprocal(RCP[:, g % 2:g % 2 + 1], SUMS[:, g % 2:g % 2 + 1]))
                    if ATT[u][8] == 1:
                        nv.tensor_scalar(p, p, RCP[:, g % 2:g % 2 + 1], NLAM[:], ALU.mult, ALU.mult).then_inc(normed_p, 1)
                    else:
                        nv.tensor_scalar(p, p, RCP[:, g % 2:g % 2 + 1], None, ALU.mult).then_inc(normed_p, 1)

                def outputs(i):
                    v.wait_ge(pv_done, l * NG + NU * (i + 1))
                    o = pair(0)[:, i % 2 * TS:(i % 2 + 1) * TS].rearrange("p (a b t) -> p a b t", a=2, b=2)
                    step.mark(nv.tensor_copy(ZT[:, AQ:AQ + 2, i * P:(i + 1) * P], o[:, 0]))
                    nv.tensor_copy(ZT[:, CQ:CQ + 2, i * P:(i + 1) * P], o[:, 1]).then_inc(o_taken, 1)

                v.wait_ge(al_ready, l * 2 + 2)
                maxima(0)
                maxima(1)
                for g in range(NG):
                    normalise(g)
                    if g + 2 < NG:
                        maxima(g + 2)
                    if g and g % NU == 0:
                        outputs(g // NU - 1)
                outputs(NT - 1)

                def norm_c(j):
                    v.wait_ge(crstd_ready, l * 2 + (j + 1))
                    nv.scalar_tensor_tensor(out=ZT[:, CQ + j, :], in0=ZT[:, CQ + j, :], scalar=SUBG[:], in1=CRSTD,
                                            op0=ALU.mult, op1=ALU.mult).then_inc(yc_done, 1)

                v.wait_ge(gla_in, l * 4 + 4)
                cnt = 0

                def keep(h, p):
                    nonlocal cnt
                    v.wait_ge(sc_full, l * NSC + (cnt + 1))
                    ps = pair(2 + cnt % 2)[:, 0:T].rearrange("p (n t) -> p n t", n=NT)
                    if p == 0:
                        ins = nv.tensor_copy(SCORE[:, h], ps)
                    else:
                        v.sem_inc(scores_seen, 1)
                        m = MASK[:, p, :].rearrange("p (o t) -> p o t", o=1).to_broadcast([P, NT, P])
                        ins = nv.copy_predicated(SCORE[:, h], m, ps)
                    ins.then_inc(sc_kept, 1)
                    cnt += 1

                def states(x, d):
                    v.wait_ge(ds_full, l * 6 + (2 * x + d + 1))
                    ds = pair(1)[:, d * TS:d * TS + 320].rearrange("p (i n) -> p i n", n=64)
                    for i in (range(0, 3) if d == 0 else range(3, 0, -1)):
                        nxt = i + 1 if d == 0 else i - 1
                        link(nv.scalar_tensor_tensor(out=ST[:, d, x, nxt, :], in0=ST[:, d, x, i, :], scalar=DEC[:, d, i:i + 1], in1=ds[:, i, :],
                                                     op0=ALU.mult, op1=ALU.add))
                    nv.tensor_copy(FIN[:, d, x, :], ds[:, NT - 1, :]).then_inc(st_ready, 1)

                for x, (q, ks, a, gate, vb, rows, groups, gain) in enumerate(GLA):
                    before = sum(g[6] for g in GLA[:x])
                    first = before * (2 * NPASS + 1)
                    if x:
                        v.wait_ge(ko_turned, l * 6 + 2 * x)
                    if ks[0] == ks[1]:
                        ins = nv.tensor_scalar(KO[:, 0], ZT[:, ks[0], :], 2.0, None, ALU.mult)
                    else:
                        ins = nv.tensor_tensor(KO[:, 0], ZT[:, ks[0], :], ZT[:, ks[1], :], ALU.add)
                    ins.then_inc(lvl_ready, 1)
                    link(nv.memset(SX, 1.0))
                    for m in range(LEVELS):
                        p, h = 1 + m, 1 << m

                        def half(ap, w):
                            return ap.rearrange("p (b w h) -> p b w h", w=2, h=h)[:, :, w, :]

                        def edge(d, w):
                            e = half(ZT[:, a[d], :], w)
                            return e[:, :, h - 1:h] if d == 0 else e[:, :, 0:1]

                        if p >= 3:
                            v.wait_ge(sc_full, l * NSC + (first + 2 * groups * (p - 1)))
                        for d in range(2):
                            step.mark(nv.tensor_tensor(half(KM[p % 2], d), half(ZT[:, ks[d], :], d), half(SX[:, d], d), ALU.mult))
                        for d in range(2):
                            ins = nv.tensor_tensor(half(QM[p % 2], 1 - d), half(ZT[:, q, :], 1 - d), half(ZT[:, a[d], :], 1 - d), ALU.mult)
                            if d == 0:
                                step.mark(ins)
                        ins.then_inc(lvl_ready, 1)
                        for d in range(2):
                            step.mark(nv.tensor_tensor(half(SX[:, d], d), half(SX[:, d], d), bc(edge(d, 1 - d), h), ALU.mult))
                        step.settle(v)
                        for d in range(2):
                            R = half(ZT[:, a[d], :], 1 - d)
                            step.mark(nv.tensor_tensor(R, R, bc(edge(d, d), h), ALU.mult))
                        for hd in range(2 * groups):
                            keep(hd, p - 1)
                        if x == 0 and m in (2, 4):
                            norm_c(m // 2 - 1)
                        step.settle(v)
                    for d in range(2):
                        step.mark(nv.tensor_copy(DEC[:, d], ZT[:, a[d], :].rearrange("p (i t) -> p i t", t=P)[:, :, P - 1 if d == 0 else 0]))
                        nv.tensor_tensor(KO[:, d], ZT[:, ks[d], :], SX[:, d], ALU.mult).then_inc(ko_ready, 1)
                    step.settle(v)
                    for d in range(2):
                        step.mark(nv.tensor_tensor(ZT[:, a[d], :], ZT[:, q, :], ZT[:, a[d], :], ALU.mult))
                    for hd in range(2 * groups):
                        keep(hd, LEVELS)
                    for d in range(2):
                        states(x, d)
                    for grp in range(groups):
                        g0 = before + grp
                        v.wait_ge(go_rstd, l * NGRP + (g0 + 1))
                        link(nv.tensor_tensor(KM[1], pair(2 + cnt % 2)[:, 0:T], KM[1], ALU.mult))
                        cnt += 1
                        v.sem_inc(sc_kept, 1)
                        nv.scalar_tensor_tensor(out=ZT[:, gate + grp, :], in0=KM[1], scalar=COLS[:, gain:gain + 1],
                                                in1=ZT[:, gate + grp, :], op0=ALU.mult, op1=ALU.mult).then_inc(gy_kept, 1)

                with v.Fori(0, KT) as it:
                    v.wait_ge(stored, l * N_STORE + N_STORE)
                    step.enter(it, 3)
                    for n in range(4):
                        g = G_MIX + 2 * n
                        p = use(g + 1)[0]
                        wait_taken(v, l, g, it * 2)
                        wait_full(v, l, g + 1, it * 8)
                        dst = ZT[:, bass.ds(it + MIXT, 1), :].rearrange("p a t -> p (a t)")
                        if n == 0:
                            nv.tensor_tensor(dst, SQ[0], pair(p)[:, 0:T], ALU.mult).then_inc(gemm_free[p], 1)
                            wait_taken(v, l, g + 1, it * 2)
                        else:
                            nv.tensor_tensor(TMP[n % 2], SQ[n % 2], pair(p)[:, 0:T], ALU.mult).then_inc(gemm_free[p], 1)
                            wait_taken(v, l, g + 1, it * 2)
                            link(nv.tensor_tensor(dst, dst, TMP[n % 2], ALU.add))
                    v.sem_inc(mix_done, 1)
                step.leave(KT)

                def residual(g, k, shift, turns, flag):
                    p = use(g)[0]
                    for s, (a, b) in enumerate(SEG):
                        x = XT[:, bass.ds(k, 1), a:b].rearrange("p a t -> p (a t)")
                        gate = MOD[:, bass.ds(k + shift, 1), s:s + 1].rearrange("p a t -> p (a t)")
                        ins = nv.scalar_tensor_tensor(out=x, in0=pair(p)[:, a:b], scalar=gate, in1=x, op0=ALU.mult, op1=ALU.add)
                        if s == 0:
                            step.mark(ins)
                    ins.then_inc(gemm_free[p], 1)

                for k in range(KT):
                    wait_full(v, l, G_OUT + k)
                    residual(G_OUT + k, k, 16, 0, None)
                wait_taken(v, l, G_OUT + KT - 2)
                wait_taken(v, l, G_OUT + KT - 1)
                normed(1, A2, 24)

                def conv(j, turns):
                    f = turns * 4 + j
                    for h in range(2):
                        g = G_UP + 2 * j + h
                        u = pair(use(g)[0])
                        c = FB[j % 2][h]
                        v.wait_ge(centre_ready, l * 44 + turns * 8 + (2 * j + h + 1))
                        col = f + h * FT
                        for s, (a, b) in enumerate(SEG):
                            step.mark(nv.scalar_tensor_tensor(out=c[:, a + 1:b], in0=u[:, a:b - 1], scalar=COLS[:, bass.ds(col + C_W0, 1)],
                                                              in1=c[:, a + 1:b], op0=ALU.mult, op1=ALU.add))
                        step.settle(v)
                        for s, (a, b) in enumerate(SEG):
                            ins = nv.scalar_tensor_tensor(out=c[:, a:b - 1], in0=u[:, a + 1:b], scalar=COLS[:, bass.ds(col + C_W2, 1)],
                                                          in1=c[:, a:b - 1], op0=ALU.mult, op1=ALU.add)
                            if s == 0:
                                step.mark(ins)
                        ins.then_inc(gemm_free[use(g)[0]], 1)
                    v.wait_ge(g_silu, l * FT + f + 1)
                    nv.tensor_tensor(ZT[:, bass.ds(f, 1), :].rearrange("p a t -> p (a t)"), FB[j % 2][0], FB[j % 2][1], ALU.mult).then_inc(act_done, 1)

                with v.Fori(0, 5) as it:
                    step.enter(it, 24)
                    for j in range(4):
                        conv(j, it)
                step.leave(5)
                for j in range(20, 22):
                    conv(j, 0)
                with v.Fori(0, 2) as it:
                    step.enter(it, 4)
                    for j in range(4):
                        wait_full(v, l, G_DOWN + j, it * 4)
                        residual(G_DOWN + j, it * 4 + j, 40, it, None)
                step.leave(2)
                for n in range(4, 8):
                    wait_taken(v, l, G_DOWN + n)
                v.sem_inc(layer_done, 1)
                step.end(v)


def shape_constants():
    import numpy as np

    def rope(hd):
        half = hd // 2
        freqs = np.float32(10000.0) ** (-np.arange(0, half, 2, dtype=np.float32) / np.float32(half))
        row = np.repeat(np.arange(TS // 64), 64).astype(np.float32)
        col = np.tile(np.arange(64), TS // 64).astype(np.float32)
        r, c = row[:, None] * freqs, col[:, None] * freqs
        ang = np.concatenate([r, r, c, c], axis=-1)
        return [np.tile(f(ang).T, (P // hd, 1)).astype(np.float32) for f in (np.cos, np.sin)]

    def rotation(hd):
        q = hd // 4
        m = np.zeros((P, P), np.float32)
        for d in range(P):
            if d // q % 2 == 0:
                m[d + q, d] = -1.0
            else:
                m[d - q, d] = 1.0
        return m

    s = np.arange(P)
    blocks = [np.eye(P), np.full((P, P), 1.0 / D), (s[:, None] // 64 == s // 64) / 64.0, (s[:, None] // 32 == s // 32) / 32.0,
              rotation(64), rotation(32)]
    const = np.concatenate(rope(64) + rope(32) + blocks, axis=1).astype(np.float32)
    mask = np.zeros((P, NPASS, P), np.float32)
    for m in range(LEVELS):
        h = 1 << m
        mask[:, 1 + m] = (s[:, None] // (2 * h) == s // (2 * h)) & (s[:, None] // h != s // h)
    return const, mask.reshape(P, -1)


def kernel(**inputs):
    import math

    import concourse.bacc as _bacc
    import numpy as np
    from concourse.bass_utils import run_bass_kernel_spmd as _run

    a = {k: np.asarray(v) for k, v in inputs.items()}

    def columns(x):
        return x.reshape(x.shape[0], -1, P).transpose(0, 2, 1)

    def twice(x):
        return np.tile(x, (1, P // x.shape[1]))[:, :, None]

    def each(x):
        return np.broadcast_to(x, (DEPTH,) + x.shape)

    lb = a["b_lb_logits"].reshape(2, DEPTH, 2, P).transpose(3, 0, 1, 2).reshape(P, 8)
    cond = np.stack([a["c"][0].reshape(KT, P), a["c_ctx"].reshape(KT, P)]).transpose(2, 0, 1).reshape(P, 16)
    lam_init = [0.8 - 0.6 * math.exp(-0.3 * l) for l in range(DEPTH)]
    layer_const = np.array([[[x, 1.0 - x, float(l > 0)]] * P for l, x in enumerate(lam_init)], np.float32)
    cols = np.concatenate([
        columns(a["b_ada"]), columns(a["norm1_g"]), columns(a["norm2_g"]), columns(a["conv_b"]),
        twice(a["a_qn_g"]), twice(a["a_kn_g"]), twice(a["c_qn_g"]), twice(a["c_kn_g"]), twice(a["c_subln_g"]),
        twice(a["b_norm_g"]), twice(a["d_norm_g"]), a["d_alpha_b"].transpose(0, 2, 1),
        columns(a["conv_w"][:, 0]), columns(a["conv_w"][:, 1]), columns(a["conv_w"][:, 2]), each(lb), each(cond), layer_const,
        np.broadcast_to(a["c_lambda"].reshape(DEPTH, 1, P), (DEPTH, P, P)),
    ], axis=2)
    assert cols.shape == (DEPTH, P, NCOL)
    w_alpha = np.zeros((DEPTH, 32, 2, P), np.float32)
    for d in range(2):
        w_alpha[:, 16 * d:16 * d + 16, d] = a["d_alpha_w"][:, d]
    keys_a = a["cache_a_k"][0].reshape(DEPTH, PAST, 1, P)
    keys_c = a["cache_c_k"][0].reshape(DEPTH, PAST, 2, P)
    const, mask = shape_constants()
    arrays = {
        "xT": np.concatenate([a["x_sample"][0], a["x_prompt"][0]]).reshape(T, KT, P).transpose(2, 1, 0),
        "cols": cols, "w_alpha": w_alpha, "const": const, "mask": mask,
        "keysT": np.concatenate([keys_a, keys_c], axis=2).transpose(0, 3, 2, 1),
        "vals": np.concatenate([a["cache_a_v"][0].reshape(DEPTH, PAST, P), a["cache_c_v"][0].reshape(DEPTH, PAST, 256)], axis=2),
        "hgrn": a["state_hgrn"][0].reshape(DEPTH, 2, 2, P, 64).transpose(0, 3, 1, 2, 4),
        "gla": a["state_gla"][0].reshape(DEPTH, 2, P, 64).transpose(0, 2, 1, 3),
        "w_ada": a["w_ada"], "w_in": a["w_in"], "w_branch": a["w_branch"], "w_out": a["w_out"], "w_up": a["w_up"], "w_down": a["w_down"],
    }
    arrays = {k: np.ascontiguousarray(x) for k, x in arrays.items()}
    outs = {"yT": (P, KT, T), "keysT": (DEPTH, P, 3, P), "vals": (DEPTH, P, V_B), "fin": (DEPTH, P, 2 * 3 * 64)}
    nc = _bacc.Bacc("TRN2", target_bir_lowering=False, num_devices=1)
    A = {k: nc.dram_tensor(f"in_{k}", x.shape, mybir.dt.from_np(x.dtype), kind="ExternalInput").ap() for k, x in arrays.items()}
    O = {k: nc.dram_tensor(f"out_{k}", s, F32, kind="ExternalOutput").ap() for k, s in outs.items()}
    build(nc, A, O)
    r = _run(nc, [{f"in_{k}": x for k, x in arrays.items()}], core_ids=[0]).results[0]
    y = r["out_yT"].transpose(2, 1, 0).reshape(T, D)
    keys_ = r["out_keysT"].transpose(0, 3, 2, 1)
    vals = r["out_vals"]
    fin = r["out_fin"].reshape(DEPTH, P, 2, 3, 64)
    hgrn = fin[:, :, :, 0:2].transpose(0, 2, 3, 1, 4).reshape(1, DEPTH, 2, 4, 64, 64)
    gla = fin[:, :, :, 2].transpose(0, 2, 1, 3).reshape(1, DEPTH, 2, 4, 32, 64)
    outputs = (y[TS:][None], y[:TS][None], keys_[:, :, 0].reshape(1, DEPTH, TC, 2, 64), vals[:, :, 0:P].reshape(1, DEPTH, TC, 2, 64),
               keys_[:, :, 1:3].reshape(1, DEPTH, TC, 4, 2, 32), vals[:, :, P:].reshape(1, DEPTH, TC, 4, 64), hgrn, gla)
    return tuple(np.ascontiguousarray(x) for x in outputs)
```

```python
from contextlib import ExitStack

import concourse.bass as bass
from concourse import mybir

F32 = mybir.dt.float32
F32R = mybir.dt.float32r
U8 = mybir.dt.uint8
ALU = mybir.AluOpType
ACT = mybir.ActivationFunctionType
AX = mybir.AxisListType

P = 128
D = 1024
KT = D // P
DEPTH = 2
TS, TC = 512, 128
T = TS + TC
NT = T // P
PAST = 256
FF = 2816
FT = FF // P
EPS = 1e-6
LB_FLOOR = 1e-30
SEG = ((0, TS), (TS, T))
Z_COLS = 3360

AQ, BG, CQ, DG, AK, CK, BQ, BFF, BFB, BKF, BKB, DQ, DK, DR, DAB, NZ = 0, 2, 4, 6, 8, 9, 11, 13, 15, 17, 19, 21, 22, 23, 24, 25
DAF = DR
MIXT = 8
V_A, V_C, V_B, V_D, NV = 0, 128, 384, 640, 896

(C_BADA, C_N1, C_N2, C_CB, C_AQ, C_AK, C_CQ, C_CK, C_SUB, C_BN, C_DN, C_AB, C_W0, C_W1, C_W2, C_LB, C_COND, C_LC, C_LAM, NCOL) = (
    0, 48, 56, 64, 108, 109, 110, 111, 112, 113, 114, 115, 117, 161, 205, 249, 257, 273, 276, 404)

N_SLOT = 4
C_MIX, C_OUT, C_UP, C_DOWN, CHUNKS = 38, 70, 74, 96, 112
SLOT_W = 2048
N_ADA1, N_ADA = 8, 24
ADA_SPLIT = range(N_ADA1, N_ADA1 + 14)
CHUNK_Z = [N_ADA1 + 2 * c for c in range(14)]
CHUNK_ADA = list(range(N_ADA1)) + [N_ADA1 + 1 + 2 * c for c in range(14)] + [36, 37]

Z_PLAN = [(0, "q", AQ), (1, "kv", AK), (2, "fm", CQ), (3, "fm", CK), (13, "r", DR), (4, "tm", V_C), (5, "silu", BQ),
          (6, "tm", V_B), (7, "ff", BFF), (8, "ff", BFB), (9, "silu", BG), (10, "dqk", DQ), (11, "tm", V_D), (12, "silu", DG)]
QK_AT = 4


def z_tiles():
    out = []
    for c, (_, kind, dst) in enumerate(Z_PLAN):
        if kind == "kv":
            out += [(c, "fm", AK, 0), (c, "tm1", V_A, 1)]
        elif kind == "tm":
            out += [(c, "tm", dst, 0), (c, "tm", dst, 1)]
        elif kind == "r":
            out += [(c, "r", dst, 0)]
        else:
            out += [(c, kind, dst + j, j) for j in range(2)]
    return out


ZT_TILES = z_tiles()
NZT = len(ZT_TILES)
USES_Z = [(NZT + 1) // 2, NZT // 2, 0, 0]
USES_MIX, USES_OUT, USES_UP, USES_DOWN = 16, 2, 11, 2
USES = [u + USES_MIX + USES_OUT + USES_UP + USES_DOWN for u in USES_Z]
N_GEMM = NZT + 64 + 8 + 44 + 8
G_MIX, G_OUT, G_UP, G_DOWN = NZT, NZT + 64, NZT + 72, NZT + 116

N_SPLIT_MIX = 32
N_SPLIT_UP = N_SPLIT_MIX + 44
N_SPLIT = N_SPLIT_UP + 16

STEPS = 4096
QK_TILES = [(AQ, C_AQ, 64), (AQ + 1, C_AQ, 64), (AK, C_AK, 64), (CQ, C_CQ, 32), (CQ + 1, C_CQ, 32),
            (CK, C_CK, 32), (CK + 1, C_CK, 32)]
NQK = len(QK_TILES)
ATT = [(AQ + j, 64 * g, 64, AK, 0, V_A + 64 * g, g, 64 * j, None) for j in range(2) for g in range(2)] + \
      [(CQ + h // 2, 64 * (h % 2) + 32 * m, 32, CK + h // 2, 1 + h // 2, V_C + 64 * h, 2 + h // 2, 64 * (h % 2), m)
       for h in range(4) for m in range(2)]
NU = len(ATT)
GLA = [(BQ, (BKF, BKB), (BFF, BFB), BG, V_B, 64, 1, C_BN), (BQ + 1, (BKF + 1, BKB + 1), (BFF + 1, BFB + 1), BG + 1, V_B + 128, 64, 1, C_BN),
       (DQ, (DK, DK), (DAF, DAB), DG, V_D, 32, 2, C_DN)]
LEVELS = 7
NG = NT * NU
NPASS = LEVELS + 1
NGRP = sum(g[6] for g in GLA)
NSC = NGRP * 2 * NPASS




def keys(i):
    return 1 if i == NT - 1 else (TS + PAST) // P


class Chain:

    def __init__(self, sem):
        self.sem, self.n, self.base = sem, 0, 0

    def layer(self, l):
        self.l, self.n, self.base = l, 0, l * STEPS

    def mark(self, ins):
        self.n += 1
        ins.then_inc(self.sem, 1)

    def settle(self, eng):
        eng.wait_ge(self.sem, self.base + self.n)

    def enter(self, it, per):
        self.n0, self.per, self.base = self.n, per, self.l * STEPS + it * per

    def leave(self, count):
        assert self.n - self.n0 == self.per, (self.n - self.n0, self.per)
        self.n, self.base = self.n0 + count * self.per, self.l * STEPS

    def end(self, eng):
        assert self.n <= STEPS, self.n
        if self.n < STEPS:
            eng.sem_inc(self.sem, STEPS - self.n)


def build(nc, A, O):
    ctx = ExitStack()
    with ctx:
        def sb(name, shape, dt=F32):
            return ctx.enter_context(nc.sbuf_tensor(name, shape, dt))

        def both(name, shape):
            with nc.sbuf_tensor(name, shape, F32) as plain:
                pass
            return plain, sb(name + "_split", shape, F32R)

        def sem(name):
            return ctx.enter_context(nc.semaphore(name))

        XT = sb("XT", [P, KT, T])
        HT, HT_R = both("HT", [P, KT, T])
        RING, RING_R = both("RING", [P, N_SLOT, SLOT_W])
        ZT, ZT_R = both("ZT", [P, NZ, T])
        V, V_R = both("V", [P, NT, NV])
        WORK, WORK_R = both("WORK", [P, 5120])
        KO, KO_R = both("KO", [P, 2, T])
        KOT = WORK[:, 2560:3840].rearrange("p (d i n) -> p d i n", d=2, i=NT)
        CONST = sb("CONST", [P, 4 * TS + 6 * P])
        MASK = sb("MASK", [P, NPASS, P], U8)
        CACHE, CACHE_R = both("CACHE", [P, 3 * PAST + 2 * V_B])
        KTC = CACHE[:, 0:3 * PAST].rearrange("p (a n) -> p a n", a=3)
        VC = CACHE[:, 3 * PAST:].rearrange("p (t n) -> p t n", t=2)
        ST = sb("ST", [P, 2, 3, NT, 64])
        FIN = sb("FIN", [P, 2, 3, 64])
        COLS = sb("COLS", [P, NCOL])
        MOD = sb("MOD", [P, 48, 2])
        A1 = sb("A1", [P, KT, 2])
        A2 = sb("A2", [P, KT, 2])
        SC = sb("SC", [P, KT, 2])
        SC4 = sb("SC4", [P, KT, 4], F32R)
        SG = sb("SG", [P, 2, KT])
        LBE = sb("LBE", [P, 2, 2, 2])
        LBM = sb("LBM", [P, 2, 2])
        LBF = sb("LBF", [P, 2, 2])
        OML = sb("OML", [P, 2, 2])
        LMS = sb("LMS", [P, 2])
        NLAM = sb("NLAM", [P, 1])
        WAL = sb("WAL", [32, 2, P])
        SUBG = sb("SUBG", [P, 1])
        EPSC = sb("EPSC", [P, 1])
        NMX = sb("NMX", [P, 2])
        SUMS = sb("SUMS", [P, 2])
        RCP = sb("RCP", [P, 2])
        QG = sb("QG", [P, 2])
        DEC = sb("DEC", [P, 2, NT])
        PS = ctx.enter_context(nc.psum_tensor("PS", [P, 4, 1024], F32))

        cosA, sinA, cosC, sinC = (CONST[:, i * TS:(i + 1) * TS] for i in range(4))
        IDENT, ONES, BLK64, BLK32, ROTA, ROTC = (CONST[:, 4 * TS + i * P:4 * TS + (i + 1) * P] for i in range(6))
        MASK_IN = ZT[:, 23:25, :].rearrange("p a t -> p (a t)")[:, 0:NPASS * P]
        LPR = WORK[:, 4096:4160].rearrange("p (a n) -> p a n", a=2)
        SQ = [WORK[:, 0:T], WORK[:, T:2 * T]]
        RSTD = [WORK[:, 2 * T:3 * T], WORK[:, 3 * T:4 * T]]
        TMP = [KO[:, 0], KO[:, 1]]
        FB = [[WORK[:, (2 * b + h) * T:(2 * b + h + 1) * T] for h in range(2)] for b in range(2)]
        ROW = [WORK[0:4, 4608 + 256 * b:4864 + 256 * b] for b in range(2)]
        ADA_HI = [WORK_R[:, 2560 + 1024 * h:3584 + 1024 * h] for h in range(2)]
        PROB = [WORK[:, 0:768], WORK[:, 768:1536]]
        PROBT = [WORK[:, 1536:2304], WORK[:, 2304:3072]]
        YSQ, YRSTD = WORK[:, 2560:3200], WORK[:, 3200:3840]
        SCORE = WORK[:, 0:2560].rearrange("p (h n t) -> p h n t", h=4, n=NT)
        KM = [WORK[:, 3840:4480], WORK[:, 4480:5120]]
        QM = [RING[:, b, 1280:1280 + T] for b in range(2)]
        SX = RING[:, 2:4, 1280:1280 + T]

        W_HI = [WORK_R[:, 2560 + 1024 * b:3584 + 1024 * b].rearrange("p (k n) -> p k n", n=P) for b in range(2)]
        W_LO = [x.rearrange("p (k n) -> p k n", n=P) for x in (KO_R[:].rearrange("p d t -> p (d t)")[:, 0:1024], CACHE_R[:, 0:1024])]
        H_LO = V_R[:].rearrange("p i n -> p (i n)")[:, 0:KT * TS].rearrange("p (k t) -> p k t", t=TS)
        H_HI = ZT_R[:, 16:16 + KT, 0:TS]

        DW_HI = [WORK_R[:, 3456:4864], WORK_R[:, 2048:3456]]
        DW_LO = [CACHE_R[:, 0:11 * P], ZT_R[:, FT:NZ, :].rearrange("p a t -> p (a t)")[:, 0:11 * P]]
        D_HI = [HT_R[:].rearrange("p k t -> p (k t)")[:, TS * k:TS * (k + 1)] for k in range(10)] + \
               [V_R[:].rearrange("p i n -> p (i n)")[:, TS * k:TS * (k + 1)] for k in range(8)] + \
               [WORK_R[:, TS * k:TS * (k + 1)] for k in range(4)]

        landed = [sem(f"landed{i}") for i in range(N_SLOT)]
        landed_q = sem("landed_q")
        slot_freed = sem("slot_freed")
        x_in, consts_in, params_in, stored, states_stored, y_stored = sem("x_in"), sem("consts_in"), sem("params_in"), sem("stored"), sem("states_stored"), sem("y_stored")
        eps_set, zero_set, mask_set = sem("eps_set"), sem("zero_set"), sem("mask_set")
        mask_in = sem("mask_in")
        cond_sig, cond_ready = sem("cond_sig"), sem("cond_ready")
        lb_shift, lb_exp, lam_sum, lam_exp, small_ready = (sem(n) for n in ("lb_shift", "lb_exp", "lam_sum", "lam_exp", "small_ready"))
        ada_row, row_kept, ada_done, mod_ready = sem("ada_row"), sem("row_kept"), sem("ada_done"), sem("mod_ready")
        sq_ready, ms_ready, rstd_ready, h_ready = sem("sq_ready"), sem("ms_ready"), sem("rstd_ready"), sem("h_ready")
        gemm_full = sem("gemm_full")
        gemm_free = [sem(f"gemm_free{i}") for i in range(4)]
        silu_sig, gla_in = sem("silu_sig"), sem("gla_in")
        qk_sq, qk_ms, qk_rstd, qk_normed, qk_rot, qk_done = (sem(f"qk_{n}") for n in ("sq", "ms", "rstd", "normed", "rot", "done"))
        al_full, al_lin, al_log, al_cut, al_ready = (sem(f"al_{n}") for n in ("full", "lin", "log", "cut", "ready"))
        s_full, nmax_ready, p_ready, normed_p, pt_full, pt_kept, pv_done, o_taken = (
            sem(n) for n in ("s_full", "nmax_ready", "p_ready", "normed_p", "pt_full", "pt_kept", "pv_done", "o_taken"))
        csq_ready, cms_ready, crstd_ready, yc_done = (sem(n) for n in ("csq_ready", "cms_ready", "crstd_ready", "yc_done"))
        lvl_ready, sc_full, sc_kept, scores_seen = sem("lvl_ready"), sem("sc_full"), sem("sc_kept"), sem("scores_seen")
        ko_ready, ko_turned, ko_kept, ds_full, st_ready = (sem(n) for n in ("ko_ready", "ko_turned", "ko_kept", "ds_full", "st_ready"))
        go_full, go_sq, go_ms, go_rstd, gy_kept = (sem(n) for n in ("go_full", "go_sq", "go_ms", "go_rstd", "gy_kept"))
        mix_done = sem("mix_done")
        gate_hi, gate_h = sem("gate_hi"), sem("gate_h")
        hi_made, lo_made, norm_hi_in, norm_hi = sem("hi_made"), sem("lo_made"), sem("norm_hi_in"), sem("norm_hi")
        ada_hi, ada_lo = sem("ada_hi"), sem("ada_lo")
        d_hi, d_ready, dw_used = sem("d_hi"), sem("d_ready"), sem("dw_used")
        centre_ready, g_silu, act_done = sem("centre_ready"), sem("g_silu"), sem("act_done")
        layer_done = sem("layer_done")
        dve_chain, act_chain = Chain(sem("dve_step")), Chain(sem("act_step"))
        N_PARAM = 16 * 8
        N_STORE = 16 * 2

        def pair(i):
            return PS[:, i, :]

        def ada_out(s):
            return pair(s % 2)[0:2, 0:256] if s < N_ADA1 else pair(3)[0:ada_rows(s), 768:1024]

        def ada_rows(s):
            return 4 if s in ADA_SPLIT else 2

        def use(n):
            if n < G_MIX:
                return n % 2, n // 2
            return (n - G_MIX) % 4, USES_Z[(n - G_MIX) % 4] + (n - G_MIX) // 4

        def wait_taken(eng, l, n, turns=0):
            p, k = use(n)
            eng.wait_ge(gemm_free[p], l * USES[p] + turns + (k + 1))

        def wait_room(eng, l, n, turns=0):
            p, k = use(n)
            eng.wait_ge(gemm_free[p], l * USES[p] + turns + k)

        def wait_full(eng, l, n, tiles=0):
            eng.wait_ge(gemm_full, l * N_GEMM + tiles + (n + 1))

        def raw(i, block):
            return RING[:, i % N_SLOT, 1024 * block:1024 * block + 1024].rearrange("p (k n) -> p k n", n=P)

        def as_f32(ap):
            return ap.bitcast(F32)

        def z_index(tile):
            return next(n for n, t in enumerate(ZT_TILES) if t[1] not in ("tm", "tm1") and t[2] == tile)

        block = ctx.enter_context(nc.Block())

        @block.sync
        def _(sp):
            w_ada = A["w_ada"].rearrange("l (k p) n -> p l k n", p=P)
            w_in = A["w_in"].rearrange("l (k p) n -> p l k n", p=P)
            w_br = A["w_branch"].rearrange("l b (k p) n -> p l b k n", p=P)
            w_out = A["w_out"].rearrange("l (k p) n -> p l k n", p=P)
            w_up = A["w_up"].rearrange("l (k p) n -> p l k n", p=P)
            w_dn = A["w_down"].rearrange("l (k p) n -> p l k n", p=P)

            sp.sem_inc(slot_freed, N_SLOT - 1)
            sp.dma_start(XT[:], A["xT"]).then_inc(x_in, 16)
            with sp.Fori(0, DEPTH) as l:
                def slot_free(i, chunks=0):
                    sp.wait_ge(slot_freed, l * CHUNKS + chunks + (i + 1))

                def part(dst, w, s, k0, k1, col, width):
                    src = w[:, bass.ds(l, 1), k0:k1, bass.ds(col, width)].rearrange("p l k n -> p (l k) n")
                    sp.dma_start(dst, src).then_inc(landed[s], 16)

                def columns(w, s, col, width):
                    dst = RING[:, s, 0:8 * width].rearrange("p (k n) -> p k n", n=width)
                    part(dst[:, 0:4, :], w, s, 0, 4, col, width)
                    part(dst[:, 4:8, :], w, s, 4, 8, col, width)

                def up_chunk(j, s, col):
                    for h in range(2):
                        dst = RING[:, s, 1024 * h:1024 * h + 1024].rearrange("p (k n) -> p k n", n=P)
                        part(dst, w_up, s, 0, 8, col + (h * FF + j * P), P)

                def ada_chunk(s):
                    i = CHUNK_ADA[s]
                    slot_free(i)
                    columns(w_ada, i % N_SLOT, 256 * s, 256)

                def z_chunk(c):
                    i = CHUNK_Z[c]
                    slot_free(i)
                    if c:
                        columns(w_in, i % N_SLOT, 256 * Z_PLAN[c][0], 32 if Z_PLAN[c][1] == "r" else 256)
                        return
                    dst = RING[:, i % N_SLOT, :].rearrange("p (k j g d) -> p k j g d", j=2, g=2, d=64)
                    src = w_in[:, bass.ds(l, 1), :, 0:256].rearrange("p l k (g j d) -> p (l k) j g d", g=2, j=2)
                    for j in range(2):
                        for g in range(2):
                            sp.dma_start(dst[:, :, j, g], src[:, :, j, g]).then_inc(landed_q if j else landed[i % N_SLOT], 16)

                for s in range(N_ADA1):
                    ada_chunk(s)
                for c in range(14):
                    z_chunk(c)
                    ada_chunk(N_ADA1 + c)
                for s in range(N_ADA1 + 14, N_ADA):
                    ada_chunk(s)
                with sp.Fori(0, KT) as it:
                    for n in range(4):
                        s = (C_MIX + n) % 4
                        slot_free(C_MIX + n, it * 4)
                        part(RING[:, s, 0:1024].rearrange("p (k n) -> p k n", n=P), w_in, s, 0, 8, it * P + (Z_COLS + n * D), P)
                        src = w_br[:, bass.ds(l, 1), n, :, bass.ds(it * P, P)].rearrange("p l k n -> p (l k) n")
                        sp.dma_start(RING[:, s, 1024:1280].rearrange("p (k n) -> p k n", n=P), src).then_inc(landed[s], 16)
                for c in range(4):
                    slot_free(C_OUT + c)
                    columns(w_out, (C_OUT + c) % 4, 256 * c, 256)
                with sp.Fori(0, 5) as it:
                    for j in range(4):
                        slot_free(C_UP + j, it * 4)
                        up_chunk(j, (C_UP + j) % 4, it * 4 * P)
                for j in range(20, 22):
                    slot_free(C_UP + j)
                    up_chunk(j, (C_UP + j) % 4, 0)
                with sp.Fori(0, 2) as it:
                    for j in range(8):
                        s = (C_DOWN + j) % 4
                        slot_free(C_DOWN + j, it * 8)
                        k0 = 11 * (j % 2)
                        dst = RING[:, s, 0:11 * P].rearrange("p (k n) -> p k n", n=P)
                        part(dst[:, 0:6, :], w_dn, s, k0, k0 + 6, it * 4 * P + (j // 2) * P, P)
                        part(dst[:, 6:11, :], w_dn, s, k0 + 6, k0 + 11, it * 4 * P + (j // 2) * P, P)
            sp.wait_ge(layer_done, DEPTH)
            sp.dma_start(O["yT"], XT[:]).then_inc(y_stored, 16)
            sp.wait_ge(y_stored, 16)

        @block.gpsimd
        def _(pool):
            pool.dma_start(CONST[:], A["const"]).then_inc(consts_in, 16)
            pool.memset(ST[:], 0.0).then_inc(zero_set, 1)

        @block.tensor
        def _(pe):
            pe.wait_ge(consts_in, 16)
            with pe.Fori(0, DEPTH) as l:
                def chunk(i, turns=0):
                    pe.wait_ge(landed[i % N_SLOT], l * (32 * CHUNKS // N_SLOT) + turns * 32 + 32 * (i // N_SLOT + 1))

                def release(ins, first):
                    if first:
                        ins.then_inc(slot_freed, 1)

                def wide(out, lhsT, rhs, start, stop, first=False):
                    release(pe.matmul(out[:, 0:TS], lhsT, rhs[:, 0:TS], start=start, stop=stop), first)
                    return pe.matmul(out[:, TS:T], lhsT, rhs[:, TS:T], start=start, stop=stop)

                def weights(i, width):
                    return RING[:, i % N_SLOT, 0:8 * width].rearrange("p (k n) -> p k n", n=width)

                def ada(s):
                    i = CHUNK_ADA[s]
                    chunk(i)
                    w = weights(i, 256)
                    if s in ADA_SPLIT:
                        for k in range(KT):
                            if k % 4 == 0:
                                pe.wait_ge(ada_lo, l * 2 * len(ADA_SPLIT) + (2 * (s - N_ADA1) + k // 4 + 1))
                            n = slice(k % 4 * 256, k % 4 * 256 + 256)
                            release(pe.matmul(ada_out(s), SC4[:, k, :], ADA_HI[k // 4][:, n], start=k == 0, stop=False), k == 0)
                            last = pe.matmul(ada_out(s), SC4[:, k, :], RING_R[:, i % N_SLOT, 256 * k:256 * k + 256], start=False, stop=k == KT - 1)
                        last.then_inc(ada_row, 1)
                        return
                    for k in range(KT):
                        last = pe.matmul(ada_out(s), SC[:, k, :], w[:, k, :], start=k == 0, stop=k == KT - 1)
                        release(last, k == 0)
                    last.then_inc(ada_row, 1)

                def ada_turn(s):
                    pe.wait_ge(row_kept, l * N_ADA + (s + 1))
                    for h in range(2):
                        r = ada_rows(s)
                        for part in range(0, r, 2):
                            last = pe.matmul(pair(3)[:, TS + 4 * s + 2 * h:TS + 4 * s + 2 * h + 2], ROW[s % 2][0:r, h * P:(h + 1) * P],
                                             IDENT[0:r, part:part + 2], start=part == 0, stop=part == r - 2)
                    last.then_inc(ada_done, 1)

                def mean_square(which):
                    if which:
                        wait_taken(pe, l, G_OUT + 6)
                    for k in range(KT):
                        pe.wait_ge(sq_ready, l * 16 + (8 * which + k + 1))
                        wide(pair(2), ONES, SQ[k % 2], k == 0, k == KT - 1).then_inc(ms_ready, 1)

                mean_square(0)
                pe.wait_ge(cond_ready, l + 1)
                for s in range(N_ADA1):
                    ada(s)
                    if s:
                        ada_turn(s - 1)
                ada_turn(N_ADA1 - 1)
                def head_mean_square(i):
                    pe.wait_ge(qk_sq, l * NQK + (i + 1))
                    if i:
                        pe.wait_ge(qk_rstd, l * NQK + i)
                    wide(pair(2), BLK64 if QK_TILES[i][2] == 64 else BLK32, SQ[i % 2], True, True).then_inc(qk_ms, 1)

                def rotate(i):
                    t, _, hd = QK_TILES[i]
                    pe.wait_ge(qk_normed, l * NQK + (i + 1))
                    if i:
                        pe.wait_ge(qk_done, l * NQK + i)
                    pe.matmul(pair(3)[:, 0:TS], ROTA if hd == 64 else ROTC, ZT[:, t, 0:TS], start=True, stop=True).then_inc(qk_rot, 1)

                def decay(d):
                    if d:
                        pe.wait_ge(al_lin, l * 2 + 1)
                    else:
                        pe.wait_ge(qk_rstd, l * NQK + NQK)
                        wait_taken(pe, l, z_index(DR))
                    wide(pair(2), WAL[:, d, :], ZT[0:32, DR, :], True, True).then_inc(al_full, 1)

                for n, (c, kind, dst, j) in enumerate(ZT_TILES):
                    chunk(CHUNK_Z[c])
                    fresh = n == 0 or ZT_TILES[n - 1][0] != c
                    if n == 1:
                        pe.wait_ge(landed_q, l * 32 + 32)
                    wait_room(pe, l, n)
                    out = pair(use(n)[0])
                    if kind == "tm":
                        w = weights(CHUNK_Z[c], 256)
                        for i in range(3 * j, 3 if j == 0 else NT):
                            for k in range(KT):
                                last = pe.matmul(out[:, (i - 3 * j) * 256:(i - 3 * j + 1) * 256], HT[:, k, i * P:(i + 1) * P],
                                                 w[:, k, :], start=k == 0, stop=k == KT - 1)
                                release(last, fresh and i == 0 and k == 0)
                    elif kind == "tm1":
                        w = weights(CHUNK_Z[c], 256)
                        for i in range(NT):
                            for k in range(KT):
                                last = pe.matmul(out[:, i * P:(i + 1) * P], HT[:, k, i * P:(i + 1) * P],
                                                 w[:, k, P:2 * P], start=k == 0, stop=k == KT - 1)
                    elif kind == "r":
                        w = weights(CHUNK_Z[c], 32)
                        for k in range(KT):
                            last = wide(out[0:32], w[:, k, :], HT[:, k, :], k == 0, k == KT - 1, k == 0)
                    else:
                        w = weights(CHUNK_Z[c], 256)
                        for k in range(KT):
                            if n == 0:
                                pe.wait_ge(h_ready, l * 16 + (k + 1))
                            last = wide(out, w[:, k, j * P:(j + 1) * P], HT[:, k, :], k == 0, k == KT - 1, fresh and k == 0)
                    last.then_inc(gemm_full, 1)
                    if n < NZT - 1 and ZT_TILES[n + 1][0] == c:
                        continue
                    if 0 <= c - QK_AT - 1 < NQK:
                        head_mean_square(c - QK_AT - 1)
                    if 0 <= c - QK_AT - 2 < NQK:
                        rotate(c - QK_AT - 2)
                    if c == 12:
                        decay(0)
                    if c:
                        ada_turn(N_ADA1 + c - 1)
                    ada(N_ADA1 + c)
                ada_turn(N_ADA1 + 13)
                decay(1)
                for s in range(N_ADA1 + 14, N_ADA):
                    ada(s)
                    ada_turn(s)
                pe.wait_ge(al_lin, l * 2 + 2)
                pe.wait_ge(mod_ready, l * 2 + 2)
                pe.wait_ge(qk_done, l * NQK + NQK)
                wait_taken(pe, l, NZT - 1)
                wait_taken(pe, l, NZT - 2)

                def scores(g):
                    i, u = divmod(g, NU)
                    q, r0, rows, k, kc = ATT[u][:5]
                    if g >= 2:
                        pe.wait_ge(p_ready, l * NG + (g - 1))
                    out = pair(1 + g % 2)
                    qs = ZT[r0:r0 + rows, q, i * P:(i + 1) * P]
                    if i < NT - 1:
                        pe.matmul(out[:, 0:TS], qs, ZT[r0:r0 + rows, k, 0:TS], start=True, stop=True)
                        last = pe.matmul(out[:, TS:TS + PAST], qs, KTC[r0:r0 + rows, kc, :], start=True, stop=True)
                    else:
                        last = pe.matmul(out[:, 0:P], qs, ZT[r0:r0 + rows, k, TS:T], start=True, stop=True)
                    last.then_inc(s_full, 1)

                def turn(g):
                    i, u = divmod(g, NU)
                    pe.wait_ge(normed_p, l * NG + (g + 1))
                    if g:
                        pe.wait_ge(pt_kept, l * NG + g)
                    for k in range(keys(i)):
                        last = pe.transpose(pair(3)[:, k * P:(k + 1) * P], PROB[g % 2][:, k * P:(k + 1) * P], IDENT)
                    last.then_inc(pt_full, 1)

                def weigh(g):
                    i, u = divmod(g, NU)
                    v, tile, o0, m = ATT[u][5:]
                    pe.wait_ge(pt_kept, l * NG + (g + 1))
                    if u == 0 and i >= 2:
                        pe.wait_ge(o_taken, l * NT + (i - 1))
                    out = pair(0)[o0:o0 + 64, i % 2 * TS + tile * P:i % 2 * TS + (tile + 1) * P]
                    for k in range(keys(i)):
                        vals = V[:, NT - 1, v:v + 64] if i == NT - 1 else V[:, k, v:v + 64] if k < 4 else VC[:, k - 4, v:v + 64]
                        last = pe.matmul(out, vals, PROBT[g % 2][:, k * P:(k + 1) * P], start=k == 0 and m != 1, stop=k == keys(i) - 1 and m != 0)
                    last.then_inc(pv_done, 1)

                scores(0)
                scores(1)
                for g in range(NG + 1):
                    if g + 2 < NG:
                        scores(g + 2)
                    if g < NG:
                        turn(g)
                    if g:
                        weigh(g - 1)

                def mean_square_c(j):
                    pe.wait_ge(csq_ready, l * 2 + (j + 1))
                    if j:
                        pe.wait_ge(crstd_ready, l * 2 + j)
                    wide(pair(0), BLK64, YSQ, True, True).then_inc(cms_ready, 1)

                pe.wait_ge(al_ready, l * 2 + 2)
                cnt = 0

                def group_room(cnt):
                    if cnt >= 2:
                        pe.wait_ge(sc_kept, l * NSC + (cnt - 1))
                    return pair(2 + cnt % 2)

                def go_pair(grp):
                    return pair(1 + grp)

                def mean_square_g(x):
                    for grp in range(GLA[x][6]):
                        g0 = sum(g[6] for g in GLA[:x]) + grp
                        pe.wait_ge(go_sq, l * NGRP + (g0 + 1))
                        if g0:
                            pe.wait_ge(go_rstd, l * NGRP + g0)
                        wide(pair(0), BLK64, YSQ, True, True).then_inc(go_ms, 1)

                for x, (q, _, a, gate, vb, rows, groups, _) in enumerate(GLA):
                    before = sum(g[6] for g in GLA[:x])
                    for p in range(NPASS):
                        pe.wait_ge(lvl_ready, l * 3 * NPASS + (x * NPASS + p + 1))
                        for h in range(2 * groups):
                            out = group_room(cnt)
                            cnt += 1
                            r = slice(h * rows, (h + 1) * rows)
                            for i in range(NT):
                                ti = slice(i * P, (i + 1) * P)
                                if p == 0:
                                    last = pe.matmul(out[:, ti], KO[r, 0, ti], ZT[r, q, ti], start=True, stop=True)
                                else:
                                    last = pe.matmul(out[:, ti], KM[p % 2][r, ti], QM[p % 2][r, ti], start=True, stop=True)
                            last.then_inc(sc_full, 1)
                        if x == 0 and p in (1, 3):
                            mean_square_c(p // 2)
                        if x and p == 1:
                            mean_square_g(x - 1)
                    for d in range(2):
                        pe.wait_ge(ko_ready, l * 6 + (2 * x + d + 1))
                        if d == 0 and x == 0:
                            pe.wait_ge(crstd_ready, l * 2 + 2)
                        elif d == 0:
                            pe.wait_ge(go_rstd, l * NGRP + before)
                        else:
                            pe.wait_ge(ko_kept, l * 6 + (2 * x + 1))
                        for i in range(NT):
                            last = pe.transpose(pair(0)[:, i * P:(i + 1) * P], KO[:, d, i * P:(i + 1) * P], IDENT)
                        last.then_inc(ko_turned, 1)
                    for d in range(2):
                        pe.wait_ge(ko_kept, l * 6 + (2 * x + d + 1))
                        if x:
                            pe.wait_ge(gy_kept, l * NGRP + before)
                        for i in range(NT):
                            for h in range(P // rows):
                                last = pe.matmul(pair(1)[h * rows:(h + 1) * rows, d * TS + i * 64:d * TS + (i + 1) * 64],
                                                 KOT[:, d, i, h * rows:(h + 1) * rows], V[:, i, vb + 64 * h:vb + 64 * h + 64],
                                                 start=True, stop=True)
                        last.then_inc(ds_full, 1)
                    pe.wait_ge(st_ready, l * 6 + (2 * x + 2))
                    pe.wait_ge(sc_kept, l * NSC + cnt)
                    for grp in range(groups):
                        for hh in range(2):
                            h = 2 * grp + hh
                            r = slice(h * rows, (h + 1) * rows)
                            for i in range(NT):
                                ti = slice(i * P, (i + 1) * P)
                                o = go_pair(grp)[64 * hh:64 * hh + 64, ti]
                                pe.matmul(o, V[:, i, vb + 64 * h:vb + 64 * h + 64], SCORE[:, h, i, :], start=True, stop=False)
                                for d in range(2):
                                    last = pe.matmul(o, ST[r, d, x, i, :], ZT[r, a[d], ti], start=False, stop=d == 1)
                        last.then_inc(go_full, 1)
                mean_square_g(len(GLA) - 1)

                def split_product(out, i, block, b, h_hi, ready):
                    w = raw(i, block)
                    for k in range(KT):
                        ready(k)
                        hi, lo = W_HI[b][:, k, :], W_LO[b][:, k, :]
                        release(pe.matmul(out[:, 0:TS], hi, h_hi[:, k, 0:TS], start=k == 0, stop=False), block == 0 and k == 0)
                        pe.matmul(out[:, 0:TS], hi, H_LO[:, k, :], start=False, stop=False)
                        pe.matmul(out[:, 0:TS], lo, h_hi[:, k, 0:TS], start=False, stop=k == KT - 1)
                        last = pe.matmul(out[:, TS:T], w[:, k, :], HT[:, k, TS:T], start=k == 0, stop=k == KT - 1)
                    last.then_inc(gemm_full, 1)

                with pe.Fori(0, KT) as it:
                    pe.wait_ge(gy_kept, l * NGRP + NGRP)
                    for n in range(4):
                        chunk(C_MIX + n, it)
                        w = RING[:, (C_MIX + n) % 4, 0:1280].rearrange("p (k n) -> p k n", n=P)
                        g = G_MIX + 2 * n
                        wait_room(pe, l, g, it * 2)
                        pe.wait_ge(lo_made, l * N_SPLIT + it * 4 + (n + 1))

                        def ready(k):
                            if n == 0:
                                pe.wait_ge(gate_h, l * KT + (k + 1))

                        split_product(pair(use(g)[0]), C_MIX + n, 0, n % 2, H_HI, ready)
                        wait_room(pe, l, g + 1, it * 2)
                        for k in range(2):
                            last = wide(pair(use(g + 1)[0]), w[:, KT + k, :], ZT[:, 2 * n + k, :], k == 0, k == 1)
                        last.then_inc(gemm_full, 1)
                pe.wait_ge(mix_done, l * KT + KT)
                for c in range(4):
                    chunk(C_OUT + c)
                    w = weights(C_OUT + c, 256)
                    for h in range(2):
                        g = G_OUT + 2 * c + h
                        wait_room(pe, l, g)
                        for k in range(KT):
                            last = wide(pair(use(g)[0]), w[:, k, h * P:(h + 1) * P], ZT[:, MIXT + k, :], k == 0, k == KT - 1, h == 0 and k == 0)
                        last.then_inc(gemm_full, 1)
                mean_square(1)

                def up(j, turns):
                    chunk(C_UP + j, turns)
                    for h in range(2):
                        g = G_UP + 2 * j + h
                        wait_room(pe, l, g, turns * 2)
                        pe.wait_ge(lo_made, l * N_SPLIT + turns * 8 + (N_SPLIT_MIX + 2 * j + h + 1))

                        def ready(k):
                            if j == 0 and h == 0:
                                pe.wait_ge(h_ready, l * 16 + (8 + k + 1))

                        split_product(pair(use(g)[0]), C_UP + j, h, h, HT_R, ready)

                with pe.Fori(0, 5) as it:
                    for j in range(4):
                        up(j, it)
                for j in range(20, 22):
                    up(j, 0)
                with pe.Fori(0, 2) as it:
                    for j in range(4):
                        g = G_DOWN + j
                        wait_room(pe, l, g, it)
                        for h in range(2):
                            i = C_DOWN + 2 * j + h
                            chunk(i, it * 2)
                            pe.wait_ge(lo_made, l * N_SPLIT + it * 8 + (N_SPLIT_UP + 2 * j + h + 1))
                            out = pair(use(g)[0])
                            for k in range(11):
                                f = 11 * h + k
                                if j == 0:
                                    pe.wait_ge(d_ready, l * FT + (f + 1))
                                kn = slice(k * P, (k + 1) * P)
                                first, end = f == 0, f == FT - 1
                                release(pe.matmul(out[:, 0:TS], DW_HI[h][:, kn], D_HI[f], start=first, stop=False), k == 0)
                                pe.matmul(out[:, 0:TS], DW_HI[h][:, kn], ZT_R[:, f, 0:TS], start=False, stop=False)
                                pe.matmul(out[:, 0:TS], DW_LO[h][:, kn], D_HI[f], start=False, stop=end)
                                last = pe.matmul(out[:, TS:T], RING[:, i % N_SLOT, kn], ZT[:, f, TS:T], start=first, stop=end)
                            last.then_inc(gemm_full if h else dw_used, 1)

        @block.scalar
        def _(act):
            step = act_chain
            act.dma_start(MASK_IN, A["mask"]).then_inc(mask_in, 16)
            act.wait_ge(eps_set, 1)
            act.wait_ge(zero_set, 1)
            with act.Fori(0, DEPTH) as l:
                step.layer(l)
                at = bass.ds(l, 1)
                act.wait_ge(layer_done, l)
                act.wait_ge(states_stored, l * 16)
                act.dma_start(COLS[:], A["cols"][at].rearrange("l p n -> p (l n)")).then_inc(params_in, 16)
                act.dma_start(WAL[:], A["w_alpha"][at].rearrange("l p d n -> p (l d) n")).then_inc(params_in, 16)
                act.dma_start(KTC, A["keysT"][at].rearrange("l p a n -> p (l a) n")).then_inc(params_in, 16)
                act.dma_start(VC, A["vals"][at].rearrange("l (t p) n -> p (l t) n", p=P)).then_inc(params_in, 16)
                for d in range(2):
                    first = 0 if d == 0 else TS // P - 1
                    act.dma_start(ST[:, d, 0:2, first, :], A["hgrn"][at, :, d].rearrange("l p u v -> p (l u) v")).then_inc(params_in, 16)
                    act.dma_start(ST[:, d, 2:3, first, :], A["gla"][at, :, d:d + 1].rearrange("l p u v -> p (l u) v")).then_inc(params_in, 16)
                act.wait_ge(x_in, 16)

                def inv_root(out, src, scale=1.0):
                    step.mark(act.activation(out, src, ACT.Ln, bias=EPSC[:, 0:1], scale=scale))
                    step.settle(act)
                    return act.activation(out, out, ACT.Exp, scale=-0.5)

                def squares(which):
                    for k in range(KT):
                        if k >= 2:
                            act.wait_ge(ms_ready, l * 16 + (8 * which + k - 1))
                        if which:
                            wait_taken(act, l, G_OUT + k)
                        act.activation(SQ[k % 2], XT[:, k, :], ACT.Square).then_inc(sq_ready, 1)
                    act.wait_ge(ms_ready, l * 16 + (8 * which + 8))
                    inv_root(RSTD[0], pair(2)[:, 0:T]).then_inc(rstd_ready, 1)

                squares(0)
                act.wait_ge(params_in, l * N_PARAM + N_PARAM)
                act.activation(SG[:].rearrange("p a b -> p (a b)"), COLS[:, C_COND:C_COND + 16], ACT.Sigmoid).then_inc(cond_sig, 1)
                act.wait_ge(lb_shift, l + 1)
                act.activation(LBE[:].rearrange("p a b c -> p (a b c)"), LBE[:].rearrange("p a b c -> p (a b c)"), ACT.Exp).then_inc(lb_exp, 1)
                act.wait_ge(lam_sum, l + 1)
                act.activation(LMS[:], LMS[:], ACT.Exp).then_inc(lam_exp, 1)

                def ada_row_out(s):
                    act.wait_ge(ada_row, l * N_ADA + (s + 1))
                    if s >= 2:
                        act.wait_ge(ada_done, l * N_ADA + (s - 1))
                    act.activation(ROW[s % 2][0:ada_rows(s)], ada_out(s), ACT.Copy).then_inc(row_kept, 1)

                def ada_split_hi(s):
                    i = CHUNK_ADA[s]
                    act.wait_ge(landed[i % N_SLOT], l * (32 * CHUNKS // N_SLOT) + 32 * (i // N_SLOT + 1))
                    for h in range(2):
                        act.activation(ADA_HI[h], RING[:, i % N_SLOT, 1024 * h:1024 * h + 1024], ACT.Copy).then_inc(ada_hi, 1)

                for s in range(N_ADA1):
                    ada_row_out(s)
                def head_square(i):
                    wait_taken(act, l, z_index(QK_TILES[i][0]))
                    if i >= 2:
                        act.wait_ge(qk_ms, l * NQK + (i - 1))
                    act.activation(SQ[i % 2], ZT[:, QK_TILES[i][0], :], ACT.Square).then_inc(qk_sq, 1)

                def head_inv_root(i):
                    act.wait_ge(qk_ms, l * NQK + (i + 1))
                    if i >= 2:
                        act.wait_ge(qk_normed, l * NQK + (i - 1))
                    inv_root(RSTD[i % 2], pair(2)[:, 0:T]).then_inc(qk_rstd, 1)

                for n, (c, kind, dst, j) in enumerate(ZT_TILES):
                    if n == 0 or ZT_TILES[n - 1][0] != c:
                        ada_split_hi(N_ADA1 + c)
                    wait_full(act, l, n)
                    p = use(n)[0]
                    src = pair(p)[:, 0:T]
                    if kind == "tm":
                        m = 3 - j
                        act.activation(V[:, 3 * j:3 * j + m, dst:dst + 256], pair(p)[:, 0:256 * m].rearrange("p (i n) -> p i n", n=256),
                                       ACT.Copy).then_inc(gemm_free[p], 1)
                    elif kind == "tm1":
                        act.activation(V[:, :, dst:dst + P], src.rearrange("p (i n) -> p i n", n=P), ACT.Copy).then_inc(gemm_free[p], 1)
                    elif kind == "r":
                        act.activation(ZT[0:32, dst, :], src[0:32], ACT.Copy).then_inc(gemm_free[p], 1)
                    elif kind == "silu":
                        act.activation(ZT[:, dst, :], src, ACT.Sigmoid).then_inc(silu_sig, 1)
                    elif kind == "ff":
                        step.mark(act.activation(ZT[:, dst, :], src, ACT.Sigmoid))
                        act.activation(ZT[:, dst + BKF - BFF, :], src, ACT.Sigmoid, scale=-1.0).then_inc(gemm_free[p], 1)
                    elif kind == "dqk" and j == 0:
                        act.activation(ZT[:, dst, :], src, ACT.Copy, scale=32 ** -0.5).then_inc(gemm_free[p], 1)
                    else:
                        act.activation(ZT[:, dst, :], src, ACT.Copy).then_inc(gemm_free[p], 1)
                    if n < NZT - 1 and ZT_TILES[n + 1][0] == c:
                        continue
                    if 0 <= c - QK_AT - 1 < NQK:
                        head_inv_root(c - QK_AT - 1)
                    if 0 <= c - QK_AT < NQK:
                        head_square(c - QK_AT)
                    ada_row_out(N_ADA1 + c)
                act.wait_ge(qk_done, l * NQK + NQK)
                for d in range(2):
                    act.wait_ge(al_full, l * 2 + (d + 1))
                    step.mark(act.activation(TMP[d], pair(2)[:, 0:T], ACT.Identity, bias=COLS[:, C_AB + d:C_AB + d + 1]))
                    act.activation(SQ[d], pair(2)[:, 0:T], ACT.Abs, bias=COLS[:, C_AB + d:C_AB + d + 1]).then_inc(al_lin, 1)
                act.wait_ge(al_lin, l * 2 + 2)
                for d in range(2):
                    step.mark(act.activation(SQ[d], SQ[d], ACT.Exp, scale=-1.0))
                ada_row_out(N_ADA - 2)
                step.settle(act)
                for d in range(2):
                    act.activation(SQ[d], SQ[d], ACT.Ln, bias=1.0).then_inc(al_log, 1)
                ada_row_out(N_ADA - 1)
                act.dma_start(O["keysT"][at].rearrange("l p a t -> p (l a) t"), ZT[:, AK:AK + 3, TS:T]).then_inc(stored, 16)
                act.dma_start(O["vals"][at].rearrange("l p n -> p (l n)"), V[:, NT - 1, 0:V_B]).then_inc(stored, 16)
                for d in range(2):
                    act.wait_ge(al_cut, l * 2 + (d + 1))
                    act.activation(ZT[:, (DAF, DAB)[d], :], TMP[d], ACT.Exp, scale=1.0 / 16).then_inc(al_ready, 1)

                def exponentials(g):
                    i, u = divmod(g, NU)
                    n = keys(i) * P
                    act.wait_ge(nmax_ready, l * NG + (g + 1))
                    act.activation(PROB[g % 2][:, 0:n], pair(1 + g % 2)[:, 0:n], ACT.Exp, bias=NMX[:, g % 2:g % 2 + 1],
                                   accum_out=SUMS[:, g % 2:g % 2 + 1]).then_inc(p_ready, 1)

                act.wait_ge(al_ready, l * 2 + 2)
                exponentials(0)
                exponentials(1)
                for g in range(NG):
                    n = keys(g // NU) * P
                    act.wait_ge(pt_full, l * NG + (g + 1))
                    if g >= 2:
                        act.wait_ge(pv_done, l * NG + (g - 1))
                    act.activation(PROBT[g % 2][:, 0:n], pair(3)[:, 0:n], ACT.Copy).then_inc(pt_kept, 1)
                    if g + 2 < NG:
                        exponentials(g + 2)
                act.wait_ge(o_taken, l * NT + NT)
                for j in range(2):
                    if j:
                        act.wait_ge(cms_ready, l * 2 + j)
                    act.activation(YSQ, ZT[:, CQ + j, :], ACT.Square).then_inc(csq_ready, 1)
                    act.wait_ge(cms_ready, l * 2 + (j + 1))
                    if j:
                        act.wait_ge(yc_done, l * 2 + j)
                    inv_root(YRSTD, pair(0)[:, 0:T]).then_inc(crstd_ready, 1)
                act.wait_ge(yc_done, l * 2 + 2)

                for x, g in enumerate(GLA):
                    before = sum(y[6] for y in GLA[:x])
                    for d in range(2):
                        act.wait_ge(ko_turned, l * 6 + (2 * x + d + 1))
                        if x and d == 0:
                            act.wait_ge(gy_kept, l * NGRP + before)
                        act.activation(KOT[:, d].rearrange("p i n -> p (i n)"), pair(0)[:, 0:T], ACT.Copy).then_inc(ko_kept, 1)
                    for grp in range(g[6]):
                        g0 = before + grp
                        act.wait_ge(go_full, l * NGRP + (g0 + 1))
                        if grp:
                            act.wait_ge(go_ms, l * NGRP + g0)
                        act.activation(YSQ, pair(1 + grp)[:, 0:T], ACT.Square).then_inc(go_sq, 1)
                        act.wait_ge(go_ms, l * NGRP + (g0 + 1))
                        if grp:
                            act.wait_ge(gy_kept, l * NGRP + g0)
                        inv_root(YRSTD, pair(0)[:, 0:T]).then_inc(go_rstd, 1)

                act.wait_ge(st_ready, l * 6 + 6)
                act.dma_start(O["fin"][at].rearrange("l p n -> p (l n)"), FIN[:].rearrange("p a b c -> p (a b c)")).then_inc(states_stored, 16)
                def split_hi(i, block, b, turns=0):
                    act.wait_ge(landed[i % N_SLOT], l * (32 * CHUNKS // N_SLOT) + turns * 32 + 32 * (i // N_SLOT + 1))
                    act.activation(W_HI[b], raw(i, block), ACT.Copy).then_inc(hi_made, 1)

                act.wait_ge(gy_kept, l * NGRP + NGRP)
                split_hi(C_MIX, 0, 0)
                for k in range(KT):
                    act.activation(H_HI[:, k, :], HT[:, k, 0:TS], ACT.Copy).then_inc(gate_hi, 1)
                split_hi(C_MIX + 1, 0, 1)

                def gates(it, last):
                    for n in range(4):
                        g = G_MIX + 2 * n
                        wait_full(act, l, g, it * 8)
                        wait_room(act, l, g + 1, it * 2)
                        act.activation(SQ[n % 2], pair(use(g)[0])[:, 0:T], ACT.Sigmoid).then_inc(gemm_free[use(g)[0]], 1)
                        if n < 2 or not last:
                            split_hi(C_MIX + n + 2, 0, n % 2, it)

                with act.Fori(0, KT - 1) as it:
                    gates(it, False)
                gates(KT - 1, True)
                for h in range(2):
                    split_hi(C_UP, h, h)
                squares(1)
                for k in range(KT):
                    act.wait_ge(norm_hi_in, l * KT + (k + 1))
                    act.activation(HT_R[:, k, 0:TS], SQ[k % 2][:, 0:TS], ACT.Copy).then_inc(norm_hi, 1)

                def ffn(j, turns):
                    f = turns * 4 + j
                    for h in range(2):
                        g = G_UP + 2 * j + h
                        wait_full(act, l, g, turns * 8)
                        if h == 0:
                            act.wait_ge(act_done, l * FT + f + 1)
                        col = f + h * FT
                        act.activation(FB[j % 2][h], pair(use(g)[0])[:, 0:T], ACT.Identity,
                                       bias=COLS[:, bass.ds(col + C_CB, 1)], scale=COLS[:, bass.ds(col + C_W1, 1)]).then_inc(centre_ready, 1)
                        if j < FT - 1:
                            split_hi(C_UP + j + 1, h, h, turns)
                    wait_taken(act, l, g, turns * 2)
                    act.activation(FB[j % 2][1], FB[j % 2][1], ACT.Silu).then_inc(g_silu, 1)

                with act.Fori(0, 5) as it:
                    for j in range(4):
                        ffn(j, it)
                for j in range(20, 22):
                    ffn(j, 0)

                def down_hi(q):
                    i = C_DOWN + q
                    act.wait_ge(landed[i % N_SLOT], l * (32 * CHUNKS // N_SLOT) + 32 * (i // N_SLOT + 1))
                    act.activation(DW_HI[q % 2], RING[:, i % N_SLOT, 0:11 * P], ACT.Copy).then_inc(hi_made, 1)

                def activation_hi(f):
                    act.wait_ge(act_done, l * FT + (f + 3))
                    act.activation(D_HI[f], ZT[:, f, 0:TS], ACT.Copy).then_inc(d_hi, 1)

                down_hi(0)
                for f in range(11):
                    activation_hi(f)
                act.wait_ge(act_done, l * FT + (FT + 2))
                down_hi(1)
                for f in range(11, FT):
                    activation_hi(f)
                for j in range(KT - 1):
                    act.wait_ge(dw_used, l * KT + (j + 1))
                    down_hi(2 * j + 2)
                    wait_full(act, l, G_DOWN + j)
                    down_hi(2 * j + 3)
                step.end(act)
            act.wait_ge(stored, DEPTH * N_STORE)
            act.wait_ge(states_stored, DEPTH * 16)

        @block.vector
        def _(v):
            step = dve_chain
            nv = nc.vector
            nv.memset(EPSC[:], EPS).then_inc(eps_set, 1)
            v.wait_ge(mask_in, 16)
            nv.tensor_copy(MASK[:].rearrange("p a b -> p (a b)"), MASK_IN).then_inc(mask_set, 1)
            v.wait_ge(mask_set, 1)
            v.wait_ge(x_in, 16)
            v.wait_ge(consts_in, 16)
            v.sem_inc(act_done, 2)
            with v.Fori(0, DEPTH) as l:
                step.layer(l)

                def link(ins):
                    step.mark(ins)
                    step.settle(v)

                def bc(ap, n):
                    return ap.to_broadcast(list(ap.shape[:-1]) + [n])

                v.wait_ge(params_in, l * N_PARAM + N_PARAM)
                lbl = COLS[:, C_LB:C_LB + 8].rearrange("p (d l t) -> p d l t", d=2, l=2)
                link(nv.tensor_tensor(LBM[:], lbl[:, :, 0, :], lbl[:, :, 1, :], ALU.max))
                step.mark(nv.tensor_tensor(LBE[:, :, 0, :], lbl[:, :, 0, :], LBM[:], ALU.subtract))
                nv.tensor_tensor(LBE[:, :, 1, :], lbl[:, :, 1, :], LBM[:], ALU.subtract).then_inc(lb_shift, 1)
                lam = COLS[:, C_LAM:C_LAM + 128].rearrange("p (a b n) -> p a b n", a=2, b=2)
                link(nv.tensor_tensor(LPR, lam[:, :, 0, :], lam[:, :, 1, :], ALU.mult))
                nv.tensor_reduce(LMS[:], LPR, AX.X, ALU.add).then_inc(lam_sum, 1)
                v.wait_ge(cond_sig, l + 1)
                nv.tensor_tensor(SC[:].rearrange("p k g -> p g k"), COLS[:, C_COND:C_COND + 16].rearrange("p (g k) -> p g k", g=2),
                                 SG[:], ALU.mult).then_inc(cond_ready, 1)
                v.wait_ge(cond_ready, l + 1)
                link(nv.tensor_copy(SC4[:, :, 0:2], SC[:]))
                step.mark(nv.tensor_tensor(SC4[:, :, 2:4], SC[:], as_f32(SC4[:, :, 0:2]), ALU.subtract))
                v.wait_ge(lb_exp, l + 1)
                link(nv.tensor_tensor(LBM[:], LBE[:, :, 0, :], LBE[:, :, 1, :], ALU.add))
                link(nv.reciprocal(LBM[:], LBM[:]))
                link(nv.tensor_tensor(LBM[:], LBM[:], LBE[:, :, 1, :], ALU.mult))
                link(nv.tensor_scalar(LBM[:], LBM[:], COLS[:, C_LC + 2:C_LC + 3], None, ALU.mult))
                step.mark(nv.tensor_scalar(LBF[:], LBM[:], LB_FLOOR, None, ALU.max))
                step.mark(nv.tensor_scalar(OML[:], LBM[:], -1.0, 1.0, ALU.mult, ALU.add))
                v.wait_ge(lam_exp, l + 1)
                link(nv.tensor_tensor(NLAM[:], LMS[:, 1:2], LMS[:, 0:1], ALU.subtract))
                step.mark(nv.tensor_tensor(NLAM[:], NLAM[:], COLS[:, C_LC:C_LC + 1], ALU.subtract))
                step.mark(nv.tensor_scalar(QG[:, 0:1], COLS[:, C_AQ:C_AQ + 1], 64 ** -0.5, None, ALU.mult))
                step.mark(nv.tensor_scalar(QG[:, 1:2], COLS[:, C_CQ:C_CQ + 1], 32 ** -0.5, None, ALU.mult))
                step.mark(nv.tensor_tensor(SUBG[:], COLS[:, C_SUB:C_SUB + 1], COLS[:, C_LC + 1:C_LC + 2], ALU.mult))

                def modulation(which, a, b):
                    v.wait_ge(ada_done, l * N_ADA + (N_ADA1, N_ADA)[which])
                    ps = pair(3)[:, TS + 2 * a:TS + 2 * b].rearrange("p (j g) -> p j g", g=2)
                    link(nv.tensor_tensor(MOD[:, a:b, :], ps, bc(COLS[:, C_BADA + a:C_BADA + b].rearrange("p (j o) -> p j o", o=1), 2), ALU.add))
                    scale, dst, gain = (MOD[:, 8:16, :], A1, C_N1) if which == 0 else (MOD[:, 32:40, :], A2, C_N2)
                    g = COLS[:, gain:gain + KT].rearrange("p (j o) -> p j o", o=1)
                    nv.scalar_tensor_tensor(out=dst[:], in0=scale, scalar=1.0, in1=bc(g, 2), op0=ALU.add, op1=ALU.mult).then_inc(mod_ready, 1)
                    v.wait_ge(mod_ready, l * 2 + (which + 1))

                def normed(which, gain, shift):
                    v.wait_ge(rstd_ready, l * 2 + (which + 1))

                    def rest(k):
                        v.wait_ge(norm_hi, l * KT + (k + 1))
                        nv.tensor_tensor(H_LO[:, k, :], SQ[k % 2][:, 0:TS], as_f32(HT_R[:, k, 0:TS]), ALU.subtract).then_inc(h_ready, 1)

                    for k in range(KT):
                        x = SQ[k % 2] if which else TMP[k % 2]
                        if which and k >= 2:
                            v.wait_ge(h_ready, l * 16 + (KT + k - 1))
                        link(nv.tensor_tensor(x, XT[:, k, :], RSTD[0], ALU.mult))
                        for g, (a, b) in reversed(list(enumerate(SEG))):
                            out = x[:, a:b] if which and g == 0 else HT[:, k, a:b]
                            last = nv.tensor_scalar(out, x[:, a:b], gain[:, k, g:g + 1], MOD[:, shift + k, g:g + 1], ALU.mult, ALU.add)
                            if g:
                                step.mark(last)
                        last.then_inc(norm_hi_in if which else h_ready, 1)
                        if which and k:
                            rest(k - 1)
                    if which:
                        rest(KT - 1)

                modulation(0, 0, 16)
                normed(0, A1, 0)

                def head_norm(i):
                    t, col, hd = QK_TILES[i]
                    gain = {C_AQ: QG[:, 0:1], C_CQ: QG[:, 1:2]}.get(col, COLS[:, col:col + 1])
                    v.wait_ge(qk_rstd, l * NQK + (i + 1))
                    nv.scalar_tensor_tensor(out=ZT[:, t, :], in0=ZT[:, t, :], scalar=gain, in1=RSTD[i % 2],
                                            op0=ALU.mult, op1=ALU.mult).then_inc(qk_normed, 1)
                    v.wait_ge(qk_normed, l * NQK + (i + 1))
                    step.mark(nv.tensor_tensor(TMP[0][:, 0:TS], ZT[:, t, 0:TS], cosA if hd == 64 else cosC, ALU.mult))

                def head_rotary(i):
                    t, _, hd = QK_TILES[i]
                    v.wait_ge(qk_rot, l * NQK + (i + 1))
                    link(nv.tensor_tensor(TMP[1][:, 0:TS], pair(3)[:, 0:TS], sinA if hd == 64 else sinC, ALU.mult))
                    nv.tensor_tensor(ZT[:, t, 0:TS], TMP[0][:, 0:TS], TMP[1][:, 0:TS], ALU.add).then_inc(qk_done, 1)

                def ada_split_lo(s):
                    for h in range(2):
                        v.wait_ge(ada_hi, l * 2 * len(ADA_SPLIT) + (2 * (s - N_ADA1) + h + 1))
                        part = slice(1024 * h, 1024 * h + 1024)
                        i = CHUNK_ADA[s] % N_SLOT
                        nv.tensor_tensor(RING_R[:, i, part], RING[:, i, part], as_f32(ADA_HI[h]), ALU.subtract).then_inc(ada_lo, 1)

                sig = 0
                for n, (c, kind, dst, j) in enumerate(ZT_TILES):
                    if n == 0 or ZT_TILES[n - 1][0] != c:
                        ada_split_lo(N_ADA1 + c)
                    if kind == "silu":
                        sig += 1
                        v.wait_ge(silu_sig, l * 6 + sig)
                        p = use(n)[0]
                        nv.tensor_tensor(ZT[:, dst, :], ZT[:, dst, :], pair(p)[:, 0:T], ALU.mult).then_inc(gemm_free[p], 1)
                    if kind == "ff":
                        d = (dst - BFF) // 2
                        wait_taken(v, l, n)
                        step.mark(nv.tensor_scalar(ZT[:, dst, :], ZT[:, dst, :], OML[:, d, j:j + 1], LBF[:, d, j:j + 1], ALU.mult, ALU.add))
                        nv.tensor_scalar(ZT[:, dst + BKF - BFF, :], ZT[:, dst + BKF - BFF, :], OML[:, d, j:j + 1], None, ALU.mult).then_inc(gla_in, 1)
                    if n < NZT - 1 and ZT_TILES[n + 1][0] == c:
                        continue
                    if 0 <= c - QK_AT - 2 < NQK:
                        head_rotary(c - QK_AT - 2)
                    if 0 <= c - QK_AT - 1 < NQK:
                        head_norm(c - QK_AT - 1)
                modulation(1, 16, 48)

                for d in range(2):
                    v.wait_ge(al_log, l * 2 + (d + 1))
                    nv.scalar_tensor_tensor(out=TMP[d], in0=TMP[d], scalar=0.0, in1=SQ[d], op0=ALU.min, op1=ALU.subtract).then_inc(al_cut, 1)

                def maxima(g):
                    v.wait_ge(s_full, l * NG + (g + 1))
                    nv.tensor_reduce(NMX[:, g % 2:g % 2 + 1], pair(1 + g % 2)[:, 0:keys(g // NU) * P], AX.X, ALU.max,
                                     negate=True).then_inc(nmax_ready, 1)

                def normalise(g):
                    i, u = divmod(g, NU)
                    p = PROB[g % 2][:, 0:keys(i) * P]
                    v.wait_ge(p_ready, l * NG + (g + 1))
                    link(nv.reciprocal(RCP[:, g % 2:g % 2 + 1], SUMS[:, g % 2:g % 2 + 1]))
                    if ATT[u][8] == 1:
                        nv.tensor_scalar(p, p, RCP[:, g % 2:g % 2 + 1], NLAM[:], ALU.mult, ALU.mult).then_inc(normed_p, 1)
                    else:
                        nv.tensor_scalar(p, p, RCP[:, g % 2:g % 2 + 1], None, ALU.mult).then_inc(normed_p, 1)

                def outputs(i):
                    v.wait_ge(pv_done, l * NG + NU * (i + 1))
                    o = pair(0)[:, i % 2 * TS:(i % 2 + 1) * TS].rearrange("p (a b t) -> p a b t", a=2, b=2)
                    step.mark(nv.tensor_copy(ZT[:, AQ:AQ + 2, i * P:(i + 1) * P], o[:, 0]))
                    nv.tensor_copy(ZT[:, CQ:CQ + 2, i * P:(i + 1) * P], o[:, 1]).then_inc(o_taken, 1)

                v.wait_ge(al_ready, l * 2 + 2)
                maxima(0)
                maxima(1)
                for g in range(NG):
                    normalise(g)
                    if g + 2 < NG:
                        maxima(g + 2)
                    if g and g % NU == 0:
                        outputs(g // NU - 1)
                outputs(NT - 1)

                def norm_c(j):
                    v.wait_ge(crstd_ready, l * 2 + (j + 1))
                    nv.scalar_tensor_tensor(out=ZT[:, CQ + j, :], in0=ZT[:, CQ + j, :], scalar=SUBG[:], in1=YRSTD,
                                            op0=ALU.mult, op1=ALU.mult).then_inc(yc_done, 1)

                v.wait_ge(gla_in, l * 4 + 4)
                cnt = 0

                def keep(h, p):
                    nonlocal cnt
                    v.wait_ge(sc_full, l * NSC + (cnt + 1))
                    ps = pair(2 + cnt % 2)[:, 0:T].rearrange("p (n t) -> p n t", n=NT)
                    if p == 0:
                        ins = nv.tensor_copy(SCORE[:, h], ps)
                    else:
                        v.sem_inc(scores_seen, 1)
                        m = MASK[:, p, :].rearrange("p (o t) -> p o t", o=1).to_broadcast([P, NT, P])
                        ins = nv.copy_predicated(SCORE[:, h], m, ps)
                    ins.then_inc(sc_kept, 1)
                    cnt += 1

                def states(x, d):
                    v.wait_ge(ds_full, l * 6 + (2 * x + d + 1))
                    ds = pair(1)[:, d * TS:d * TS + 320].rearrange("p (i n) -> p i n", n=64)
                    for i in (range(0, 3) if d == 0 else range(3, 0, -1)):
                        nxt = i + 1 if d == 0 else i - 1
                        link(nv.scalar_tensor_tensor(out=ST[:, d, x, nxt, :], in0=ST[:, d, x, i, :], scalar=DEC[:, d, i:i + 1], in1=ds[:, i, :],
                                                     op0=ALU.mult, op1=ALU.add))
                    nv.tensor_copy(FIN[:, d, x, :], ds[:, NT - 1, :]).then_inc(st_ready, 1)

                def normed_outputs(x):
                    _, _, _, gate, _, _, groups, gain = GLA[x]
                    for grp in range(groups):
                        g0 = sum(g[6] for g in GLA[:x]) + grp
                        v.wait_ge(go_rstd, l * NGRP + (g0 + 1))
                        link(nv.tensor_tensor(YRSTD, pair(1 + grp)[:, 0:T], YRSTD, ALU.mult))
                        nv.scalar_tensor_tensor(out=ZT[:, gate + grp, :], in0=YRSTD, scalar=COLS[:, gain:gain + 1],
                                                in1=ZT[:, gate + grp, :], op0=ALU.mult, op1=ALU.mult).then_inc(gy_kept, 1)

                for x, (q, ks, a, gate, vb, rows, groups, gain) in enumerate(GLA):
                    before = sum(g[6] for g in GLA[:x])
                    first = before * 2 * NPASS
                    if x:
                        v.wait_ge(ko_turned, l * 6 + 2 * x)
                    if ks[0] == ks[1]:
                        ins = nv.tensor_scalar(KO[:, 0], ZT[:, ks[0], :], 2.0, None, ALU.mult)
                    else:
                        ins = nv.tensor_tensor(KO[:, 0], ZT[:, ks[0], :], ZT[:, ks[1], :], ALU.add)
                    ins.then_inc(lvl_ready, 1)
                    link(nv.memset(SX, 1.0))
                    for m in range(LEVELS):
                        p, h = 1 + m, 1 << m

                        def half(ap, w):
                            return ap.rearrange("p (b w h) -> p b w h", w=2, h=h)[:, :, w, :]

                        def edge(d, w):
                            e = half(ZT[:, a[d], :], w)
                            return e[:, :, h - 1:h] if d == 0 else e[:, :, 0:1]

                        if p >= 3:
                            v.wait_ge(sc_full, l * NSC + (first + 2 * groups * (p - 1)))
                        for d in range(2):
                            step.mark(nv.tensor_tensor(half(KM[p % 2], d), half(ZT[:, ks[d], :], d), half(SX[:, d], d), ALU.mult))
                        for d in range(2):
                            ins = nv.tensor_tensor(half(QM[p % 2], 1 - d), half(ZT[:, q, :], 1 - d), half(ZT[:, a[d], :], 1 - d), ALU.mult)
                            if d == 0:
                                step.mark(ins)
                        ins.then_inc(lvl_ready, 1)
                        keep(0, p - 1)
                        for d in range(2):
                            step.mark(nv.tensor_tensor(half(SX[:, d], d), half(SX[:, d], d), bc(edge(d, 1 - d), h), ALU.mult))
                        keep(1, p - 1)
                        if groups == 2:
                            keep(2, p - 1)
                        step.settle(v)
                        for d in range(2):
                            R = half(ZT[:, a[d], :], 1 - d)
                            step.mark(nv.tensor_tensor(R, R, bc(edge(d, d), h), ALU.mult))
                        if groups == 2:
                            keep(3, p - 1)
                        if x == 0 and m in (2, 4):
                            norm_c(m // 2 - 1)
                        if x and m == 3:
                            normed_outputs(x - 1)
                        step.settle(v)
                    for d in range(2):
                        step.mark(nv.tensor_copy(DEC[:, d], ZT[:, a[d], :].rearrange("p (i t) -> p i t", t=P)[:, :, P - 1 if d == 0 else 0]))
                        nv.tensor_tensor(KO[:, d], ZT[:, ks[d], :], SX[:, d], ALU.mult).then_inc(ko_ready, 1)
                    step.settle(v)
                    for d in range(2):
                        step.mark(nv.tensor_tensor(ZT[:, a[d], :], ZT[:, q, :], ZT[:, a[d], :], ALU.mult))
                    for hd in range(2 * groups):
                        keep(hd, LEVELS)
                    for d in range(2):
                        states(x, d)
                normed_outputs(len(GLA) - 1)

                def split_lo(i, block, b, number):
                    v.wait_ge(hi_made, l * N_SPLIT + number)
                    nv.tensor_tensor(W_LO[b], raw(i, block), as_f32(W_HI[b]), ALU.subtract).then_inc(lo_made, 1)

                v.wait_ge(stored, l * N_STORE + N_STORE)
                split_lo(C_MIX, 0, 0, 1)
                for k in range(KT):
                    v.wait_ge(gate_hi, l * KT + (k + 1))
                    nv.tensor_tensor(H_LO[:, k, :], HT[:, k, 0:TS], as_f32(H_HI[:, k, :]), ALU.subtract).then_inc(gate_h, 1)
                split_lo(C_MIX + 1, 0, 1, 2)

                def merge(it, last):
                    for n in range(4):
                        g = G_MIX + 2 * n
                        p = use(g + 1)[0]
                        wait_taken(v, l, g, it * 2)
                        if n < 2 or not last:
                            split_lo(C_MIX + n + 2, 0, n % 2, it * 4 + (n + 3))
                        wait_full(v, l, g + 1, it * 8)
                        dst = ZT[:, bass.ds(it + MIXT, 1), :].rearrange("p a t -> p (a t)")
                        if n == 0:
                            nv.tensor_tensor(dst, SQ[0], pair(p)[:, 0:T], ALU.mult).then_inc(gemm_free[p], 1)
                            wait_taken(v, l, g + 1, it * 2)
                        else:
                            m = RSTD[n % 2]
                            nv.tensor_tensor(m, SQ[n % 2], pair(p)[:, 0:T], ALU.mult).then_inc(gemm_free[p], 1)
                            wait_taken(v, l, g + 1, it * 2)
                            link(nv.tensor_tensor(dst, dst, m, ALU.add))
                    v.sem_inc(mix_done, 1)

                with v.Fori(0, KT - 1) as it:
                    step.enter(it, 3)
                    merge(it, False)
                step.leave(KT - 1)
                merge(KT - 1, True)

                def residual(g, k, shift):
                    p = use(g)[0]
                    for s, (a, b) in enumerate(SEG):
                        x = XT[:, bass.ds(k, 1), a:b].rearrange("p a t -> p (a t)")
                        gate = MOD[:, bass.ds(k + shift, 1), s:s + 1].rearrange("p a t -> p (a t)")
                        ins = nv.scalar_tensor_tensor(out=x, in0=pair(p)[:, a:b], scalar=gate, in1=x, op0=ALU.mult, op1=ALU.add)
                        if s == 0:
                            step.mark(ins)
                    ins.then_inc(gemm_free[p], 1)

                for k in range(KT):
                    wait_full(v, l, G_OUT + k)
                    residual(G_OUT + k, k, 16)
                    if k == 4:
                        for h in range(2):
                            split_lo(C_UP, h, h, N_SPLIT_MIX + h + 1)
                wait_taken(v, l, G_OUT + KT - 2)
                wait_taken(v, l, G_OUT + KT - 1)
                normed(1, A2, 24)

                def conv(j, turns):
                    f = turns * 4 + j
                    for h in range(2):
                        g = G_UP + 2 * j + h
                        u = pair(use(g)[0])
                        c = FB[j % 2][h]
                        v.wait_ge(centre_ready, l * 44 + turns * 8 + (2 * j + h + 1))
                        col = f + h * FT
                        for s, (a, b) in enumerate(SEG):
                            step.mark(nv.scalar_tensor_tensor(out=c[:, a + 1:b], in0=u[:, a:b - 1], scalar=COLS[:, bass.ds(col + C_W0, 1)],
                                                              in1=c[:, a + 1:b], op0=ALU.mult, op1=ALU.add))
                        step.settle(v)
                        for s, (a, b) in enumerate(SEG):
                            ins = nv.scalar_tensor_tensor(out=c[:, a:b - 1], in0=u[:, a + 1:b], scalar=COLS[:, bass.ds(col + C_W2, 1)],
                                                          in1=c[:, a:b - 1], op0=ALU.mult, op1=ALU.add)
                            if s == 0:
                                step.mark(ins)
                        ins.then_inc(gemm_free[use(g)[0]], 1)
                        if j < FT - 1:
                            split_lo(C_UP + j + 1, h, h, turns * 8 + (N_SPLIT_MIX + 2 * j + h + 3))
                    v.wait_ge(g_silu, l * FT + f + 1)
                    nv.tensor_tensor(ZT[:, bass.ds(f, 1), :].rearrange("p a t -> p (a t)"), FB[j % 2][0], FB[j % 2][1], ALU.mult).then_inc(act_done, 1)

                with v.Fori(0, 5) as it:
                    step.enter(it, 24)
                    for j in range(4):
                        conv(j, it)
                step.leave(5)
                for j in range(20, 22):
                    conv(j, 0)
                def down_lo(q):
                    v.wait_ge(hi_made, l * N_SPLIT + (N_SPLIT_UP + q + 1))
                    nv.tensor_tensor(DW_LO[q % 2], RING[:, (C_DOWN + q) % N_SLOT, 0:11 * P], as_f32(DW_HI[q % 2]), ALU.subtract).then_inc(lo_made, 1)

                for f in range(FT):
                    if f % 11 == 0:
                        down_lo(f // 11)
                    v.wait_ge(d_hi, l * FT + (f + 1))
                    nv.tensor_tensor(ZT_R[:, f, 0:TS], ZT[:, f, 0:TS], as_f32(D_HI[f]), ALU.subtract).then_inc(d_ready, 1)
                for j in range(KT):
                    if j < KT - 1:
                        down_lo(2 * j + 2)
                        down_lo(2 * j + 3)
                    wait_full(v, l, G_DOWN + j)
                    residual(G_DOWN + j, j, 40)
                for n in range(4, 8):
                    wait_taken(v, l, G_DOWN + n)
                v.sem_inc(layer_done, 1)
                step.end(v)


def shape_constants():
    import numpy as np

    def rope(hd):
        half = hd // 2
        freqs = np.float32(10000.0) ** (-np.arange(0, half, 2, dtype=np.float32) / np.float32(half))
        row = np.repeat(np.arange(TS // 64), 64).astype(np.float32)
        col = np.tile(np.arange(64), TS // 64).astype(np.float32)
        r, c = row[:, None] * freqs, col[:, None] * freqs
        ang = np.concatenate([r, r, c, c], axis=-1)
        return [np.tile(f(ang).T, (P // hd, 1)).astype(np.float32) for f in (np.cos, np.sin)]

    def rotation(hd):
        q = hd // 4
        m = np.zeros((P, P), np.float32)
        for d in range(P):
            if d // q % 2 == 0:
                m[d + q, d] = -1.0
            else:
                m[d - q, d] = 1.0
        return m

    s = np.arange(P)
    blocks = [np.eye(P), np.full((P, P), 1.0 / D), (s[:, None] // 64 == s // 64) / 64.0, (s[:, None] // 32 == s // 32) / 32.0,
              rotation(64), rotation(32)]
    const = np.concatenate(rope(64) + rope(32) + blocks, axis=1).astype(np.float32)
    mask = np.zeros((P, NPASS, P), np.float32)
    for m in range(LEVELS):
        h = 1 << m
        mask[:, 1 + m] = (s[:, None] // (2 * h) == s // (2 * h)) & (s[:, None] // h != s // h)
    return const, mask.reshape(P, -1)


def kernel(**inputs):
    import math

    import concourse.bacc as _bacc
    import numpy as np
    from concourse.bass_utils import run_bass_kernel_spmd as _run

    a = {k: np.asarray(v) for k, v in inputs.items()}

    def columns(x):
        return x.reshape(x.shape[0], -1, P).transpose(0, 2, 1)

    def twice(x):
        return np.tile(x, (1, P // x.shape[1]))[:, :, None]

    def each(x):
        return np.broadcast_to(x, (DEPTH,) + x.shape)

    lb = a["b_lb_logits"].reshape(2, DEPTH, 2, P).transpose(3, 0, 1, 2).reshape(P, 8)
    cond = np.stack([a["c"][0].reshape(KT, P), a["c_ctx"].reshape(KT, P)]).transpose(2, 0, 1).reshape(P, 16)
    lam_init = [0.8 - 0.6 * math.exp(-0.3 * l) for l in range(DEPTH)]
    layer_const = np.array([[[x, 1.0 - x, float(l > 0)]] * P for l, x in enumerate(lam_init)], np.float32)
    cols = np.concatenate([
        columns(a["b_ada"]), columns(a["norm1_g"]), columns(a["norm2_g"]), columns(a["conv_b"]),
        twice(a["a_qn_g"]), twice(a["a_kn_g"]), twice(a["c_qn_g"]), twice(a["c_kn_g"]), twice(a["c_subln_g"]),
        twice(a["b_norm_g"]), twice(a["d_norm_g"]), a["d_alpha_b"].transpose(0, 2, 1),
        columns(a["conv_w"][:, 0]), columns(a["conv_w"][:, 1]), columns(a["conv_w"][:, 2]), each(lb), each(cond), layer_const,
        np.broadcast_to(a["c_lambda"].reshape(DEPTH, 1, P), (DEPTH, P, P)),
    ], axis=2)
    assert cols.shape == (DEPTH, P, NCOL)
    w_alpha = np.zeros((DEPTH, 32, 2, P), np.float32)
    for d in range(2):
        w_alpha[:, 16 * d:16 * d + 16, d] = a["d_alpha_w"][:, d]
    keys_a = a["cache_a_k"][0].reshape(DEPTH, PAST, 1, P)
    keys_c = a["cache_c_k"][0].reshape(DEPTH, PAST, 2, P)
    const, mask = shape_constants()
    arrays = {
        "xT": np.concatenate([a["x_sample"][0], a["x_prompt"][0]]).reshape(T, KT, P).transpose(2, 1, 0),
        "cols": cols, "w_alpha": w_alpha, "const": const, "mask": mask,
        "keysT": np.concatenate([keys_a, keys_c], axis=2).transpose(0, 3, 2, 1),
        "vals": np.concatenate([a["cache_a_v"][0].reshape(DEPTH, PAST, P), a["cache_c_v"][0].reshape(DEPTH, PAST, 256)], axis=2),
        "hgrn": a["state_hgrn"][0].reshape(DEPTH, 2, 2, P, 64).transpose(0, 3, 1, 2, 4),
        "gla": a["state_gla"][0].reshape(DEPTH, 2, P, 64).transpose(0, 2, 1, 3),
        "w_ada": a["w_ada"], "w_in": a["w_in"], "w_branch": a["w_branch"], "w_out": a["w_out"], "w_up": a["w_up"], "w_down": a["w_down"],
    }
    arrays = {k: np.ascontiguousarray(x) for k, x in arrays.items()}
    outs = {"yT": (P, KT, T), "keysT": (DEPTH, P, 3, P), "vals": (DEPTH, P, V_B), "fin": (DEPTH, P, 2 * 3 * 64)}
    nc = _bacc.Bacc("TRN2", target_bir_lowering=False, num_devices=1)
    A = {k: nc.dram_tensor(f"in_{k}", x.shape, mybir.dt.from_np(x.dtype), kind="ExternalInput").ap() for k, x in arrays.items()}
    O = {k: nc.dram_tensor(f"out_{k}", s, F32, kind="ExternalOutput").ap() for k, s in outs.items()}
    build(nc, A, O)
    r = _run(nc, [{f"in_{k}": x for k, x in arrays.items()}], core_ids=[0]).results[0]
    y = r["out_yT"].transpose(2, 1, 0).reshape(T, D)
    keys_ = r["out_keysT"].transpose(0, 3, 2, 1)
    vals = r["out_vals"]
    fin = r["out_fin"].reshape(DEPTH, P, 2, 3, 64)
    hgrn = fin[:, :, :, 0:2].transpose(0, 2, 3, 1, 4).reshape(1, DEPTH, 2, 4, 64, 64)
    gla = fin[:, :, :, 2].transpose(0, 2, 1, 3).reshape(1, DEPTH, 2, 4, 32, 64)
    outputs = (y[TS:][None], y[:TS][None], keys_[:, :, 0].reshape(1, DEPTH, TC, 2, 64), vals[:, :, 0:P].reshape(1, DEPTH, TC, 2, 64),
               keys_[:, :, 1:3].reshape(1, DEPTH, TC, 4, 2, 32), vals[:, :, P:].reshape(1, DEPTH, TC, 4, 64), hgrn, gla)
    return tuple(np.ascontiguousarray(x) for x in outputs)
```
